# Optimizing a Trainium2 kernel written in Bass

```python
import jax, jax.numpy as jnp
from jax import lax
import numpy as np

D_MODEL = 1024
BATCH = 1
SEQ = 256
DEPTH = 2

D_MIX = D_MODEL
HEAD_DIM = 64
A_HEADS = 6
A_DIM = A_HEADS * HEAD_DIM
IDX_HEADS = 4
IDX_DIM = 64
TOPK_MAX = 256
Q_BLOCK = 128
B_HEADS = 6
B_DK = 64
B_DV = 64
B_DIM = B_HEADS * B_DV
HGRN_CHUNK = 64
C_GROUPS = 4
C_DIM = D_MIX - A_DIM - B_DIM
C_GROUP_DIM = C_DIM // C_GROUPS
C_CHUNK = 128
ROPE_THETA = 10000.0
F_DENSE = 2816
N_EXPERTS = 8
TOP_K = 2
F_EXPERT = 3584
N_DENSE = (DEPTH + 1) // 2
N_MOE = DEPTH // 2
EPS = 1e-6
IN_WIDTHS = (A_DIM, HEAD_DIM, HEAD_DIM, IDX_HEADS * IDX_DIM, IDX_DIM, IDX_HEADS, B_HEADS * B_DK, B_HEADS * B_DK, B_HEADS * B_DV, B_HEADS * B_DV, 2 * C_DIM)
IN_DIM = sum(IN_WIDTHS)


def rms_norm(x, g):
    xf = x.astype(jnp.float32)
    y = xf * lax.rsqrt(jnp.mean(xf * xf, axis=-1, keepdims=True) + EPS)
    return (y * g.astype(jnp.float32)).astype(x.dtype)

def layer_norm(x, g, b):
    xf = x.astype(jnp.float32)
    mu = jnp.mean(xf, axis=-1, keepdims=True)
    var = jnp.mean(jnp.square(xf - mu), axis=-1, keepdims=True)
    y = (xf - mu) * lax.rsqrt(var + EPS)
    return (y * g.astype(jnp.float32) + b.astype(jnp.float32)).astype(x.dtype)

def rope(x, pos):
    d = x.shape[-1]
    inv = ROPE_THETA ** (-jnp.arange(0, d, 2, dtype=jnp.float32) / d)
    ang = pos.astype(jnp.float32)[..., None] * inv
    cos = jnp.cos(ang)[:, :, None, :]
    sin = jnp.sin(ang)[:, :, None, :]
    xf = x.astype(jnp.float32)
    x1, x2 = xf[..., : d // 2], xf[..., d // 2:]
    return jnp.concatenate([x1 * cos - x2 * sin, x2 * cos + x1 * sin], axis=-1).astype(x.dtype)

def dsa_mixer(q, k, v, iq, ik, iw, positions):
    Bn, S = q.shape[0], q.shape[1]
    q = rope(q, positions)
    k = rope(k[:, :, None, :], positions)[:, :, 0, :]
    iq = rope(iq, positions)
    ik = rope(ik[:, :, None, :], positions)[:, :, 0, :]
    n_top = min(TOPK_MAX, S // 4)
    nb = S // Q_BLOCK
    to_blocks = lambda a: jnp.swapaxes(a.reshape((Bn, nb, Q_BLOCK) + a.shape[2:]), 0, 1)
    s_idx = jnp.arange(S)

    def one_block(args):
        qj, iqj, iwj, j = args
        t = j * Q_BLOCK + jnp.arange(Q_BLOCK)
        rel = jax.nn.relu(jnp.einsum('bqhd,bsd->bqhs', iqj, ik).astype(jnp.float32) * IDX_DIM ** -0.5)
        score = jnp.einsum('bqh,bqhs->bqs', iwj.astype(jnp.float32) * IDX_HEADS ** -0.5, rel)
        causal = s_idx[None, :] <= t[:, None]
        score = jnp.where(causal[None], score, -jnp.inf)
        _, idx = lax.top_k(score, n_top)
        flat = idx.reshape(Bn, Q_BLOCK * n_top, 1)
        kg = jnp.take_along_axis(k, flat, axis=1).reshape(Bn, Q_BLOCK, n_top, HEAD_DIM)
        vg = jnp.take_along_axis(v, flat, axis=1).reshape(Bn, Q_BLOCK, n_top, HEAD_DIM)
        logits = jnp.einsum('bqhd,bqkd->bqhk', qj, kg).astype(jnp.float32) * HEAD_DIM ** -0.5
        valid = idx <= t[None, :, None]
        logits = jnp.where(valid[:, :, None, :], logits, -jnp.inf)
        p = jax.nn.softmax(logits, axis=-1).astype(v.dtype)
        return jnp.einsum('bqhk,bqkd->bqhd', p, vg)

    out = lax.map(one_block, (to_blocks(q), to_blocks(iq), to_blocks(iw), jnp.arange(nb)))
    return jnp.swapaxes(out, 0, 1).reshape(Bn, S, A_HEADS * HEAD_DIM)

def hgrn2_mixer(q, f_logit, i, g, lb, onorm_g):
    Bn, S, H, dk = q.shape
    dv = i.shape[-1]
    lb = lb.reshape(H, dk).astype(jnp.float32)
    log_f = jnp.logaddexp(jnp.log(lb), jnp.log1p(-lb) + jax.nn.log_sigmoid(f_logit.astype(jnp.float32)))
    kk = -jnp.expm1(log_f)
    nc = S // HGRN_CHUNK
    chunk = lambda a: a.astype(jnp.float32).reshape(Bn, nc, HGRN_CHUNK, H, a.shape[-1]).transpose(1, 0, 3, 2, 4)
    qc, kc, vc, lfc = chunk(q), chunk(kk), chunk(i), chunk(log_f)
    bc = jnp.cumsum(lfc, axis=3)
    tril = jnp.arange(HGRN_CHUNK)[:, None] >= jnp.arange(HGRN_CHUNK)[None, :]

    def step(state, xs):
        qj, kj, vj, bj = xs
        diff = bj[:, :, :, None, :] - bj[:, :, None, :, :]
        decay = jnp.exp(jnp.where(tril[:, :, None], diff, -jnp.inf))
        attn = jnp.einsum('bhtd,bhsd,bhtsd->bhts', qj, kj, decay)
        o = jnp.einsum('bhts,bhsv->bhtv', attn, vj) + jnp.einsum('bhtd,bhdv->bhtv', qj * jnp.exp(bj), state)
        b_last = bj[:, :, -1:, :]
        new_state = jnp.exp(b_last[:, :, 0, :])[..., None] * state + jnp.einsum('bhsd,bhsv->bhdv', kj * jnp.exp(b_last - bj), vj)
        return new_state, o

    s0 = jnp.zeros((Bn, H, dk, dv), jnp.float32)
    _, o = lax.scan(step, s0, (qc, kc, vc, bc))
    o = o.transpose(1, 0, 3, 2, 4).reshape(Bn, S, H, dv)
    o = rms_norm(o, onorm_g) * jax.nn.silu(g.astype(jnp.float32))
    return o.reshape(Bn, S, H * dv).astype(q.dtype)

def gmlp_mixer(uv, vn_g, vn_b, ws, bs):
    Bn, S = uv.shape[0], uv.shape[1]
    uv = jax.nn.gelu(uv, approximate=False)
    u, v = uv[..., :C_DIM], uv[..., C_DIM:]
    v = layer_norm(v, vn_g, vn_b)
    nc = S // C_CHUNK
    v = v.reshape(Bn, nc, C_CHUNK, C_GROUPS, C_GROUP_DIM)
    mask = jnp.tril(jnp.ones((C_CHUNK, C_CHUNK), ws.dtype))
    w = ws * mask[None]
    mixed = jnp.einsum('gts,bnsgd->bntgd', w, v) + bs.T[None, None, :, :, None]
    return u * mixed.reshape(Bn, S, C_DIM)

def swiglu(h, w_gate, w_up, w_down):
    return (jax.nn.silu(h @ w_gate) * (h @ w_up)) @ w_down

def moe_swiglu(h, w_router, w_gate, w_up, w_down):
    logits = jnp.einsum('bsd,de->bse', h, w_router).astype(jnp.float32)
    top_v, top_i = lax.top_k(logits, TOP_K)
    wts = jax.nn.softmax(top_v, axis=-1)
    gates = jnp.sum(jax.nn.one_hot(top_i, N_EXPERTS, dtype=jnp.float32) * wts[..., None], axis=-2)

    def per_seq(args):
        hb, gb = args
        a = jnp.einsum('sd,edf->sef', hb, w_gate)
        u = jnp.einsum('sd,edf->sef', hb, w_up)
        act = jax.nn.silu(a) * u * gb[:, :, None]
        return jnp.einsum('sef,efd->sd', act, w_down)

    return lax.map(per_seq, (h, gates.astype(h.dtype)))

def first_inputs(seed: int = 0) -> dict:
    key = jax.random.key(seed)
    ks = jax.random.split(key, 24)
    nrm = lambda k, shape, s: jax.random.normal(k, shape, jnp.float32) * s
    x = nrm(ks[0], (BATCH, SEQ, D_MODEL), 1.0)
    c = nrm(ks[1], (BATCH, D_MODEL), 1.0)
    offsets = jax.random.randint(ks[2], (BATCH, 1), 0, 4096, dtype=jnp.int32)
    positions = offsets + jnp.arange(SEQ, dtype=jnp.int32)[None, :]
    return {
        "x": x,
        "c": c,
        "positions": positions,
        "w_ada": nrm(ks[3], (DEPTH, D_MODEL, 6 * D_MODEL), 0.5 * D_MODEL ** -0.5),
        "b_ada": nrm(ks[4], (DEPTH, 6 * D_MODEL), 0.02),
        "g_norm_mix": 1.0 + nrm(ks[5], (DEPTH, D_MODEL), 0.02),
        "g_norm_ffn": 1.0 + nrm(ks[6], (DEPTH, D_MODEL), 0.02),
        "w_in": nrm(ks[7], (DEPTH, D_MODEL, IN_DIM), D_MODEL ** -0.5),
        "w_out": nrm(ks[8], (DEPTH, D_MIX, D_MODEL), D_MIX ** -0.5),
        "hgrn_lb_logits": nrm(ks[9], (DEPTH, B_HEADS * B_DK), 0.5),
        "hgrn_out_norm": 1.0 + nrm(ks[10], (DEPTH, B_DV), 0.02),
        "gmlp_vnorm_g": 1.0 + nrm(ks[11], (DEPTH, C_DIM), 0.02),
        "gmlp_vnorm_b": nrm(ks[12], (DEPTH, C_DIM), 0.02),
        "gmlp_w_s": nrm(ks[13], (DEPTH, C_GROUPS, C_CHUNK, C_CHUNK), C_CHUNK ** -0.5),
        "gmlp_b_s": 1.0 + nrm(ks[14], (DEPTH, C_GROUPS, C_CHUNK), 0.02),
        "ffn_w_gate": nrm(ks[15], (N_DENSE, D_MODEL, F_DENSE), D_MODEL ** -0.5),
        "ffn_w_up": nrm(ks[16], (N_DENSE, D_MODEL, F_DENSE), D_MODEL ** -0.5),
        "ffn_w_down": nrm(ks[17], (N_DENSE, F_DENSE, D_MODEL), F_DENSE ** -0.5),
        "moe_w_router": nrm(ks[18], (N_MOE, D_MODEL, N_EXPERTS), D_MODEL ** -0.5),
        "moe_w_gate": nrm(ks[19], (N_MOE, N_EXPERTS, D_MODEL, F_EXPERT), D_MODEL ** -0.5),
        "moe_w_up": nrm(ks[20], (N_MOE, N_EXPERTS, D_MODEL, F_EXPERT), D_MODEL ** -0.5),
        "moe_w_down": nrm(ks[21], (N_MOE, N_EXPERTS, F_EXPERT, D_MODEL), F_EXPERT ** -0.5),
        "g_final": 1.0 + nrm(ks[22], (D_MODEL,), 0.02),
    }

def first_block(x, c, positions, w_ada, b_ada, g_norm_mix, g_norm_ffn, w_in, w_out, hgrn_lb_logits, hgrn_out_norm, gmlp_vnorm_g, gmlp_vnorm_b, gmlp_w_s, gmlp_b_s, ffn_w_gate, ffn_w_up, ffn_w_down, moe_w_router, moe_w_gate, moe_w_up, moe_w_down, g_final):
    Bn, S = x.shape[0], x.shape[1]
    p_lb = jax.nn.softmax(hgrn_lb_logits.astype(jnp.float32), axis=0)
    cum = jnp.cumsum(p_lb, axis=0)
    lower_bounds = cum - cum[0:1]
    splits = [int(s) for s in np.cumsum(IN_WIDTHS)[:-1]]
    cond = jax.nn.silu(c)
    for l in range(DEPTH):
        mod = cond @ w_ada[l] + b_ada[l]
        sh1, sc1, g1, sh2, sc2, g2 = [m[:, None, :] for m in jnp.split(mod, 6, axis=-1)]
        h = rms_norm(x, g_norm_mix[l]) * (1 + sc1) + sh1
        z = h @ w_in[l]
        aq, ak, av, iq, ik, iw, bq, bf, bi, bg, cuv = jnp.split(z, splits, axis=-1)
        a_out = dsa_mixer(aq.reshape(Bn, S, A_HEADS, HEAD_DIM), ak, av, iq.reshape(Bn, S, IDX_HEADS, IDX_DIM), ik, iw, positions)
        b_out = hgrn2_mixer(bq.reshape(Bn, S, B_HEADS, B_DK), bf.reshape(Bn, S, B_HEADS, B_DK), bi.reshape(Bn, S, B_HEADS, B_DV), bg.reshape(Bn, S, B_HEADS, B_DV), lower_bounds[l], hgrn_out_norm[l])
        c_out = gmlp_mixer(cuv, gmlp_vnorm_g[l], gmlp_vnorm_b[l], gmlp_w_s[l], gmlp_b_s[l])
        mix = jnp.concatenate([a_out, b_out, c_out], axis=-1) @ w_out[l]
        x = x + g1 * mix
        h = rms_norm(x, g_norm_ffn[l]) * (1 + sc2) + sh2
        if l % 2 == 0:
            y = swiglu(h, ffn_w_gate[l // 2], ffn_w_up[l // 2], ffn_w_down[l // 2])
        else:
            y = moe_swiglu(h, moe_w_router[l // 2], moe_w_gate[l // 2], moe_w_up[l // 2], moe_w_down[l // 2])
        x = x + g2 * y
    return rms_norm(x, g_final)


N_MEM = 256
SC_WIDTH = D_MODEL // 2
SC_GROUPS = 8
CONV_K = 3
POOL_WIDTH = D_MODEL // 2
POOL_WINDOWS = (2, 4, 8, 16)
POOL_GROUP = POOL_WIDTH // len(POOL_WINDOWS)
EVEN_IN = 3 * SC_WIDTH + POOL_WIDTH
EVEN_MIX = SC_WIDTH + POOL_WIDTH
ML_HEADS = 4
ML_HEAD_DIM = 128
ML_WIDTH = ML_HEADS * ML_HEAD_DIM
ML_CHUNK = 64
MLA_HEADS = 8
QK_NOPE = 64
QK_ROPE = 32
V_DIM = 64
Q_LORA = 384
KV_LORA = 256
MLA_WIDTH = MLA_HEADS * V_DIM
ODD_SIZES = (ML_WIDTH, ML_WIDTH, ML_WIDTH, ML_WIDTH, 2 * ML_HEADS, Q_LORA, KV_LORA, QK_ROPE)
ODD_SPLIT = tuple(int(v) for v in np.cumsum(ODD_SIZES)[:-1])
ODD_IN = sum(ODD_SIZES)
ODD_MIX = ML_WIDTH + MLA_WIDTH
XA_HEADS = 4
XA_HEAD_DIM = 128
XA_WIDTH = XA_HEADS * XA_HEAD_DIM
FFN_HIDDEN = ((8 * D_MODEL + 3 * 256 - 1) // (3 * 256)) * 256
N_EVEN = (DEPTH + 1) // 2
N_ODD = DEPTH // 2


def rmsnorm(x, g):
    xf = x.astype(jnp.float32)
    y = xf * lax.rsqrt(jnp.mean(xf * xf, axis=-1, keepdims=True) + EPS)
    return (y * g.astype(jnp.float32)).astype(x.dtype)

def causal_dwconv(u, w):
    c = u.shape[-1]
    return lax.conv_general_dilated(u, w[:, None, :].astype(u.dtype), window_strides=(1,),
                                    padding=[(CONV_K - 1, 0)],
                                    dimension_numbers=('NWC', 'WIO', 'NWC'),
                                    feature_group_count=c)

def causal_pool_mixer(u, pool_w, pool_scale):
    B, S, _ = u.shape
    ug = u.reshape(B, S, len(POOL_WINDOWS), POOL_GROUP)
    csum = jnp.cumsum(ug.astype(jnp.float32), axis=1)
    t1 = jnp.arange(1, S + 1)
    means = []
    for gi, w in enumerate(POOL_WINDOWS):
        cg = csum[:, :, gi]
        shifted = jnp.pad(cg, ((0, 0), (w, 0), (0, 0)))[:, :S]
        cnt = jnp.minimum(t1, w).astype(jnp.float32)
        means.append((cg - shifted) / cnt[None, :, None])
    pooled = jnp.stack(means, axis=2).astype(u.dtype)
    y = jnp.einsum('bsgc,gcd->bsgd', pooled - ug, pool_w)
    return y.reshape(B, S, POOL_WIDTH) * pool_scale

def even_mixer(h, w_in, conv_w, pool_w, pool_scale, w_out):
    z = h @ w_in
    g_b, g_c, xa, xb = jnp.split(z, [SC_WIDTH, 2 * SC_WIDTH, 3 * SC_WIDTH], axis=-1)
    ya = g_b * causal_dwconv(g_c * xa, conv_w)
    yb = causal_pool_mixer(xb, pool_w, pool_scale)
    return jnp.concatenate([ya, yb], axis=-1) @ w_out

def mlstm_chunkwise(q, k, v, i_pre, f_pre):
    B, S, H, D = q.shape
    L = ML_CHUNK
    NC = S // L

    def chunk(t):
        return t.reshape(B, NC, L, H, D).transpose(0, 3, 1, 2, 4)

    def chunk_g(t):
        return t.reshape(B, NC, L, H).transpose(0, 3, 1, 2)

    qc, kc, vc = chunk(q), chunk(k) * (D ** -0.5), chunk(v)
    ig = chunk_g(i_pre)
    bcum = jnp.cumsum(chunk_g(jax.nn.log_sigmoid(f_pre)), axis=-1)
    gtot = bcum[..., -1]

    a = gtot[..., None] - bcum + ig
    m_loc = jnp.max(a, axis=-1)
    w_loc = jnp.exp(a - m_loc[..., None])
    C_loc = jnp.einsum('bhcl,bhclv,bhclk->bhcvk', w_loc, vc, kc)
    n_loc = jnp.einsum('bhcl,bhclk->bhck', w_loc, kc)

    def step(carry, xs):
        C, n, m = carry
        g_c, m_l, C_l, n_l = xs
        m_new = jnp.maximum(g_c + m, m_l)
        s_old = jnp.exp(g_c + m - m_new)
        s_new = jnp.exp(m_l - m_new)
        C_new = s_old[..., None, None] * C + s_new[..., None, None] * C_l
        n_new = s_old[..., None] * n + s_new[..., None] * n_l
        return (C_new, n_new, m_new), (C, n, m)

    init = (jnp.zeros((B, H, D, D), jnp.float32), jnp.zeros((B, H, D), jnp.float32),
            jnp.zeros((B, H), jnp.float32))
    xs = (jnp.moveaxis(gtot, 2, 0), jnp.moveaxis(m_loc, 2, 0),
          jnp.moveaxis(C_loc, 2, 0), jnp.moveaxis(n_loc, 2, 0))
    _, (C_prev, n_prev, m_prev) = lax.scan(step, init, xs)
    C_prev = jnp.moveaxis(C_prev, 0, 2)
    n_prev = jnp.moveaxis(n_prev, 0, 2)
    m_prev = jnp.moveaxis(m_prev, 0, 2)

    causal = jnp.tril(jnp.ones((L, L), dtype=bool))
    dmat = jnp.where(causal, bcum[..., :, None] - bcum[..., None, :] + ig[..., None, :], -jnp.inf)
    inter = bcum + m_prev[..., None]
    m_t = jnp.maximum(inter, jnp.max(dmat, axis=-1))
    w_intra = jnp.exp(dmat - m_t[..., None])
    w_inter = jnp.exp(inter - m_t)
    sw = w_intra * jnp.einsum('bhcld,bhcsd->bhcls', qc, kc)
    num = (w_inter[..., None] * jnp.einsum('bhcvk,bhclk->bhclv', C_prev, qc)
           + jnp.einsum('bhcls,bhcsv->bhclv', sw, vc))
    den_raw = w_inter * jnp.einsum('bhck,bhclk->bhcl', n_prev, qc) + jnp.sum(sw, axis=-1)
    den = jnp.maximum(jnp.abs(den_raw), jnp.exp(-m_t))
    hc = num / den[..., None]
    return hc.transpose(0, 2, 3, 1, 4).reshape(B, S, H, D)

def rope_tables(positions):
    half = QK_ROPE // 2
    inv_freq = ROPE_THETA ** (-jnp.arange(half, dtype=jnp.float32) / half)
    ang = positions.astype(jnp.float32)[..., None] * inv_freq
    return jnp.cos(ang)[:, :, None, :], jnp.sin(ang)[:, :, None, :]

def apply_rope(t, cos, sin):
    half = t.shape[-1] // 2
    tf = t.astype(jnp.float32)
    t1, t2 = tf[..., :half], tf[..., half:]
    return jnp.concatenate([t1 * cos - t2 * sin, t1 * sin + t2 * cos], axis=-1).astype(t.dtype)

def mla_attention(q_nope, q_rope, k_nope, k_rope, v):
    B, S, H, _ = q_nope.shape
    nb = S // Q_BLOCK
    scale = (QK_NOPE + QK_ROPE) ** -0.5
    k_idx = jnp.arange(S)

    def to_blocks(t):
        return jnp.moveaxis(t.reshape(B, nb, Q_BLOCK, H, t.shape[-1]), 1, 0)

    def attend_block(args):
        blk, qn, qr = args
        s = (jnp.einsum('bqhd,bkhd->bhqk', qn, k_nope)
             + jnp.einsum('bqhr,bkr->bhqk', qr, k_rope)).astype(jnp.float32) * scale
        q_idx = blk * Q_BLOCK + jnp.arange(Q_BLOCK)
        s = jnp.where(k_idx[None, :] <= q_idx[:, None], s, -jnp.inf)
        p = jax.nn.softmax(s, axis=-1).astype(v.dtype)
        return jnp.einsum('bhqk,bkhd->bqhd', p, v)

    out = lax.map(attend_block, (jnp.arange(nb), to_blocks(q_nope), to_blocks(q_rope)))
    return jnp.moveaxis(out, 0, 1).reshape(B, S, H * V_DIM)

def odd_mixer(h, positions, w_in, gate_bias, ml_norm_g, q_norm_g, kv_norm_g, w_uq, w_ukv, w_out):
    B, S, _ = h.shape
    z = h @ w_in
    q_m, k_m, v_m, o_m, gates, c_q, c_kv, k_r = jnp.split(z, ODD_SPLIT, axis=-1)
    gates = (gates + gate_bias).astype(jnp.float32)
    i_pre, f_pre = gates[..., :ML_HEADS], gates[..., ML_HEADS:]
    hs = (B, S, ML_HEADS, ML_HEAD_DIM)
    hm = mlstm_chunkwise(q_m.reshape(hs).astype(jnp.float32), k_m.reshape(hs).astype(jnp.float32),
                         v_m.reshape(hs).astype(jnp.float32), i_pre, f_pre).astype(h.dtype)
    hm = jax.nn.sigmoid(o_m).reshape(hs) * hm
    hm = rmsnorm(hm, ml_norm_g.reshape(ML_HEADS, ML_HEAD_DIM)).reshape(B, S, ML_WIDTH)

    q = (rmsnorm(c_q, q_norm_g) @ w_uq).reshape(B, S, MLA_HEADS, QK_NOPE + QK_ROPE)
    kv = (rmsnorm(c_kv, kv_norm_g) @ w_ukv).reshape(B, S, MLA_HEADS, QK_NOPE + V_DIM)
    cos, sin = rope_tables(positions)
    q_nope, q_rope = q[..., :QK_NOPE], apply_rope(q[..., QK_NOPE:], cos, sin)
    k_nope, v = kv[..., :QK_NOPE], kv[..., QK_NOPE:]
    k_rope = apply_rope(k_r[:, :, None, :], cos, sin)[:, :, 0]
    ha = mla_attention(q_nope, q_rope, k_nope, k_rope, v)
    return jnp.concatenate([hm, ha], axis=-1) @ w_out

def memory_cross_attention(h, mem_n, wq, wkv, wo):
    B, S, _ = h.shape
    q = (h @ wq).reshape(B, S, XA_HEADS, XA_HEAD_DIM)
    k, v = jnp.split(mem_n @ wkv, 2, axis=-1)
    k = k.reshape(B, N_MEM, XA_HEADS, XA_HEAD_DIM)
    v = v.reshape(B, N_MEM, XA_HEADS, XA_HEAD_DIM)
    s = jnp.einsum('bshd,bmhd->bhsm', q, k).astype(jnp.float32) * (XA_HEAD_DIM ** -0.5)
    p = jax.nn.softmax(s, axis=-1).astype(v.dtype)
    return jnp.einsum('bhsm,bmhd->bshd', p, v).reshape(B, S, XA_WIDTH) @ wo

def swiglu_2(h, w_gate_up, w_down):
    g, u = jnp.split(h @ w_gate_up, 2, axis=-1)
    return (jax.nn.silu(g) * u) @ w_down

def second_inputs(seed: int = 0) -> dict:
    key = jax.random.key(seed)
    ks = iter(jax.random.split(key, 40))
    f32 = jnp.float32

    def dense(shape, fan_in):
        return jax.random.normal(next(ks), shape, f32) * (fan_in ** -0.5)

    def gain(shape):
        return 1.0 + 0.05 * jax.random.normal(next(ks), shape, f32)

    x = jax.random.normal(next(ks), (BATCH, SEQ, D_MODEL), f32)
    mem = jax.random.normal(next(ks), (BATCH, N_MEM, D_MODEL), f32)
    offsets = jax.random.randint(next(ks), (BATCH, 1), 0, 1024, dtype=jnp.int32)
    positions = offsets + jnp.arange(SEQ, dtype=jnp.int32)[None, :]

    f_bias = jnp.linspace(3.0, 6.0, ML_HEADS, dtype=f32)[None, :] + 0.1 * jax.random.normal(next(ks), (N_ODD, ML_HEADS), f32)
    i_bias = 0.1 * jax.random.normal(next(ks), (N_ODD, ML_HEADS), f32)

    return {
        'x': x,
        'mem': mem,
        'positions': positions,
        'norm_mix_g': gain((DEPTH, D_MODEL)),
        'norm_xattn_g': gain((DEPTH, D_MODEL)),
        'mem_norm_g': gain((DEPTH, D_MODEL)),
        'xattn_wq': dense((DEPTH, D_MODEL, XA_WIDTH), D_MODEL),
        'xattn_wkv': dense((DEPTH, D_MODEL, 2 * XA_WIDTH), D_MODEL),
        'xattn_wo': dense((DEPTH, XA_WIDTH, D_MODEL), XA_WIDTH),
        'norm_ffn_g': gain((DEPTH, D_MODEL)),
        'ffn_w_gate_up': dense((DEPTH, D_MODEL, 2 * FFN_HIDDEN), D_MODEL),
        'ffn_w_down': dense((DEPTH, FFN_HIDDEN, D_MODEL), FFN_HIDDEN),
        'ev_w_in': dense((N_EVEN, D_MODEL, EVEN_IN), D_MODEL),
        'ev_conv_w': dense((N_EVEN, CONV_K, SC_WIDTH), CONV_K),
        'ev_pool_w': dense((N_EVEN, len(POOL_WINDOWS), POOL_GROUP, POOL_GROUP), POOL_GROUP),
        'ev_pool_scale': 1.0 + 0.1 * jax.random.normal(next(ks), (N_EVEN, POOL_WIDTH), f32),
        'ev_w_out': dense((N_EVEN, EVEN_MIX, D_MODEL), EVEN_MIX),
        'od_w_in': dense((N_ODD, D_MODEL, ODD_IN), D_MODEL),
        'od_gate_bias': jnp.concatenate([i_bias, f_bias], axis=-1),
        'od_ml_norm_g': gain((N_ODD, ML_WIDTH)),
        'od_q_norm_g': gain((N_ODD, Q_LORA)),
        'od_kv_norm_g': gain((N_ODD, KV_LORA)),
        'od_w_uq': dense((N_ODD, Q_LORA, MLA_HEADS * (QK_NOPE + QK_ROPE)), Q_LORA),
        'od_w_ukv': dense((N_ODD, KV_LORA, MLA_HEADS * (QK_NOPE + V_DIM)), KV_LORA),
        'od_w_out': dense((N_ODD, ODD_MIX, D_MODEL), ODD_MIX),
        'final_norm_g': gain((D_MODEL,)),
    }

def second_block(x, mem, positions, norm_mix_g, norm_xattn_g, mem_norm_g, xattn_wq, xattn_wkv, xattn_wo,
              norm_ffn_g, ffn_w_gate_up, ffn_w_down, ev_w_in, ev_conv_w, ev_pool_w, ev_pool_scale,
              ev_w_out, od_w_in, od_gate_bias, od_ml_norm_g, od_q_norm_g, od_kv_norm_g, od_w_uq,
              od_w_ukv, od_w_out, final_norm_g):
    for layer in range(DEPTH):
        h = rmsnorm(x, norm_mix_g[layer])
        if layer % 2 == 0:
            e = layer // 2
            mix = even_mixer(h, ev_w_in[e], ev_conv_w[e], ev_pool_w[e], ev_pool_scale[e], ev_w_out[e])
        else:
            o = layer // 2
            mix = odd_mixer(h, positions, od_w_in[o], od_gate_bias[o], od_ml_norm_g[o], od_q_norm_g[o],
                            od_kv_norm_g[o], od_w_uq[o], od_w_ukv[o], od_w_out[o])
        x = x + mix
        mem_n = rmsnorm(mem, mem_norm_g[layer])
        x = x + memory_cross_attention(rmsnorm(x, norm_xattn_g[layer]), mem_n,
                                       xattn_wq[layer], xattn_wkv[layer], xattn_wo[layer])
        x = x + swiglu_2(rmsnorm(x, norm_ffn_g[layer]), ffn_w_gate_up[layer], ffn_w_down[layer])
    return rmsnorm(x, final_norm_g)


def setup_inputs(seed=0):
    out = dict(first_inputs(seed))
    for name, value in second_inputs(seed + 1).items():
        if name != "x":
            out[name + "_2"] = value
    return out


def reference(
    x, c, positions, w_ada, b_ada, g_norm_mix, g_norm_ffn, w_in, w_out, hgrn_lb_logits,
    hgrn_out_norm, gmlp_vnorm_g, gmlp_vnorm_b, gmlp_w_s, gmlp_b_s, ffn_w_gate, ffn_w_up,
    ffn_w_down, moe_w_router, moe_w_gate, moe_w_up, moe_w_down, g_final, mem_2, positions_2,
    norm_mix_g_2, norm_xattn_g_2, mem_norm_g_2, xattn_wq_2, xattn_wkv_2, xattn_wo_2,
    norm_ffn_g_2, ffn_w_gate_up_2, ffn_w_down_2, ev_w_in_2, ev_conv_w_2, ev_pool_w_2,
    ev_pool_scale_2, ev_w_out_2, od_w_in_2, od_gate_bias_2, od_ml_norm_g_2, od_q_norm_g_2,
    od_kv_norm_g_2, od_w_uq_2, od_w_ukv_2, od_w_out_2, final_norm_g_2,
):
    x = first_block(
        x, c, positions, w_ada, b_ada, g_norm_mix, g_norm_ffn, w_in, w_out, hgrn_lb_logits,
        hgrn_out_norm, gmlp_vnorm_g, gmlp_vnorm_b, gmlp_w_s, gmlp_b_s, ffn_w_gate, ffn_w_up,
        ffn_w_down, moe_w_router, moe_w_gate, moe_w_up, moe_w_down, g_final,
    )
    return second_block(
        x, mem_2, positions_2, norm_mix_g_2, norm_xattn_g_2, mem_norm_g_2, xattn_wq_2,
        xattn_wkv_2, xattn_wo_2, norm_ffn_g_2, ffn_w_gate_up_2, ffn_w_down_2, ev_w_in_2,
        ev_conv_w_2, ev_pool_w_2, ev_pool_scale_2, ev_w_out_2, od_w_in_2, od_gate_bias_2,
        od_ml_norm_g_2, od_q_norm_g_2, od_kv_norm_g_2, od_w_uq_2, od_w_ukv_2, od_w_out_2,
        final_norm_g_2,
    )


_drawn_inputs = setup_inputs


def setup_inputs(seed=0):
    import zlib

    import numpy as np

    out = dict(_drawn_inputs(seed))
    spreads = {}
    factors = {'hgrn_out_norm': 4.284,
     'gmlp_vnorm_g': 5.027,
     'gmlp_vnorm_b': 3.792,
     'gmlp_b_s': 6.053,
     'norm_xattn_g_2': 8.0,
     'mem_norm_g_2': 5.849,
     'od_q_norm_g_2': 8.0,
     'od_kv_norm_g_2': 8.0,
     'od_ml_norm_g_2': 3.313}
    for name, (base, spread) in spreads.items():
        noise = np.random.default_rng([zlib.crc32(name.encode()), seed]).standard_normal(out[name].shape)
        drawn = base * np.exp(spread * noise) if base else spread * noise
        out[name] = __import__('jax').numpy.asarray(drawn.astype(out[name].dtype))
    for name, factor in factors.items():
        out[name] = (out[name] * factor).astype(out[name].dtype)
    return out
```

```python
from contextlib import ExitStack

import numpy as np

import concourse.bass as bass
from concourse import mybir

F32 = mybir.dt.float32
I32 = mybir.dt.int32
U8 = mybir.dt.uint8
ALU = mybir.AluOpType
ACT = mybir.ActivationFunctionType
AX = mybir.AxisListType.X

P = 128
S = 256
NT = S // P
D = 1024
KD = D // P
HD = 64
A_HEADS, IDX_HEADS, TOPK = 6, 4, 64
B_HEADS, PAIRS = 6, 3
CHUNK = 64
IN1 = 2884
Z_AQ, Z_AK, Z_AV, Z_IQ, Z_IK, Z_IW = 0, 384, 448, 512, 768, 832
Z_BQ, Z_BF, Z_BI, Z_BG, Z_UV = 836, 1220, 1604, 1988, 2372
F_DENSE, F_EXPERT, N_EXP = 2816, 3584, 8
FT = 256
ML_HEADS, MLA_HEADS, NOPE, ROPE_W, VD = 4, 8, 64, 32, 64
QKW = NOPE + ROPE_W
XA_HEADS, XA_D = 4, 128
EPS = 1e-6
NEG = -1.0e30
LOWEST = -3.0e38
TAKEN = -3.3e38
RING = 6
SLOT = 2048
LOAD = 32

INPUTS = ['x', 'c', 'positions', 'w_ada', 'b_ada', 'g_norm_mix', 'g_norm_ffn', 'w_in', 'w_out',
          'hgrn_lb_logits', 'hgrn_out_norm', 'gmlp_vnorm_g', 'gmlp_vnorm_b', 'gmlp_w_s', 'gmlp_b_s',
          'ffn_w_gate', 'ffn_w_up', 'ffn_w_down', 'moe_w_router', 'moe_w_gate', 'moe_w_up',
          'moe_w_down', 'g_final', 'mem_2', 'positions_2', 'norm_mix_g_2', 'norm_xattn_g_2',
          'mem_norm_g_2', 'xattn_wq_2', 'xattn_wkv_2', 'xattn_wo_2', 'norm_ffn_g_2',
          'ffn_w_gate_up_2', 'ffn_w_down_2', 'ev_w_in_2', 'ev_conv_w_2', 'ev_pool_w_2',
          'ev_pool_scale_2', 'ev_w_out_2', 'od_w_in_2', 'od_gate_bias_2', 'od_ml_norm_g_2',
          'od_q_norm_g_2', 'od_kv_norm_g_2', 'od_w_uq_2', 'od_w_ukv_2', 'od_w_out_2',
          'final_norm_g_2']

ROWS1 = [('g_norm_mix', 'l (c p) -> (l c) p', 16), ('g_norm_ffn', 'l (c p) -> (l c) p', 16),
         ('norm_mix_g_2', 'l (c p) -> (l c) p', 16), ('norm_xattn_g_2', 'l (c p) -> (l c) p', 16),
         ('mem_norm_g_2', 'l (c p) -> (l c) p', 16), ('norm_ffn_g_2', 'l (c p) -> (l c) p', 16),
         ('od_q_norm_g_2', 'l (c p) -> (l c) p', 3), ('od_kv_norm_g_2', 'l (c p) -> (l c) p', 2),
         ('ev_pool_scale_2', 'l (c p) -> (l c) p', 4), ('ev_conv_w_2', 'l k (c p) -> (l k c) p', 12)]
ROWS2 = [('b_ada', 'l (c p) -> (l c) p', 96), ('hgrn_lb_logits', 'l (c p) -> (l c) p', 6),
         ('gmlp_b_s', 'l g p -> (l g) p', 8), ('c', 'l (c p) -> (l c) p', 8)]


def offsets(rows):
    at, out = 0, {}
    for name, _, n in rows:
        out[name] = at
        at += n
    return out, at


COL1, NCOL1 = offsets(ROWS1)
COL2, NCOL2 = offsets(ROWS2)


class Core:
    pass


def chain(eng, sem):
    done = [0]

    def step(ins):
        done[0] += 1
        ins.then_inc(sem, 1)
        eng.wait_ge(sem, done[0])
    return step


def signal(eng, ins, sem, value):
    ins.then_inc(sem, 1)
    eng.wait_ge(sem, value)


def magnitude(dve, out, x):
    return dve.scalar_tensor_tensor(out, x, -1.0, x, ALU.mult, ALU.max)


def in_order(**events):
    at, before = 0, {}
    for name, times in events.items():
        before[name] = at
        at += times
    return before


def rows_view(ap):
    return ap.rearrange("(k p) n -> p k n", p=P)


def job(core, loads, release):
    j = len(core.jobs)
    core.jobs.append((loads, release))
    return j


def slot_of(core, j, k, w, lo=0):
    return core.ring[:, j % RING, lo:lo + k * w].rearrange('p (k w) -> p k w', k=k)


def gemm_jobs(core, view, col, w, k, release):
    per = min(k, SLOT // w, 4)
    jobs = []
    for k0 in range(0, k, per):
        kk = min(per, k - k0)
        h = (kk + 1) // 2
        loads = [(0, h, w, view[:, k0:k0 + h, col:col + w])]
        if kk > h:
            loads.append((h * w, kk - h, w, view[:, k0 + h:k0 + kk, col:col + w]))
        else:
            hw = w // 2
            loads = [(0, 1, (hw, w), view[:, k0:k0 + 1, col:col + hw]),
                     (hw, 1, (w - hw, w), view[:, k0:k0 + 1, col + hw:col + w])]
        jobs.append((job(core, loads, release), k0, kk))
    return jobs


def start_job(core, sp, j):
    loads, _ = core.jobs[j]
    for off, k, w, src in loads:
        dst = core.ring[:, j % RING, off:off + k * (w[0] if isinstance(w, tuple) else w)]
        sp.dma_start(dst.rearrange('p (k w) -> p k w', k=k), src).then_inc(core.landed[j % RING], 16)


def wait_job(core, pe, j):
    pe.wait_ge(core.landed[j % RING], LOAD * (j // RING + 1))


def proj(core, name, src, waits, tiles):
    st = dict(kind='proj', name=name, src=src, waits=waits, tiles=[])
    for view, col, w, k, ksrc, layout, evac, dst in tiles:
        t = core.n_tiles
        core.n_tiles += 1
        jobs = gemm_jobs(core, view, col, w, k, ('proj_done', 2 * t + 2))
        st['tiles'].append(dict(t=t, jobs=jobs, w=w, k=k, ksrc=ksrc, layout=layout, evac=evac, dst=dst))
    return st


def proj_pe(c, pe, st):
    for sem, v in st['waits']:
        pe.wait_ge(c.s[sem], v)
    for tl in st['tiles']:
        t, w, k = tl['t'], tl['w'], tl['k']
        if t >= 2:
            pe.wait_ge(c.s['proj_evac_a'], t - 1)
            pe.wait_ge(c.s['proj_evac_b'], t - 1)
        for j, _, _ in tl['jobs']:
            wait_job(c, pe, j)
        parts = [(j, k0 + i, i, kk) for j, k0, kk in tl['jobs'] for i in range(kk)]
        for half in range(2):
            bank = c.pb[4 + 2 * (t % 2) + half]
            if tl['layout'] == 'tok':
                for j, kc, i, kk in parts:
                    mm = pe.matmul(bank[:, 0:w], st['src'][:, tl['ksrc'] + kc, half * P:half * P + P],
                                   slot_of(c, j, kk, w)[:, i, :], start=kc == 0, stop=kc == k - 1)
            else:
                n = w // (2 * P)
                for u in range(n):
                    col = (half * n + u) * P
                    for j, kc, i, kk in parts:
                        mm = pe.matmul(bank[:, u * S:u * S + S], slot_of(c, j, kk, w)[:, i, col:col + P],
                                       st['src'][:, tl['ksrc'] + kc, :], start=kc == 0, stop=kc == k - 1)
            mm.then_inc(c.s['proj_done'], 1)


def proj_out(c, tl, half):
    w = tl['w']
    bank = c.pb[4 + 2 * (tl['t'] % 2) + half]
    if tl['layout'] == 'tok':
        return bank[:, 0:w], tl['dst'](half)
    n = w // (2 * P)
    return bank[:, 0:n * S].rearrange('p (u t) -> p u t', u=n), tl['dst'](half * n, n)


def proj_act(c, act, st):
    for tl in st['tiles']:
        if tl['evac'] == 'copy':
            act.wait_ge(c.s['proj_done'], 2 * tl['t'] + 1)
            src, dst = proj_out(c, tl, 0)
            act.activation(dst, src, ACT.Copy).then_inc(c.s['proj_evac_a'], 1)


def proj_dve(c, dve, st):
    for tl in st['tiles']:
        t, w = tl['t'], tl['w']
        if tl['evac'] == 'copy':
            dve.wait_ge(c.s['proj_done'], 2 * t + 2)
            src, dst = proj_out(c, tl, 1)
            dve.tensor_copy(dst, src).then_inc(c.s['proj_evac_b'], 1)
            continue
        for half in range(2):
            dve.wait_ge(c.s['proj_done'], 2 * t + 1 + half)
            src, dst = proj_out(c, tl, half)
            if tl['evac'] == 'add':
                signal(dve, dve.tensor_tensor(dst, src, dst, ALU.add), c.s['proj_evac_' + 'ab'[half]], t + 1)
            else:
                tmp = c.tmp[:, 0:w]
                gate = c.grow[:, 0, tl['evac']:tl['evac'] + w]
                signal(dve, dve.tensor_tensor(tmp, src, gate, ALU.mult), c.s['proj_evac_' + 'ab'[half]], t + 1)
                c.vstep(dve.tensor_tensor(dst, dst, tmp, ALU.add))
    if st['tiles'][-1]['evac'] != 'copy':
        dve.wait_ge(c.s['proj_evac_b'], st['tiles'][-1]['t'] + 1)
        c.x_written(dve)


def proj_evacuated(st):
    last = st['tiles'][-1]['t'] + 1
    return [('proj_evac_a', last), ('proj_evac_b', last)]


def norm_act(c, act, st):
    k = st['k']
    for sem, v in st['waits']:
        act.wait_ge(c.s[sem], v)
    for n in range(NT):
        act.activation(c.xn[:, n, :], st['src'][:, n, :], ACT.Square,
                       accum_out=c.ss[:, n:n + 1]).then_inc(c.s['norm_ss'], 1)
        act.wait_ge(c.s['norm_ss'], NT * k + n + 1)
    for j in (0, 2):
        act.wait_ge(c.s['norm_turned'], 4 * k + j + 1)
        for i in range(2):
            kc = 2 * j + i
            scale, shift = st['scale'](kc), st['shift'](kc) if st['shift'] else 0.0
            o = act.activation(c.hT[:, kc, :], c.pb[j][:, i * S:i * S + S],
                               ACT.Identity if st['shift'] else ACT.Copy, bias=shift, scale=scale)
        o.then_inc(c.s['hT_act'], 1)


def norm_pool(c, pool, st):
    k = st['k']
    pool.wait_ge(c.s['norm_ss'], NT * k + NT)
    c.pstep(pool.tensor_scalar(c.ms[:, 0:NT], c.ss[:, 0:NT], 1.0 / D, EPS, ALU.mult, ALU.add))
    pool.tensor_tensor(c.rstd[:, 0:NT], c.ms[:, 0:NT], c.neghalf[:, 0:NT], ALU.pow)\
        .then_inc(c.s['norm_rstd'], 1)


def norm_dve(c, dve, st):
    k = st['k']
    dve.wait_ge(c.s['norm_rstd'], k + 1)
    for sem, v in st['waits']:
        dve.wait_ge(c.s[sem], v)
    for n in range(NT):
        dve.tensor_scalar(c.xn[:, n, :], st['src'][:, n, :], c.rstd[:, n:n + 1], None, ALU.mult)\
           .then_inc(c.s['norm_xn'], 1)
    for j in (1, 3):
        dve.wait_ge(c.s['norm_turned'], 4 * k + j + 1)
        for i in range(2):
            kc = 2 * j + i
            shift = st['shift'](kc) if st['shift'] else 0.0
            o = dve.tensor_scalar(c.hT[:, kc, :], c.pb[j][:, i * S:i * S + S], st['scale'](kc), shift,
                                  ALU.mult, ALU.add)
        o.then_inc(c.s['hT_dve'], 1)


def norm_pe(c, pe, st):
    k = st['k']
    pe.wait_ge(c.s['norm_xn'], NT * (k + 1))
    for j in range(4):
        for i in range(2):
            for n in range(NT):
                kc = 2 * j + i
                mm = pe.transpose(c.pb[j][:, i * S + n * P:i * S + n * P + P],
                                  c.xn[:, n, kc * P:kc * P + P], c.ident[:, :])
        mm.then_inc(c.s['norm_turned'], 1)


def hT_ready(k):
    return [('hT_act', 2 * (k + 1)), ('hT_dve', 2 * (k + 1))]


def final_act(c, act, st):
    k = st['k']
    act.wait_ge(c.s['x_ready'], st['x_before'])
    for n in range(NT):
        act.activation(c.xn[:, n, :], c.x[:, n, :], ACT.Square,
                       accum_out=c.ss[:, n:n + 1]).then_inc(c.s['final_ss'], 1)
        act.wait_ge(c.s['final_ss'], NT * k + n + 1)


def final_pool(c, pool, st):
    k = st['k']
    pool.wait_ge(c.s['final_ss'], NT * (k + 1))
    c.pstep(pool.tensor_scalar(c.ms[:, 0:NT], c.ss[:, 0:NT], 1.0 / D, EPS, ALU.mult, ALU.add))
    pool.tensor_tensor(c.rstd[:, 0:NT], c.ms[:, 0:NT], c.neghalf[:, 0:NT], ALU.pow)\
        .then_inc(c.s['final_rstd'], 1)


def final_dve(c, dve, st):
    k = st['k']
    dve.wait_ge(c.s['final_rstd'], k + 1)
    dve.wait_ge(c.s['gain_row'], 16 * (k + 1))
    for n in range(NT):
        c.vstep(dve.scalar_tensor_tensor(c.x[:, n, :], c.x[:, n, :], c.rstd[:, n:n + 1], c.gain[:, :],
                                         ALU.mult, ALU.mult))
    c.x_written(dve)


def final_sp(c, act, st):
    for sem, v in st['waits']:
        act.wait_ge(c.s[sem], v)
    act.dma_start(c.gain[:, :], st['gain'].rearrange('(a n) -> a n', a=1).partition_broadcast(P))\
       .then_inc(c.s['gain_row'], 16)


def ffn_stage(core, gate_view, up_view, up_col, down_view, gated, k):
    st = dict(kind='ffn', k=k, gate=gate_view, up=up_view, up_col=up_col, down=down_view, gated=gated,
              j0=len(core.jobs), steps=F_DENSE // FT)
    for i in range(st['steps']):
        for q in range(2):
            job(core, None, ('ffn_gu', st['steps'] * 2 * k + 2 * i + 2))
        job(core, None, ('ffn_down', st['steps'] * 2 * k + 2 * i + 2))
    return st


def ffn_load(c, sp, st, q, i, slot):
    w = c.ring[:, slot, :]
    if q < 2:
        w = w.rearrange('p (k s n) -> p k s n', k=4, s=2)
        sp.dma_start(w[:, :, 0, :], st['gate'][:, 4 * q:4 * q + 4, bass.ds(i * FT, FT)])\
          .then_inc(c.landed[slot], 16)
        sp.dma_start(w[:, :, 1, :], st['up'][:, 4 * q:4 * q + 4, bass.ds(i * FT + st['up_col'], FT)])\
          .then_inc(c.landed[slot], 16)
    else:
        w = w.rearrange('p (k n) -> p k n', k=2)
        for a in range(2):
            sp.dma_start(w[:, a:a + 1, :], st['down'][:, bass.ds(i * 2 + a, 1), :])\
              .then_inc(c.landed[slot], 16)


def ffn_sp(c, sp, st):
    k, j0, steps = st['k'], st['j0'], st['steps']
    base = 2 * steps * k

    def load(q, i, j):
        sem, v = c.jobs[j - RING][1]
        sp.wait_ge(c.s[sem], v)
        ffn_load(c, sp, st, q, i, j % RING)
    for i in range(2):
        for q in range(3):
            load(q, i, j0 + 3 * i + q)
    with sp.Fori(1, steps // 2) as it:
        for r in range(2):
            for q in range(3):
                sp.wait_ge(c.s['ffn_gu' if q < 2 else 'ffn_down'], it * 4 + (base + 2 * r + 2 - 4))
                ffn_load(c, sp, st, q, it * 2 + r, (j0 + 3 * r + q) % RING)
    for q in range(3):
        load(q, steps - 1, j0 + 3 * (steps - 1) + q)


def ffn_loop(eng, steps, body):
    for i in range(2):
        body(i, i % 2, i)
    with eng.Fori(1, steps // 2) as it:
        for r in range(2):
            body(None, r, it * 2 + r)
    body(steps - 1, 0, steps - 1)


def ffn_pe(c, pe, st):
    k, j0, steps = st['k'], st['j0'], st['steps']
    base = 2 * steps * k
    for sem, v in st['waits']:
        pe.wait_ge(c.s[sem], v)

    def landed(q, r, m):
        j = j0 + 3 * r + q
        pe.wait_ge(c.landed[j % RING], (m - r) * (LOAD // 2) + LOAD * (j // RING + 1))
        return c.ring[:, j % RING, :]

    def gate_up(n, r, q):
        w = c.ring[:, (j0 + 3 * r + q) % RING, :].rearrange('p (k w) -> p k w', k=4)
        for i in range(4):
            mm = pe.matmul(c.pb[4 + n][:, :], c.hT[:, 4 * q + i, n * P:n * P + P], w[:, i, :],
                           start=q + i == 0, stop=q + i == 4)
        return mm

    def turn(n, m):
        pe.wait_ge(c.s[f'ffn_act{n}'], m + (steps * k + 1))
        for a in range(2):
            mm = pe.transpose(c.pb[6 + n][:, a * P:a * P + P], c.fa[:, n, a * P:a * P + P], c.ident[:, :])
        mm.then_inc(c.s[f'ffn_turned{n}'], 1)

    def down(n, r, m, first, last):
        landed(2, r, m)
        pe.wait_ge(c.s[f'ffn_actT{n}'], m + (steps * k + 1))
        w = c.ring[:, (j0 + 3 * r + 2) % RING, :].rearrange('p (k n) -> p k n', k=2)
        for h in range(2):
            for a in range(2):
                mm = pe.matmul(c.pb[2 * n + h][:, :], c.faT[:, n, a, :], w[:, a, h * 512:h * 512 + 512],
                               start=first and a == 0, stop=last and a == 1, skip_group_check=True)
        mm.then_inc(c.s['ffn_down'], 1)

    def body(i, r, m):
        first = i == 0
        landed(0, r, m)
        if not first:
            pe.wait_ge(c.s['ffn_act0'], m + steps * k)
        gate_up(0, r, 0)
        if not first:
            turn(1, m - 1)
        landed(1, r, m)
        gate_up(0, r, 1).then_inc(c.s['ffn_gu'], 1)
        if not first:
            down(1, 1 - r, m - 1, i == 1, False)
        gate_up(1, r, 0)
        turn(0, m)
        gate_up(1, r, 1).then_inc(c.s['ffn_gu'], 1)
        down(0, r, m, first, i == steps - 1)
    ffn_loop(pe, steps, body)
    turn(1, steps - 1)
    down(1, 0, steps - 1, False, True)


def ffn_act(c, act, st):
    k, steps = st['k'], st['steps']
    base = 2 * steps * k

    def silu(n, m):
        act.wait_ge(c.s['ffn_gu'], m * 2 + (base + n + 1))
        act.activation(c.fs[:, n, :], c.pb[4 + n][:, 0:FT], ACT.Silu).then_inc(c.s[f'ffn_silu{n}'], 1)

    def copyT(n, m):
        act.wait_ge(c.s[f'ffn_turned{n}'], m + (steps * k + 1))
        act.activation(c.faT[:, n, :, :], c.pb[6 + n][:, 0:2 * P].rearrange('p (a t) -> p a t', a=2),
                       ACT.Copy).then_inc(c.s[f'ffn_actT{n}'], 1)

    def body(i, r, m):
        if i != 0:
            copyT(1, m - 1)
        silu(0, m)
        copyT(0, m)
        silu(1, m)
    ffn_loop(act, steps, body)
    copyT(1, steps - 1)


def ffn_dve(c, dve, st):
    k, steps = st['k'], st['steps']

    def body(i, r, m):
        for n in range(NT):
            dve.wait_ge(c.s[f'ffn_silu{n}'], m + (steps * k + 1))
            dve.tensor_tensor(c.fa[:, n, :], c.fs[:, n, :], c.pb[4 + n][:, FT:2 * FT], ALU.mult)\
               .then_inc(c.s[f'ffn_act{n}'], 1)
    ffn_loop(dve, steps, body)
    base = 2 * steps * k
    for n in range(NT):
        dve.wait_ge(c.s['ffn_down'], base + 2 * steps - 1 + n)
        for h in range(2):
            out = c.x[:, n, h * 512:h * 512 + 512]
            if st['gated']:
                c.vstep(dve.tensor_tensor(c.tmp[:, :], c.pb[2 * n + h][:, :],
                                          c.grow[:, 1, h * 512:h * 512 + 512], ALU.mult))
                c.vstep(dve.tensor_tensor(out, out, c.tmp[:, :], ALU.add))
            else:
                c.vstep(dve.tensor_tensor(out, out, c.pb[2 * n + h][:, :], ALU.add))
    c.x_written(dve)


ADA_VECTORS = ((0, 1), (3, 4))
ADA_EVENTS = 20


def ada_stage(core, layer, part):
    view = rows_view(core.t['w_ada'][layer])
    st = dict(kind='ada', k=layer, part=part, cols=[], rows=[])
    n = ADA_EVENTS * layer + 8 * part
    for vi, vec in enumerate(ADA_VECTORS[part]):
        for q in range(4):
            n += 1
            col = vec * D + q * 256
            loads = [(0, 4, 256, view[:, 0:4, col:col + 256]), (1024, 4, 256, view[:, 4:8, col:col + 256])]
            st['cols'].append((job(core, loads, ('ada_done', n)), 16 * part + 8 * vi + 2 * q))
    if part:
        for g, vec in enumerate((2, 5)):
            for h in range(2):
                n += 1
                st['rows'].append((gemm_jobs(core, view, vec * D + 512 * h, 512, KD, ('ada_done', n)), g, h))
    return st


def ada_pe(c, pe, st):
    pe.wait_ge(c.s['cond_ready'], 2)
    if st['x_before']:
        pe.wait_ge(c.s['x_ready'], st['x_before'])
    if st['k'] or st['part']:
        pe.wait_ge(c.s['ada_cols'], 2 * st['k'] + st['part'])
    for j, at in st['cols']:
        wait_job(c, pe, j)
        w = slot_of(c, j, KD, 256)
        for u in range(2):
            for kc in range(KD):
                mm = pe.matmul(c.pb[0][:, at + u:at + u + 1], w[:, kc, u * P:u * P + P],
                               c.condT[:, kc:kc + 1], start=kc == 0, stop=kc == KD - 1)
        mm.then_inc(c.s['ada_done'], 1)
    for i, (jobs, g, h) in enumerate(st['rows']):
        if i == 3:
            pe.wait_ge(c.s['ada_rows'], 4 * st['k'] + 1)
        for j, _, _ in jobs:
            wait_job(c, pe, j)
        for j, k0, kk in jobs:
            for a in range(kk):
                mm = pe.matmul(c.pb[1 + i % 3][:, :], c.condB[:, k0 + a, :], slot_of(c, j, kk, 512)[:, a, :],
                               start=k0 + a == 0, stop=k0 + a == KD - 1)
        mm.then_inc(c.s['ada_done'], 1)


def ada_act(c, act, st):
    if st['part']:
        if st['x_before']:
            act.wait_ge(c.s['x_ready'], st['x_before'])
        for g, vec in enumerate((2, 5)):
            act.dma_start(c.grow[:, g, :], c.t['b_ada'][st['k']:st['k'] + 1, vec * D:vec * D + D]
                          .partition_broadcast(P)).then_inc(c.s['gate_bias'], 16)


def ada_dve(c, dve, st):
    k, part = st['k'], st['part']
    dve.wait_ge(c.s['ada_done'], ADA_EVENTS * k + 8 + 8 * part)
    lo = 16 * part
    bias = COL2['b_ada'] + 48 * k + 8 * ADA_VECTORS[part][0]
    signal(dve, dve.tensor_tensor(c.modC[:, lo:lo + 16], c.pb[0][:, lo:lo + 16],
                                  c.col2[:, bias:bias + 16], ALU.add), c.s['ada_cols'], 2 * k + part + 1)
    gain = COL1['g_norm_ffn' if part else 'g_norm_mix'] + 8 * k
    dve.scalar_tensor_tensor(c.modA[:, 8 * part:8 * part + 8], c.modC[:, lo + 8:lo + 16], 1.0,
                             c.col1[:, gain:gain + 8], ALU.add, ALU.mult).then_inc(c.s['mod_ready'], 1)
    if part:
        dve.wait_ge(c.s['gate_bias'], 32 * (k + 1))
    for i, (_, g, h) in enumerate(st['rows']):
        dve.wait_ge(c.s['ada_done'], ADA_EVENTS * k + 17 + i)
        row = c.grow[:, g, h * 512:h * 512 + 512]
        dve.tensor_tensor(row, row, c.pb[1 + i % 3][:, :], ALU.add).then_inc(c.s['ada_rows'], 1)


def setup_act(c, act):
    t = c.t
    for n in range(NT):
        act.dma_start(c.x[:, n, :], t['x'][0, n * P:n * P + P, :]).then_inc(c.s['x_loaded'], 16)
    n_in = 0

    def load(dst, src, **kw):
        act.dma_start(dst, src, **kw).then_inc(c.s['params_loaded'], 16)
    for rows, buf, at in ((ROWS1, c.prow1, COL1), (ROWS2, c.prow2, COL2)):
        for name, how, n in rows:
            a = t[name]
            load(buf[at[name]:at[name] + n, :], a.rearrange(how, p=P))
    for i, name in enumerate(('positions', 'positions_2')):
        load(c.posi[:, 2 * i:2 * i + 2], t[name].rearrange('a (n p) -> p (a n)', p=P), allow_slow_non_contiguous=True)
    load(c.onorm[:, :, :], t['hgrn_out_norm'].rearrange('(a l) v -> a l v', a=1).partition_broadcast(P))
    load(c.vng[:, :, :], t['gmlp_vnorm_g'].rearrange('(a l) v -> a l v', a=1).partition_broadcast(P))
    load(c.vnb[:, :, :], t['gmlp_vnorm_b'].rearrange('(a l) v -> a l v', a=1).partition_broadcast(P))
    load(c.mlg[:, :], t['od_ml_norm_g_2'].partition_broadcast(P))
    load(c.gbias[:, :], t['od_gate_bias_2'].partition_broadcast(P))
    load(c.wrouter[:, :, :], t['moe_w_router'][0].rearrange('(k p) e -> p k e', p=P))
    load(c.wpool[:, :, :], t['ev_pool_w_2'][0].rearrange('g c d -> c g d'))
    load(c.wsraw[:, :, :], t['gmlp_w_s'].rearrange('l g t s -> t (l g) s'))
    act.wait_ge(c.s['cols_ready'], 2)
    at = COL2['c']
    signal(act, act.activation(c.condT[:, :], c.col2[:, at:at + KD], ACT.Silu), c.s['cond_ready'], 1)
    act.wait_ge(c.s['angles_ready'], 2)
    act.activation(c.sin[:, :], c.ang[:, :], ACT.Sin).then_inc(c.s['rope_ready'], 1)
    act.activation(c.cos[:, :], c.angc[:, :], ACT.Sin).then_inc(c.s['rope_ready'], 1)


N_PARAM_LOADS = len(ROWS1) + len(ROWS2) + 2 + 3 + 2 + 1 + 2


def setup_pool(c, pool):
    step = c.pstep
    step(pool.memset(c.ident[:, :], 0.0))
    step(pool.affine_select(out=c.ident[:, :], in_=c.ident[:, :], compare_op=ALU.not_equal, fill=1.0, base=0,
                            pattern=[[-1, P]], channel_multiplier=1))
    step(pool.memset(c.ones[:, :], 1.0))
    step(pool.affine_select(out=c.triT[:, :], in_=c.ones[:, 0:P], compare_op=ALU.is_ge, fill=0.0, base=0,
                            pattern=[[1, P]], channel_multiplier=-1))
    step(pool.memset(c.zero[:, :], 0.0))
    step(pool.memset(c.maskQ2[:, 0:P], 0.0))
    step(pool.affine_select(out=c.maskQ2[:, P:2 * P], in_=c.zero[:, 0:P], compare_op=ALU.is_ge, fill=NEG, base=0,
                            pattern=[[-1, P]], channel_multiplier=1))
    step(pool.affine_select(out=c.maskK[:, :], in_=c.zero[:, 0:P], compare_op=ALU.is_ge, fill=NEG, base=0,
                            pattern=[[1, P]], channel_multiplier=-1))
    step(pool.memset(c.neghalf[:, :], -0.5))
    for j in range(HD // 2):
        step(pool.memset(c.invf[:, j:j + 1], float(np.float32(10000.0 ** (-j / 32.0)))))
    step(pool.memset(c.selT[:, :, :], 0.0))
    step(pool.affine_select(out=c.selT[:, :, :], in_=c.selT[:, :, :], compare_op=ALU.not_equal, fill=1.0, base=0,
                            pattern=[[-1, 8], [0, P]], channel_multiplier=1))
    step(pool.iota(c.iotaT[:, :], pattern=[[1, P]], base=0, channel_multiplier=0))
    step(pool.iota(c.iotaS[:, :], pattern=[[0, P]], base=0, channel_multiplier=1))
    step(pool.iota(c.iota1[:, :], pattern=[[1, 16]], base=1, channel_multiplier=0))
    step(pool.memset(c.resume[:, :], 1.0))
    step(pool.memset(c.resume[:, :].rearrange('p (c t) -> p c t', t=CHUNK)[:, :, 0:1], 0.0))
    step(pool.memset(c.AT[:, :, :, :], 0.0))
    pool.memset(c.sink[:, :], 0.0).then_inc(c.s['consts_ready'], 1)


LEVELS = (64, 32, 16, 8, 4, 2, 1)


def setup_dve(c, dve):
    step = c.vstep
    dve.wait_ge(c.s['consts_ready'], 1)
    dve.wait_ge(c.s['params_loaded'], 16 * N_PARAM_LOADS)
    for i, (buf, n) in enumerate(((c.col1, NCOL1), (c.col2, NCOL2))):
        dve.wait_ge(c.s['params_turned'], i + 1)
        signal(dve, dve.tensor_copy(buf[:, 0:n], c.pb[i][:, 0:n]), c.s['cols_ready'], i + 1)
    for i in range(2):
        dve.wait_ge(c.s['ws_turned'], i + 1)
        step(dve.tensor_tensor(c.wsT[:, 4 * i:4 * i + 4, :], c.pb[2 + i][:, :].rearrange('p (g t) -> p g t', g=4),
                               c.triT[:, :].unsqueeze(1).broadcast_to([P, 4, P]), ALU.mult))
    dve.wait_ge(c.s['cond_ready'], 1)
    signal(dve, dve.tensor_copy(c.condB[:, :, :], c.condT[:, :].unsqueeze(2).broadcast_to([P, KD, P])),
           c.s['cond_ready'], 2)
    step(dve.tensor_copy(c.posf[:, :], c.posi[:, :]))
    for i in range(2):
        step(dve.tensor_scalar(c.ang[:, 32 * i:32 * i + 32], c.invf[:, :], c.posf[:, i:i + 1], None, ALU.mult))
        step(dve.tensor_scalar(c.ang[:, 64 + 16 * i:80 + 16 * i], c.invf[:, 0:32:2], c.posf[:, 2 + i:3 + i], None,
                               ALU.mult))
    turn = 2 * np.pi
    c1 = 6.28125
    c2 = float(np.float32(np.round((turn - c1) * 2 ** 24) / 2 ** 24))
    c3 = float(np.float32(turn - c1 - c2))
    magic = 12582912.0
    step(dve.tensor_scalar(c.turns[:, :], c.ang[:, :], float(1 / turn), magic, ALU.mult, ALU.add))
    step(dve.tensor_scalar(c.turns[:, :], c.turns[:, :], magic, None, ALU.subtract))
    for part in (c1, c2, c3):
        step(dve.scalar_tensor_tensor(c.ang[:, :], c.turns[:, :], -part, c.ang[:, :], ALU.mult, ALU.add))
    signal(dve, dve.tensor_scalar(c.ang[:, :], c.ang[:, :], 3.1415925, -3.1415925, ALU.min, ALU.max),
           c.s['angles_ready'], 1)
    step(dve.scalar_tensor_tensor(c.angc[:, :], c.ang[:, :], -1.0, c.ang[:, :], ALU.mult, ALU.min))
    signal(dve, dve.tensor_scalar(c.angc[:, :], c.angc[:, :], float(np.pi / 2), None, ALU.add),
           c.s['angles_ready'], 2)
    step(dve.tensor_tensor(c.xor[:, :], c.iotaS[:, :], c.iotaT[:, :], ALU.bitwise_xor))
    step(dve.tensor_tensor(c.less[:, :], c.iotaS[:, :], c.iotaT[:, :], ALU.is_lt))
    for i, b in enumerate(LEVELS):
        step(dve.tensor_scalar(c.bits[:, :], c.xor[:, :], int(np.log2(b)), None, ALU.logical_shift_right))
        step(dve.scalar_tensor_tensor(c.lmask[:, i, :], c.bits[:, :], 1.0, c.less[:, :], ALU.is_equal, ALU.mult))
    step(dve.tensor_tensor(c.lmask[:, len(LEVELS), :], c.iotaS[:, :], c.iotaT[:, :], ALU.is_equal))
    step(dve.tensor_copy(c.slotF2[:, 0:P], c.iotaT[:, :]))
    step(dve.tensor_scalar(c.slotF2[:, P:2 * P], c.slotF2[:, 0:P], float(P), None, ALU.add))
    step(dve.tensor_copy(c.slotP[:, 0:1], c.iotaS[:, 0:1]))
    step(dve.tensor_copy(c.inv1[:, :], c.iota1[:, :]))
    step(dve.reciprocal(c.inv1[:, :], c.inv1[:, :]))


def setup_pe(c, pe):
    pe.wait_ge(c.s['consts_ready'], 1)
    pe.wait_ge(c.s['params_loaded'], 16 * N_PARAM_LOADS)
    for i, (buf, n) in enumerate(((c.prow1, NCOL1), (c.prow2, NCOL2))):
        pe.transpose(c.pb[i][:, 0:n], buf[0:n, :], c.ident[0:n, 0:n]).then_inc(c.s['params_turned'], 1)
    for i in range(2):
        for g in range(4):
            mm = pe.transpose(c.pb[2 + i][:, g * P:g * P + P], c.wsraw[:, 4 * i + g, :], c.ident[:, :])
        mm.then_inc(c.s['ws_turned'], 1)


def att_blocks(a, n):
    return a['heads'] * (a['keys'](n) // P)


def attend_plan(core, a):
    a['calls'] = []
    for n in range(NT):
        nb = -(-att_blocks(a, n) // 4)
        a['calls'].append(dict(a=core.att['a'], e0=core.att['e'], t0=core.att['t'], a0=core.att['ta'],
                               b0=core.att['tb'], nb=nb))
        core.att['a'] += 1
        core.att['e'] += a['heads']
        core.att['t'] += nb
        core.att['ta'] += (nb + 1) // 2
        core.att['tb'] += nb // 2
    return a


def attend_pe(c, pe, a):
    H = a['heads']
    for sem, v in a['ready']:
        pe.wait_ge(c.s[sem], v)
    for n in range(NT):
        call, s = a['calls'][n], a['keys'](n)
        for bank, rows in enumerate(a['banks']):
            for u, i in enumerate(rows):
                mm = pe.matmul(c.pb[bank][:, u * S:u * S + s], a['q'](i, n), a['k'](i, n), start=True, stop=True)
        mm.then_inc(c.s['att_scores'], 1)
        pe.wait_ge(c.s['att_probs'], call['a'] + 1)
        nblk = att_blocks(a, n)
        for b in range(call['nb']):
            if b >= 3:
                x = b - 3
                pe.wait_ge(c.s['att_PT_' + 'ab'[x % 2]], call['ab'[x % 2] + '0'] + x // 2 + 1)
            for blk in range(4 * b, min(4 * b + 4, nblk)):
                ch, i = divmod(blk, H)
                mm = pe.transpose(c.pb[4 + b % 3][:, (blk % 4) * P:(blk % 4) * P + P],
                                  c.L[:, i * S + ch * P:i * S + ch * P + P], c.ident[:, :])
            mm.then_inc(c.s['att_turned'], 1)
        pe.wait_ge(c.s['att_PT_a'], call['a0'] + (call['nb'] + 1) // 2)
        if call['nb'] > 1:
            pe.wait_ge(c.s['att_PT_b'], call['b0'] + call['nb'] // 2)
        if call['a']:
            pe.wait_ge(c.s['att_mixT'], call['a'])
        for out, terms in a['pv'](n):
            for x, (v, blk, m) in enumerate(terms):
                mm = pe.matmul(out, v, c.PT[:, blk * P:(blk + m) * P], start=x == 0, stop=x == len(terms) - 1)
        mm.then_inc(c.s['att_out'], 1)


def attend_dve(c, dve, a):
    H = a['heads']
    L = c.L[:, :].rearrange('p (h s) -> p h s', s=S)
    for n in range(NT):
        call, s = a['calls'][n], a['keys'](n)
        if a['mask'] is not None:
            for sem, v in a['mask_ready'](n):
                dve.wait_ge(c.s[sem], v)
        dve.wait_ge(c.s['att_scores'], call['a'] + 1)
        for bank, rows in enumerate(a['banks']):
            m, i = len(rows), rows[0]
            src = c.pb[bank][:, 0:m * S].rearrange('p (h s) -> p h s', s=S)[:, :, 0:s]
            if a['mask'] is None:
                c.vstep(dve.tensor_copy(L[:, i:i + m, 0:s], src))
            else:
                mask = a['mask'](n).unsqueeze(1).broadcast_to([P, m, s])
                c.vstep(dve.tensor_tensor(L[:, i:i + m, 0:s], src, mask, ALU.add))
        c.vstep(dve.tensor_reduce(c.mx[:, 0:H], L[:, 0:H, 0:s], AX, ALU.max))
        dve.tensor_scalar(c.nmx[:, 0:H], c.mx[:, 0:H], -a['scale'], None, ALU.mult)\
           .then_inc(c.s['att_max'], 1)
        dve.wait_ge(c.s['att_exp'], call['e0'] + H)
        c.vstep(dve.reciprocal(c.rsum[:, 0:H], c.esum[:, 0:H]))
        dve.tensor_tensor(L[:, 0:H, 0:s], L[:, 0:H, 0:s], c.rsum[:, 0:H].unsqueeze(2).broadcast_to([P, H, s]),
                          ALU.mult).then_inc(c.s['att_probs'], 1)
        nblk = att_blocks(a, n)
        for b in range(1, call['nb'], 2):
            dve.wait_ge(c.s['att_turned'], call['t0'] + b + 1)
            w = min(4, nblk - 4 * b) * P
            dve.tensor_copy(c.PT[:, 4 * b * P:4 * b * P + w], c.pb[4 + b % 3][:, 0:w]).then_inc(c.s['att_PT_b'], 1)


def attend_act(c, act, a):
    H = a['heads']
    for n in range(NT):
        call, s = a['calls'][n], a['keys'](n)
        act.wait_ge(c.s['att_max'], call['a'] + 1)
        for i in range(H):
            row = c.L[:, i * S:i * S + s]
            act.activation(row, row, ACT.Exp, bias=c.nmx[:, i:i + 1], scale=a['scale'],
                           accum_out=c.esum[:, i:i + 1]).then_inc(c.s['att_exp'], 1)
        nblk = att_blocks(a, n)
        for b in range(0, call['nb'], 2):
            act.wait_ge(c.s['att_turned'], call['t0'] + b + 1)
            w = min(4, nblk - 4 * b) * P
            act.activation(c.PT[:, 4 * b * P:4 * b * P + w], c.pb[4 + b % 3][:, 0:w], ACT.Copy)\
               .then_inc(c.s['att_PT_a'], 1)
        act.wait_ge(c.s['att_out'], call['a'] + 1)
        dst = a['out'](n)
        act.activation(dst, c.pb[7][:, 0:dst.shape[1] * P].rearrange('p (m t) -> p m t', t=P), ACT.Copy)\
           .then_inc(c.s['att_mixT'], 1)


def rotate(c, dve, x, out, heads, half, cos, sin, s1, s2):
    x4 = x.rearrange('p h (a j) -> p h a j', a=2)
    o4 = out.rearrange('p h (a j) -> p h a j', a=2)
    v1 = s1.rearrange('p (h a j) -> p h a j', a=2, j=half)
    v2 = s2.rearrange('p (h a j) -> p h a j', a=2, j=half)
    full = [P, heads, 2, half]
    c.vstep(dve.tensor_tensor(v1, x4, cos.unsqueeze(1).unsqueeze(1).broadcast_to(full), ALU.mult))
    c.vstep(dve.tensor_tensor(v2, x4, sin.unsqueeze(1).unsqueeze(1).broadcast_to(full), ALU.mult))
    c.vstep(dve.tensor_tensor(o4[:, :, 0, :], v1[:, :, 0, :], v2[:, :, 1, :], ALU.subtract))
    c.vstep(dve.tensor_tensor(o4[:, :, 1, :], v1[:, :, 1, :], v2[:, :, 0, :], ALU.add))


def dsa_stage(core, k, evacuated):
    c = core
    order = [0, 2, 4, 1, 3, 5]
    a = dict(heads=A_HEADS, scale=HD ** -0.5, banks=[[0, 1], [2], [3, 4], [5]],
             keys=lambda n: P * (n + 1),
             q=lambda i, n: c.rT[HD * (order[i] % 2):HD * (order[i] % 2) + HD, order[i] // 2, n * P:n * P + P],
             k=lambda i, n: c.rT[HD * (order[i] % 2):HD * (order[i] % 2) + HD, 3, 0:P * (n + 1)],
             mask=lambda n: c.sel[:, n, 0:P * (n + 1)],
             mask_ready=lambda n: [('dsa_bias', 2 * k + n + 1)],
             pv=lambda n: [(c.pb[7][HD * g:HD * g + HD, 0:3 * P],
                            [(c.z[:, ch, Z_AV:Z_AV + HD], ch * A_HEADS + 3 * g, 3) for ch in range(n + 1)])
                           for g in range(2)],
             out=lambda n: c.mixT[:, 0:3, n * P:n * P + P], ready=[('dsa_rel', 2 * k + 2)])
    return dict(kind='dsa', k=k, evacuated=evacuated, att=attend_plan(core, a))


def dsa_dve(c, dve, st):
    k = st['k']
    for sem, v in st['evacuated']:
        dve.wait_ge(c.s[sem], v)
    if k == 0:
        dve.wait_ge(c.s['rope_ready'], 2)
    rot = c.xn[:, :, :].rearrange('p n d -> p (n d)')[:, 0:NT * 14 * HD].rearrange('p (n h d) -> p n h d', n=NT, h=14)
    for n in range(NT):
        cos, sin = c.cos[:, 32 * n:32 * n + 32], c.sin[:, 32 * n:32 * n + 32]
        for at, slot, heads in ((Z_AQ, 0, 7), (Z_IQ, 8, 5)):
            w = heads * HD
            rotate(c, dve, c.z[:, n, at:at + w].rearrange('p (h d) -> p h d', d=HD), rot[:, n, slot:slot + heads, :],
                   heads, HD // 2, cos, sin, c.L[:, 0:w], c.L[:, 512:512 + w])
        c.vstep(dve.tensor_copy(rot[:, n, 7, :], rot[:, n, 6, :]))
        dve.tensor_copy(rot[:, n, 13, :], rot[:, n, 12, :]).then_inc(c.s['dsa_rot'], 1)
        c.vstep(dve.tensor_scalar(c.iw[:, n, :], c.z[:, n, Z_IW:Z_IW + IDX_HEADS], IDX_HEADS ** -0.5, None, ALU.mult))
    for n in range(NT):
        dve.wait_ge(c.s['dsa_turned'], 4 * k + 2 * n + 2)
        dve.tensor_copy(c.rT[:, 4:7, n * P:n * P + P], c.pb[2 * n + 1][:, 0:3 * P]
                        .rearrange('p (m t) -> p m t', t=P)).then_inc(c.s['dsa_rT_b'], 1)
    for n in range(NT):
        s = P * (n + 1)
        dve.wait_ge(c.s['dsa_rel'], 2 * k + n + 1)
        score = c.score[:, n, 0:s]
        rel = c.L[:, n * 1024:n * 1024 + 1024].rearrange('p (h s) -> p h s', s=S)
        for h in range(IDX_HEADS):
            r = rel[:, 2 * (h % 2) + h // 2, 0:s]
            if h == 0:
                c.vstep(dve.tensor_scalar(score, r, c.iw[:, n, 0:1], None, ALU.mult))
            else:
                ins = dve.scalar_tensor_tensor(score, r, c.iw[:, n, h:h + 1], score, ALU.mult, ALU.add)
                if h < IDX_HEADS - 1:
                    c.vstep(ins)
        ins.then_inc(c.s['dsa_score'], 1)
    for n in range(NT):
        s = P * (n + 1)
        score, work, top = c.score[:, n, 0:s], c.work[:, 0:s], c.top8[:, :]
        dve.wait_ge(c.s['dsa_causal'], 2 * k + n + 1)
        src = score
        for r in range(TOPK // 8):
            c.vstep(dve.max(top, src))
            if r < TOPK // 8 - 1:
                c.vstep(dve.match_replace(work, top, src, TAKEN))
                src = work
        thr = c.top8[:, 7:8]
        sel, eq, pre = c.sel[:, n, 0:s], c.eq[:, 0:s], c.work[:, 0:s]
        c.vstep(dve.tensor_scalar(sel, score, thr, None, ALU.is_gt, ALU.add, accum_out=c.cnt[:, 0:1]))
        c.vstep(dve.tensor_scalar(c.cnt[:, 1:2], c.cnt[:, 0:1], -1.0, float(TOPK), ALU.mult, ALU.add))
        c.vstep(dve.tensor_scalar(eq, score, thr, None, ALU.is_equal))
        c.vstep(dve.tensor_tensor_scan(pre, c.ones[:, 0:s], eq, 0.0, ALU.mult, ALU.add))
        c.vstep(dve.scalar_tensor_tensor(eq, pre, c.cnt[:, 1:2], eq, ALU.is_le, ALU.mult))
        c.vstep(dve.tensor_tensor(sel, sel, eq, ALU.add))
        dve.tensor_scalar(sel, sel, 1.0, -NEG, ALU.subtract, ALU.mult).then_inc(c.s['dsa_sel'], 1)
    attend_dve(c, dve, st['att'])


def dsa_pool(c, pool, st):
    k = st['k']
    for buf, sem_in, sem_out, fill in ((c.score, 'dsa_score', 'dsa_causal', LOWEST), (c.sel, 'dsa_sel', 'dsa_bias', NEG)):
        for n in range(NT):
            pool.wait_ge(c.s[sem_in], 2 * k + n + 1)
            v = buf[:, n, 0:P * (n + 1)]
            pool.affine_select(out=v, in_=v, compare_op=ALU.is_ge, fill=fill, base=n * P,
                               pattern=[[-1, P * (n + 1)]], channel_multiplier=1).then_inc(c.s[sem_out], 1)


def dsa_pe(c, pe, st):
    k = st['k']
    rot = c.xn[:, :, :].rearrange('p n d -> p (n d)')
    for n in range(NT):
        pe.wait_ge(c.s['dsa_rot'], 2 * k + n + 1)
        for m in range(7):
            mm = pe.transpose(c.pb[2 * n + m // 4][:, (m % 4) * P:(m % 4) * P + P],
                              rot[:, (n * 7 + m) * P:(n * 7 + m) * P + P], c.ident[:, :])
            if m in (3, 6):
                mm.then_inc(c.s['dsa_turned'], 1)
    pe.wait_ge(c.s['dsa_rT_a'], 2 * k + 2)
    pe.wait_ge(c.s['dsa_rT_b'], 2 * k + 2)
    for n in range(NT):
        s = P * (n + 1)
        for g in range(2):
            for u in range(2):
                mm = pe.matmul(c.pb[2 * n + g][:, u * S:u * S + s], c.rT[HD * g:HD * g + HD, 4 + u, n * P:n * P + P],
                               c.rT[HD * g:HD * g + HD, 6, 0:s], start=True, stop=True)
        mm.then_inc(c.s['dsa_index'], 1)
    attend_pe(c, pe, st['att'])


def dsa_act(c, act, st):
    k = st['k']
    for n in range(NT):
        act.wait_ge(c.s['dsa_turned'], 4 * k + 2 * n + 1)
        act.activation(c.rT[:, 0:4, n * P:n * P + P], c.pb[2 * n][:, :].rearrange('p (m t) -> p m t', t=P),
                       ACT.Copy).then_inc(c.s['dsa_rT_a'], 1)
    for n in range(NT):
        s = P * (n + 1)
        act.wait_ge(c.s['dsa_index'], 2 * k + n + 1)
        rel = c.L[:, n * 1024:n * 1024 + 1024].rearrange('p (h s) -> p h s', s=S)
        for g in range(2):
            ins = act.activation(rel[:, 2 * g:2 * g + 2, 0:s],
                                 c.pb[2 * n + g][:, :].rearrange('p (u s) -> p u s', s=S)[:, :, 0:s],
                                 ACT.Relu, scale=HD ** -0.5)
        ins.then_inc(c.s['dsa_rel'], 1)
    attend_act(c, act, st['att'])


HG_LEVELS = ['cross'] + list(LEVELS) + ['diag']
HG_GROUPS = 1 + 2 * (len(LEVELS) + 1)
HG_EXPS = len(LEVELS) + 1


def hg_groups():
    return [(lv, n) for lv in range(len(HG_LEVELS)) for n in ((1,) if lv == 0 else (0, 1))]


def hg_buffers(c):
    w = PAIRS * S
    zT = c.zT[:, :, :].rearrange('p m t -> p (m t)')
    PT = c.PT[:, :]
    b = Core()
    b.q, b.f = zT[:, 0:w], zT[:, w:2 * w]
    b.D = [zT[:, 2 * w:3 * w], zT[:, 3 * w:4 * w]]
    b.k, b.b = zT[:, 4 * w:5 * w], PT[:, 0:w]
    b.QK = [PT[:, w:2 * w], c.L[:, 1024:1024 + w]]
    b.cross = c.L[:, 0:w]
    b.o = c.xn[:, 0, 0:w]
    b.sq = c.xn[:, 1, 0:w]
    return b


def by_block(ap, B):
    return ap.rearrange('p (b t) -> p b t', t=2 * B)


def hgrn_dve(c, dve, st):
    k = st['k']
    h = hg_buffers(c)
    for sem, v in st['evacuated']:
        dve.wait_ge(c.s[sem], v)

    def to_act(ins, sem='hg_gate'):
        ins.then_inc(c.s[sem], 1)
    to_act(magnitude(dve, h.D[0], h.f))
    if k:
        lb = COL2['hgrn_lb_logits']
        c.vstep(dve.tensor_tensor(c.lbd[:, 0:3], c.col2[:, lb:lb + 3], c.col2[:, lb + 3:lb + 6], ALU.subtract))
        c.vstep(dve.tensor_scalar(c.lbd[:, 3:6], c.lbd[:, 0:3], -1.0, None, ALU.mult))
        to_act(magnitude(dve, c.lbe[:, :], c.lbd[:, :]))
    dve.wait_ge(c.s['hg_log'], 1 if k == 0 else 4)
    c.vstep(dve.scalar_tensor_tensor(h.b, h.f, 0.0, h.D[0], ALU.min, ALU.subtract))
    if k:
        c.vstep(dve.scalar_tensor_tensor(c.lbl[:, :], c.lbd[:, :], 0.0, c.lbe[:, :], ALU.min, ALU.subtract))
    to_act(dve.tensor_tensor(h.k, h.b, h.f, ALU.subtract))
    lf = h.b
    if k:
        for p in range(PAIRS):
            v = slice(p * S, p * S + S)
            c.vstep(dve.tensor_scalar(h.D[1][:, v], h.b[:, v], c.lbd[:, p:p + 1], None, ALU.add))
        to_act(magnitude(dve, h.D[1], h.D[1]))
        for p in range(PAIRS):
            v = slice(p * S, p * S + S)
            c.vstep(dve.tensor_scalar(h.b[:, v], h.b[:, v], c.lbl[:, p:p + 1], c.lbl[:, 3 + p:4 + p], ALU.add, ALU.max))
        dve.wait_ge(c.s['hg_log'], 6)
        c.vstep(dve.tensor_tensor(h.b, h.b, h.D[1], ALU.add))
    c.vstep(dve.tensor_copy(h.D[0], lf))
    for p in range(PAIRS):
        v = slice(p * S, p * S + S)
        c.vstep(dve.tensor_tensor_scan(h.b[:, v], c.resume[:, :], h.D[0][:, v], 0.0, ALU.mult, ALU.add))
    dve.wait_ge(c.s['hg_log'], 2 if k == 0 else 5)
    b4 = h.b.rearrange('p (a c t) -> p a c t', a=PAIRS, c=4)
    n_exp = HG_EXPS * k

    def diff(lv):
        Dn = h.D[lv % 2]
        B = HG_LEVELS[lv]
        if B == 'cross':
            d4 = Dn.rearrange('p (a c t) -> p a c t', a=PAIRS, c=4)
            half = [P, PAIRS, 2, CHUNK]
            last = b4[:, :, :, CHUNK - 1:CHUNK]
            c.vstep(dve.tensor_tensor(d4[:, :, 0:2, :], b4[:, :, 0:2, :], last[:, :, 0:2, :].broadcast_to(half), ALU.subtract))
            one = [P, PAIRS, CHUNK]
            c.vstep(dve.tensor_tensor(d4[:, :, 0, :], d4[:, :, 0, :], last[:, :, 1, :].broadcast_to(one), ALU.subtract))
            c.vstep(dve.tensor_copy(d4[:, :, 2, :], b4[:, :, 2, :]))
            ins = dve.tensor_tensor(d4[:, :, 3, :], b4[:, :, 3, :], last[:, :, 2, :].broadcast_to(one), ALU.add)
        elif B == CHUNK:
            dv, bv = by_block(Dn, B), by_block(h.b, B)
            nb = S * PAIRS // (2 * B)
            c.vstep(dve.tensor_tensor(dv[:, :, 0:B], bv[:, :, 0:B], bv[:, :, B - 1:B].broadcast_to([P, nb, B]), ALU.subtract))
            ins = dve.tensor_copy(dv[:, :, B:2 * B], bv[:, :, B:2 * B])
        else:
            dv, bv = by_block(Dn, B), by_block(h.b, B)
            nb = S * PAIRS // (2 * B)
            ins = dve.tensor_tensor(dv, bv, bv[:, :, B - 1:B].broadcast_to([P, nb, 2 * B]), ALU.subtract)
        ins.then_inc(c.s['hg_diff'], 1)

    def queries_keys(lv):
        B = P if HG_LEVELS[lv] == 'cross' else HG_LEVELS[lv]
        dve.wait_ge(c.s['hg_exp'], n_exp + lv + 1)
        if lv >= 2:
            dve.wait_ge(c.s['hg_pairs'], HG_GROUPS * k + (1 + 2 * (lv - 2)))
        o, e = by_block(h.QK[lv % 2], B), by_block(h.D[lv % 2], B)
        c.vstep(dve.tensor_tensor(o[:, :, 0:B], e[:, :, 0:B], by_block(h.k, B)[:, :, 0:B], ALU.mult))
        dve.tensor_tensor(o[:, :, B:2 * B], e[:, :, B:2 * B], by_block(h.q, B)[:, :, B:2 * B], ALU.mult)\
           .then_inc(c.s['hg_QK'], 1)

    groups = hg_groups()

    def take(lv):
        for g, (glv, n) in enumerate(groups):
            if glv != lv:
                continue
            dve.wait_ge(c.s['hg_pairs'], HG_GROUPS * k + g + 1)
            for par in range(2):
                src = c.pb[2 * (g % 4) + par][:, 0:3 * P].rearrange('p (m t) -> p m t', t=P)
                if lv == 0:
                    dst = h.cross[:, par * 3 * P:(par + 1) * 3 * P].rearrange('p (m t) -> p m t', t=P)
                    ins = dve.tensor_copy(dst, src)
                else:
                    mask = c.lmask[:, lv - 1, :].unsqueeze(1).broadcast_to([P, 3, P])
                    ins = dve.copy_predicated(c.AT[:, n, 3 * par:3 * par + 3, :], mask, src)
            signal(dve, ins, c.s['hg_taken'], HG_GROUPS * k + g + 1)

    diff(0)
    for lv in range(HG_EXPS):
        queries_keys(lv)
        if lv + 1 < HG_EXPS:
            diff(lv + 1)
        if lv:
            take(lv - 1)
    take(HG_EXPS - 1)
    take(HG_EXPS)
    dve.wait_ge(c.s['hg_square'], 2 * (k + 1))
    dve.tensor_reduce(c.hss[:, :], h.sq.rearrange('p (m v) -> p m v', v=HD), AX, ALU.add).then_inc(c.s['hg_ss'], 1)
    for n in range(NT):
        dve.wait_ge(c.s['hg_silu'], 2 * k + n + 1)
        g = c.z[:, n, Z_BG:Z_BG + 384].rearrange('p (m v) -> p m v', v=HD)
        c.vstep(dve.tensor_tensor(g, g, c.onorm[:, k, :].unsqueeze(1).broadcast_to([P, B_HEADS, HD]), ALU.mult))
    dve.wait_ge(c.s['hg_rstd'], k + 1)
    o3 = h.o.rearrange('p (m v) -> p m v', v=HD)
    c.vstep(dve.tensor_tensor(o3, o3, c.hrstd[:, :].unsqueeze(2).broadcast_to([P, NT * B_HEADS, HD]), ALU.mult))
    for n in range(NT):
        dve.tensor_tensor(c.mix[:, n, 384:768], h.o[:, n * 384:n * 384 + 384], c.z[:, n, Z_BG:Z_BG + 384], ALU.mult)\
           .then_inc(c.s['mix_ready'], 1)


def hgrn_act(c, act, st):
    k = st['k']
    h = hg_buffers(c)

    def log_one_plus(buf, n_in, n_out):
        act.wait_ge(c.s['hg_gate'], n_in)
        signal(act, act.activation(buf, buf, ACT.Exp, scale=-1.0), c.s['hg_log_e'], c.n_log_e + 1)
        c.n_log_e += 1
        act.activation(buf, buf, ACT.Ln, bias=1.0).then_inc(c.s['hg_log'], 1)
    g0, l0 = (0, 0) if k == 0 else (2, 2)
    log_one_plus(h.D[0], g0 + 1, l0 + 1)
    if k:
        log_one_plus(c.lbe[:, :], g0 + 2, l0 + 2)
        act.wait_ge(c.s['hg_gate'], g0 + 3)
        for p in range(PAIRS):
            v = slice(p * S, p * S + S)
            ins = act.activation(h.k[:, v], h.k[:, v], ACT.Exp, bias=c.lbl[:, p:p + 1])
        ins.then_inc(c.s['hg_log'], 1)
        log_one_plus(h.D[1], g0 + 4, l0 + 4)
    else:
        act.wait_ge(c.s['hg_gate'], 2)
        act.activation(h.k, h.k, ACT.Exp).then_inc(c.s['hg_log'], 1)
    for lv in range(HG_EXPS):
        B = P if HG_LEVELS[lv] == 'cross' else HG_LEVELS[lv]
        act.wait_ge(c.s['hg_diff'], HG_EXPS * k + lv + 1)
        v = by_block(h.D[lv % 2], B)
        act.activation(v[:, :, 0:B], v[:, :, 0:B], ACT.Exp, scale=-1.0)
        act.activation(v[:, :, B:2 * B], v[:, :, B:2 * B], ACT.Exp).then_inc(c.s['hg_exp'], 1)
    for n in range(NT):
        act.wait_ge(c.s['hg_out'], 2 * k + n + 1)
        o = h.o[:, n * 384:n * 384 + 384]
        signal(act, act.activation(o, c.pb[n][:, 0:384], ACT.Copy), c.s['hg_o'], 2 * k + n + 1)
        act.activation(h.sq[:, n * 384:n * 384 + 384], o, ACT.Square).then_inc(c.s['hg_square'], 1)


def hgrn_pool(c, pool, st):
    pool.wait_ge(c.s['hg_ss'], st['k'] + 1)
    c.pstep(pool.tensor_scalar(c.hms[:, :], c.hss[:, :], 1.0 / HD, EPS, ALU.mult, ALU.add))
    pool.tensor_tensor(c.hrstd[:, :], c.hms[:, :], c.neghalf[:, 0:NT * B_HEADS], ALU.pow).then_inc(c.s['hg_rstd'], 1)


def hgrn_pe(c, pe, st):
    k = st['k']
    h = hg_buffers(c)
    for g, (lv, n) in enumerate(hg_groups()):
        if lv < HG_EXPS:
            pe.wait_ge(c.s['hg_QK'], HG_EXPS * k + lv + 1)
            keys = queries = h.QK[lv % 2]
        else:
            keys, queries = h.k, h.q
        if g >= 4:
            pe.wait_ge(c.s['hg_taken'], HG_GROUPS * k + g - 3)
        m = 0 if lv == 0 else n
        for par in range(2):
            half = slice(HD * par, HD * par + HD)
            for p in range(PAIRS):
                mm = pe.matmul(c.pb[2 * (g % 4) + par][:, p * P:p * P + P],
                               keys[half, p * S + m * P:p * S + m * P + P],
                               queries[half, p * S + n * P:p * S + n * P + P], start=True, stop=True)
        mm.then_inc(c.s['hg_pairs'], 1)
    pe.wait_ge(c.s['hg_taken'], HG_GROUPS * (k + 1))
    for n in range(NT):
        for hd in range(B_HEADS):
            i = 3 * (hd % 2) + hd // 2
            out = c.pb[n][:, hd * HD:hd * HD + HD]
            v = slice(Z_BI + hd * HD, Z_BI + hd * HD + HD)
            mm = pe.matmul(out, c.AT[:, n, i, :], c.z[:, n, v], start=True, stop=n == 0)
            if n:
                mm = pe.matmul(out, h.cross[:, i * P:i * P + P], c.z[:, 0, v], start=False, stop=True)
        mm.then_inc(c.s['hg_out'], 1)


def gmlp_act(c, act, st):
    k = st['k']
    for n in range(NT):
        uv = c.z[:, n, Z_UV:Z_UV + 512]
        act.activation(uv, uv, ACT.Gelu).then_inc(c.s['gm_gelu'], 1)
    for n in range(NT):
        act.wait_ge(c.s['gm_centred'], 2 * k + n + 1)
        act.activation(c.L[:, 0:256], c.z[:, n, Z_UV + 256:Z_UV + 512], ACT.Square,
                       accum_out=c.gss[:, n:n + 1]).then_inc(c.s['gm_ss'], 1)
        act.wait_ge(c.s['gm_ss'], 2 * k + n + 1)
    for n in range(NT):
        g = c.z[:, n, Z_BG:Z_BG + 384]
        act.activation(g, g, ACT.Silu).then_inc(c.s['hg_silu'], 1)


def gmlp_pool(c, pool, st):
    k = st['k']
    pool.wait_ge(c.s['gm_ss'], 2 * (k + 1))
    c.pstep(pool.tensor_scalar(c.gms[:, :], c.gss[:, :], 1.0 / 256, EPS, ALU.mult, ALU.add))
    pool.tensor_tensor(c.grstd[:, :], c.gms[:, :], c.neghalf[:, 0:NT], ALU.pow).then_inc(c.s['gm_rstd'], 1)


def gmlp_dve(c, dve, st):
    k = st['k']
    for sem, v in st['evacuated']:
        dve.wait_ge(c.s[sem], v)
    for n in range(NT):
        v = c.z[:, n, Z_UV + 256:Z_UV + 512]
        dve.wait_ge(c.s['gm_gelu'], 2 * k + n + 1)
        c.vstep(dve.tensor_reduce(c.gsum[:, n:n + 1], v, AX, ALU.add))
        c.vstep(dve.tensor_scalar(c.gsum[:, n:n + 1], c.gsum[:, n:n + 1], 1.0 / 256, None, ALU.mult))
        signal(dve, dve.tensor_scalar(v, v, c.gsum[:, n:n + 1], None, ALU.subtract), c.s['gm_centred'], 2 * k + n + 1)
    dve.wait_ge(c.s['gm_rstd'], k + 1)
    for n in range(NT):
        v = c.z[:, n, Z_UV + 256:Z_UV + 512]
        c.vstep(dve.scalar_tensor_tensor(v, v, c.grstd[:, n:n + 1], c.vng[:, k, :], ALU.mult, ALU.mult))
        dve.tensor_tensor(v, v, c.vnb[:, k, :], ALU.add).then_inc(c.s['gm_v'], 1)
    for n in range(NT):
        dve.wait_ge(c.s['gm_mixed'], 2 * k + n + 1)
        for g in range(4):
            bs = COL2['gmlp_b_s'] + 4 * k + g
            u = c.z[:, n, Z_UV + 64 * g:Z_UV + 64 * g + 64]
            ins = dve.scalar_tensor_tensor(c.mix[:, n, 768 + 64 * g:832 + 64 * g], c.pb[2 + n][:, 64 * g:64 * g + 64],
                                           c.col2[:, bs:bs + 1], u, ALU.add, ALU.mult)
        ins.then_inc(c.s['mix_ready'], 1)


def gmlp_pe(c, pe, st):
    k = st['k']
    for n in range(NT):
        pe.wait_ge(c.s['gm_v'], 2 * k + n + 1)
        for g in range(4):
            at = Z_UV + 256 + 64 * g
            mm = pe.matmul(c.pb[2 + n][:, 64 * g:64 * g + 64], c.wsT[:, 4 * k + g, :], c.z[:, n, at:at + 64],
                           start=True, stop=True)
        mm.then_inc(c.s['gm_mixed'], 1)


def turn_stage(core, k, chunks, ready):
    st = dict(kind='turn', k=k, ready=ready, banks=[chunks[i:i + 2] for i in range(0, len(chunks), 2)],
              a0=core.turn['a'], b0=core.turn['b'])
    nb = len(st['banks'])
    core.turn['a'] += (nb + 1) // 2
    core.turn['b'] += nb // 2
    return st


def turn_pe(c, pe, st):
    for sem, v in st['ready']:
        pe.wait_ge(c.s[sem], v)
    for b, chunks in enumerate(st['banks']):
        for i, ch in enumerate(chunks):
            for n in range(NT):
                mm = pe.transpose(c.pb[b][:, i * S + n * P:i * S + n * P + P], c.mix[:, n, ch * P:ch * P + P], c.ident[:, :])
        mm.then_inc(c.s['turned'], 1)


def turn_evacuate(c, eng, st, par):
    t0 = st['a0'] + st['b0']
    for b, chunks in enumerate(st['banks']):
        if b % 2 != par:
            continue
        m = len(chunks)
        eng.wait_ge(c.s['turned'], t0 + b + 1)
        src = c.pb[b][:, 0:m * S].rearrange('p (m t) -> p m t', t=S)
        dst = c.mixT[:, chunks[0]:chunks[0] + m, :]
        ins = eng.tensor_copy(dst, src) if par else eng.activation(dst, src, ACT.Copy)
        ins.then_inc(c.s['turn_' + 'ab'[par]], 1)


def turn_act(c, act, st):
    turn_evacuate(c, act, st, 0)


def turn_dve(c, dve, st):
    turn_evacuate(c, dve, st, 1)


def turned_events(st):
    nb = len(st['banks'])
    return [('turn_a', st['a0'] + (nb + 1) // 2), ('turn_b', st['b0'] + nb // 2)]


POOL_WINDOWS = (2, 4, 8, 16)


def even_dve(c, dve, st):
    for sem, v in st['evacuated']:
        dve.wait_ge(c.s[sem], v)
    flat = c.zT[:, :, :].rearrange('p m t -> p (m t)')
    gb, gc, xa = flat[:, 0:4 * S], flat[:, 4 * S:8 * S], flat[:, 8 * S:12 * S]
    c.vstep(dve.tensor_tensor(gc, gc, xa, ALU.mult))
    for m in range(4):
        u, y = c.zT[:, 4 + m, :], c.zT[:, 8 + m, :]
        w = [c.col1[:, COL1['ev_conv_w_2'] + 4 * j + m:COL1['ev_conv_w_2'] + 4 * j + m + 1] for j in range(3)]
        c.vstep(dve.tensor_scalar(y, u, w[2], None, ALU.mult))
        for lag in (1, 2):
            c.vstep(dve.scalar_tensor_tensor(y[:, lag:], u[:, 0:S - lag], w[2 - lag], y[:, lag:], ALU.mult, ALU.add))
    c.vstep(dve.tensor_tensor(c.mixT[:, 0:4, :].rearrange('p m t -> p (m t)'), gb, xa, ALU.mult))
    for g, w in enumerate(POOL_WINDOWS):
        x, cs, d = c.zT[:, 12 + g, :], c.work[:, 0:S], c.L[:, g * S:g * S + S]
        c.vstep(dve.tensor_tensor_scan(cs, c.ones[:, 0:S], x, 0.0, ALU.mult, ALU.add))
        c.vstep(dve.tensor_tensor(d[:, w:], cs[:, w:], cs[:, 0:S - w], ALU.subtract))
        c.vstep(dve.tensor_tensor(d[:, 0:w], cs[:, 0:w], c.inv1[:, 0:w], ALU.mult))
        c.vstep(dve.tensor_tensor(d[:, 0:w], d[:, 0:w], x[:, 0:w], ALU.subtract))
        dve.scalar_tensor_tensor(d[:, w:], d[:, w:], 1.0 / w, x[:, w:], ALU.mult, ALU.subtract)\
           .then_inc(c.s['ev_pooled'], 1)
    for g in range(4):
        dve.wait_ge(c.s['ev_product'], g // 2 + 1)
        sc = COL1['ev_pool_scale_2'] + g
        dve.tensor_scalar(c.mixT[:, 4 + g, :], c.pb[g // 2][:, (g % 2) * S:(g % 2) * S + S], c.col1[:, sc:sc + 1],
                          None, ALU.mult).then_inc(c.s['ev_mixT'], 1)


def even_pe(c, pe, st):
    for g in range(4):
        pe.wait_ge(c.s['ev_pooled'], g + 1)
        mm = pe.matmul(c.pb[g // 2][:, (g % 2) * S:(g % 2) * S + S], c.wpool[:, g, :], c.L[:, g * S:g * S + S],
                       start=True, stop=True)
        if g % 2:
            mm.then_inc(c.s['ev_product'], 1)


def xa_stage(core, ready):
    c = core
    a = dict(heads=XA_HEADS, scale=XA_D ** -0.5, banks=[[0, 1], [2, 3]], keys=lambda n: S,
             q=lambda i, n: c.zT[:, i, n * P:n * P + P], k=lambda i, n: c.zT[:, 8 + i, :], mask=None,
             pv=lambda n: [(c.pb[7][:, h * P:h * P + P],
                            [(c.z[:, ch, h * P:h * P + P], ch * XA_HEADS + h, 1) for ch in range(NT)])
                           for h in range(XA_HEADS)],
             out=lambda n: c.mixT[:, 0:4, n * P:n * P + P], ready=ready)
    return dict(kind='xa', att=attend_plan(core, a))


def xa_pe(c, pe, st):
    attend_pe(c, pe, st['att'])


def xa_act(c, act, st):
    attend_act(c, act, st['att'])


def xa_dve(c, dve, st):
    attend_dve(c, dve, st['att'])


OD_V, OD_O, OD_G, OD_CQ, OD_CKV, OD_KR, OD_Q = 0, 512, 1024, 1032, 1416, 1672, 1704
ML_TILES = ((0, 0), (0, 1), (1, 1))


ML_TENSOR = in_order(rows=1, scores=3, turned=1, num=2)
ML_VECTOR = in_order(gates=2, abs=1, scans=1, cols=1, exponent=3, sw=3, h=2, ms=1)
ML_SCALAR = in_order(log=2, weight=3, em=1, sigmoid=2, square=2)


def mlstm_dve(c, dve, st):
    for sem, v in st['evacuated']:
        dve.wait_ge(c.s[sem], v)
    H = ML_HEADS
    for n in range(NT):
        g = c.z[:, n, OD_G:OD_G + 8]
        dve.tensor_tensor(g, g, c.gbias[:, :], ALU.add).then_inc(c.s['ml_vector'], 1)
    dve.wait_ge(c.s['ml_tensor'], ML_TENSOR['rows'] + 1)
    r = c.grows
    c.vstep(dve.tensor_copy(r[:, 0:2, :], c.pb[0][0:H, 0:512].rearrange('p (a t) -> p a t', a=2)))
    magnitude(dve, r[:, 2, :], r[:, 1, :]).then_inc(c.s['ml_vector'], 1)
    dve.wait_ge(c.s['ml_scalar'], ML_SCALAR['log'] + 2)
    c.vstep(dve.scalar_tensor_tensor(r[:, 1, :], r[:, 1, :], 0.0, r[:, 2, :], ALU.min, ALU.subtract))
    c.vstep(dve.tensor_tensor_scan(r[:, 3, :], c.ones[0:H, 0:S], r[:, 1, :], 0.0, ALU.mult, ALU.add))
    c.vstep(dve.tensor_tensor(r[:, 4, :], r[:, 0, :], r[:, 3, :], ALU.subtract))
    c.vstep(dve.tensor_tensor_scan(r[:, 5, :], r[:, 4, :], r[:, 4, :], 0.0, ALU.max, ALU.max))
    c.vstep(dve.tensor_tensor(r[:, 6, :], r[:, 3, :], r[:, 5, :], ALU.add))
    dve.tensor_scalar(r[:, 5, :], r[:, 5, :], -1.0, None, ALU.mult).then_inc(c.s['ml_vector'], 1)
    dve.wait_ge(c.s['ml_tensor'], ML_TENSOR['turned'] + 1)
    signal(dve, dve.tensor_copy(c.gcols[:, :], c.pb[1][:, 0:4 * H]), c.s['ml_vector'], ML_VECTOR['cols'] + 1)
    w = c.PT[:, 0:3 * H * P].rearrange('p (x h t) -> p x h t', x=3, h=H)
    for x, (m, n) in enumerate(ML_TILES):
        for h in range(H):
            row = c.pb[2 + h // 2][:, (h % 2) * S + n * P:(h % 2) * S + n * P + P]
            a = c.gcols[:, m * H + h:m * H + h + 1]
            if m == n:
                ins = dve.scalar_tensor_tensor(w[:, x, h, :], row, a, c.maskK[:, :], ALU.add, ALU.min)
            else:
                ins = dve.tensor_scalar(w[:, x, h, :], row, a, 0.0, ALU.add, ALU.min)
        ins.then_inc(c.s['ml_vector'], 1)
    for x in range(3):
        dve.wait_ge(c.s['ml_scalar'], ML_SCALAR['weight'] + x + 1)
        dve.wait_ge(c.s['ml_tensor'], ML_TENSOR['scores'] + x + 1)
        dve.scalar_tensor_tensor(w[:, x, :, :], c.pb[4 + x][:, :].rearrange('p (h t) -> p h t', h=H),
                                 XA_D ** -0.5, w[:, x, :, :], ALU.mult, ALU.mult).then_inc(c.s['ml_vector'], 1)
    dve.wait_ge(c.s['ml_scalar'], ML_SCALAR['em'] + 1)
    dve.wait_ge(c.s['ml_tensor'], ML_TENSOR['num'] + 2)
    sums = c.pb[1][:, 0:NT * H]
    c.vstep(dve.tensor_tensor(c.mden[:, :], sums, c.gcols[:, NT * H:2 * NT * H], ALU.max))
    c.vstep(dve.scalar_tensor_tensor(c.mden[:, :], sums, -1.0, c.mden[:, :], ALU.mult, ALU.max))
    c.vstep(dve.reciprocal(c.mden[:, :], c.mden[:, :]))
    for n in range(NT):
        bank = c.pb[0 if n == 0 else 7]
        out = c.mix[:, n, 0:512].rearrange('p (h v) -> p h v', h=H)
        c.vstep(dve.tensor_tensor(out, bank[:, :].rearrange('p (h v) -> p h v', h=H),
                                  c.mden[:, n * H:n * H + H].unsqueeze(2).broadcast_to([P, H, P]), ALU.mult))
        dve.wait_ge(c.s['ml_scalar'], ML_SCALAR['sigmoid'] + n + 1)
        dve.tensor_tensor(c.mix[:, n, 0:512], c.mix[:, n, 0:512], c.z[:, n, OD_O:OD_O + 512], ALU.mult)\
           .then_inc(c.s['ml_vector'], 1)
    for n in range(NT):
        dve.wait_ge(c.s['ml_scalar'], ML_SCALAR['square'] + n + 1)
        c.vstep(dve.tensor_reduce(c.mss[:, n * H:n * H + H], c.z[:, n, OD_O:OD_O + 512]
                                  .rearrange('p (h v) -> p h v', h=H), AX, ALU.add))
    dve.tensor_scalar(c.mss[:, :], c.mss[:, :], 1.0 / P, EPS, ALU.mult, ALU.add).then_inc(c.s['ml_vector'], 1)
    dve.wait_ge(c.s['ml_rstd'], 1)
    for n in range(NT):
        out = c.mix[:, n, 0:512].rearrange('p (h v) -> p h v', h=H)
        c.vstep(dve.tensor_tensor(out, out, c.mrstd[:, n * H:n * H + H].unsqueeze(2).broadcast_to([P, H, P]), ALU.mult))
        dve.tensor_tensor(c.mix[:, n, 0:512], c.mix[:, n, 0:512], c.mlg[:, :], ALU.mult).then_inc(c.s['mix_ready'], 1)


def mlstm_pool(c, pool, st):
    pool.wait_ge(c.s['ml_vector'], ML_VECTOR['ms'] + 1)
    pool.tensor_tensor(c.mrstd[:, :], c.mss[:, :], c.neghalf[:, 0:NT * ML_HEADS], ALU.pow).then_inc(c.s['ml_rstd'], 1)


def mlstm_act(c, act, st):
    r = c.grows
    act.wait_ge(c.s['ml_vector'], ML_VECTOR['abs'] + 1)
    signal(act, act.activation(r[:, 2, :], r[:, 2, :], ACT.Exp, scale=-1.0), c.s['ml_scalar'], ML_SCALAR['log'] + 1)
    act.activation(r[:, 2, :], r[:, 2, :], ACT.Ln, bias=1.0).then_inc(c.s['ml_scalar'], 1)
    w = c.PT[:, 0:3 * ML_HEADS * P].rearrange('p (x f) -> p x f', x=3)
    for x in range(3):
        act.wait_ge(c.s['ml_vector'], ML_VECTOR['exponent'] + x + 1)
        act.activation(w[:, x, :], w[:, x, :], ACT.Exp).then_inc(c.s['ml_scalar'], 1)
    act.wait_ge(c.s['ml_vector'], ML_VECTOR['cols'] + 1)
    em = c.gcols[:, NT * ML_HEADS:2 * NT * ML_HEADS]
    act.activation(em, em, ACT.Exp, scale=-1.0).then_inc(c.s['ml_scalar'], 1)
    for n in range(NT):
        o = c.z[:, n, OD_O:OD_O + 512]
        act.activation(o, o, ACT.Sigmoid).then_inc(c.s['ml_scalar'], 1)
    for n in range(NT):
        act.wait_ge(c.s['ml_vector'], ML_VECTOR['h'] + n + 1)
        act.activation(c.z[:, n, OD_O:OD_O + 512], c.mix[:, n, 0:512], ACT.Square).then_inc(c.s['ml_scalar'], 1)


def mlstm_pe(c, pe, st):
    H = ML_HEADS
    pe.wait_ge(c.s['ml_vector'], ML_VECTOR['gates'] + 2)
    for a in range(2):
        for n in range(NT):
            mm = pe.transpose(c.pb[0][0:H, a * S + n * P:a * S + n * P + P],
                              c.z[:, n, OD_G + a * H:OD_G + a * H + H], c.ident[:, :])
    mm.then_inc(c.s['ml_tensor'], 1)
    for x, (m, n) in enumerate(ML_TILES):
        for h in range(H):
            mm = pe.matmul(c.pb[4 + x][:, h * P:h * P + P], c.zT[:, 4 + h, m * P:m * P + P],
                           c.zT[:, h, n * P:n * P + P], start=True, stop=True)
        mm.then_inc(c.s['ml_tensor'], 1)
    pe.wait_ge(c.s['ml_vector'], ML_VECTOR['scans'] + 1)
    for i, row in enumerate((4, 6)):
        for n in range(NT):
            at = (i * NT + n) * H
            mm = pe.transpose(c.pb[1][:, at:at + H], c.grows[:, row, n * P:n * P + P], c.ident[0:H, 0:H])
    for h in range(H):
        mm = pe.matmul(c.pb[2 + h // 2][:, (h % 2) * S:(h % 2) * S + S], c.selT[0:H, h, :], c.grows[:, 5, :],
                       start=True, stop=True)
    mm.then_inc(c.s['ml_tensor'], 1)
    pe.wait_ge(c.s['ml_vector'], ML_VECTOR['cols'] + 1)
    for n in range(NT):
        pe.wait_ge(c.s['ml_vector'], ML_VECTOR['sw'] + (1 if n == 0 else 3))
        bank = c.pb[0 if n == 0 else 7]
        for h in range(H):
            xs = [x for x, (_, nn) in enumerate(ML_TILES) if nn == n]
            for i, x in enumerate(xs):
                lhs = c.PT[:, (x * H + h) * P:(x * H + h) * P + P]
                m = ML_TILES[x][0]
                pe.matmul(bank[:, h * P:h * P + P], lhs, c.z[:, m, OD_V + h * P:OD_V + h * P + P],
                          start=i == 0, stop=i == len(xs) - 1)
            for i, x in enumerate(xs):
                lhs = c.PT[:, (x * H + h) * P:(x * H + h) * P + P]
                mm = pe.matmul(c.pb[1][:, n * H + h:n * H + h + 1], lhs, c.ones[:, 0:1],
                               start=i == 0, stop=i == len(xs) - 1)
        mm.then_inc(c.s['ml_tensor'], 1)


LATENTS = ((OD_CQ, 3), (OD_CKV, 2))


def mla_in_act(c, act, st):
    for i, (at, m) in enumerate(LATENTS):
        for n in range(NT):
            act.activation(c.L[:, 0:m * P], c.z[:, n, at:at + m * P], ACT.Square,
                           accum_out=c.lss[:, 2 * i + n:2 * i + n + 1]).then_inc(c.s['la_ss'], 1)
            act.wait_ge(c.s['la_ss'], 2 * i + n + 1)


def mla_in_pool(c, pool, st):
    pool.wait_ge(c.s['la_ss'], 4)
    for i, (_, m) in enumerate(LATENTS):
        c.pstep(pool.tensor_scalar(c.lms[:, 2 * i:2 * i + 2], c.lss[:, 2 * i:2 * i + 2], 1.0 / (m * P), EPS,
                                   ALU.mult, ALU.add))
    pool.tensor_tensor(c.lrstd[:, :], c.lms[:, :], c.neghalf[:, 0:4], ALU.pow).then_inc(c.s['la_rstd'], 1)


def mla_in_dve(c, dve, st):
    dve.wait_ge(c.s['la_rstd'], 1)
    for i, (at, m) in enumerate(LATENTS):
        for n in range(NT):
            v = c.z[:, n, at:at + m * P]
            dve.tensor_scalar(v, v, c.lrstd[:, 2 * i + n:2 * i + n + 1], None, ALU.mult).then_inc(c.s['la_normed'], 1)
    dve.wait_ge(c.s['la_turned'], 1)
    for ch in range(5):
        col = COL1['od_q_norm_g_2'] + ch
        dve.tensor_scalar(c.rT[:, ch, :], c.pb[ch // 2][:, (ch % 2) * S:(ch % 2) * S + S], c.col1[:, col:col + 1],
                          None, ALU.mult).then_inc(c.s['la_ready'], 1)


def mla_in_pe(c, pe, st):
    pe.wait_ge(c.s['la_normed'], 4)
    ch = 0
    for at, m in LATENTS:
        for u in range(m):
            for n in range(NT):
                mm = pe.transpose(c.pb[ch // 2][:, (ch % 2) * S + n * P:(ch % 2) * S + n * P + P],
                                  c.z[:, n, at + u * P:at + u * P + P], c.ident[:, :])
            ch += 1
    mm.then_inc(c.s['la_turned'], 1)


def mla_stage(core, ready):
    c = core
    a = dict(heads=MLA_HEADS, scale=QKW ** -0.5, banks=[[0, 1], [2, 3], [4, 5], [6, 7]],
             keys=lambda n: P * (n + 1),
             q=lambda i, n: c.zT[0:QKW, i, n * P:n * P + P], k=lambda i, n: c.zT[0:QKW, 8 + i, 0:P * (n + 1)],
             mask=lambda n: c.maskQ2[:, P - n * P:2 * P], mask_ready=lambda n: [],
             pv=lambda n: [(c.pb[7][HD * (h % 2):HD * (h % 2) + HD, (h // 2) * P:(h // 2) * P + P],
                            [(c.xn[:, ch, h * P + NOPE:h * P + P], ch * MLA_HEADS + h, 1) for ch in range(n + 1)])
                           for h in range(MLA_HEADS)],
             out=lambda n: c.mixT[:, 4:8, n * P:n * P + P], ready=[('la_T_a', 4), ('la_T_b', 4)])
    return dict(kind='mla', evacuated=ready, att=attend_plan(core, a))


def mla_dve(c, dve, st):
    for sem, v in st['evacuated']:
        dve.wait_ge(c.s[sem], v)
    kcat = c.L[:, 0:NT * MLA_HEADS * QKW].rearrange('p (n h d) -> p n h d', n=NT, h=MLA_HEADS)
    for n in range(NT):
        cos, sin = c.cos[:, 64 + 16 * n:80 + 16 * n], c.sin[:, 64 + 16 * n:80 + 16 * n]
        q = c.z[:, n, OD_Q:OD_Q + MLA_HEADS * QKW].rearrange('p (h d) -> p h d', h=MLA_HEADS)[:, :, NOPE:QKW]
        rotate(c, dve, q, q, MLA_HEADS, ROPE_W // 2, cos, sin, c.PT[:, 0:256], c.PT[:, 256:512])
        kr = c.z[:, n, OD_KR:OD_KR + ROPE_W].unsqueeze(1)
        rotate(c, dve, kr, kr, 1, ROPE_W // 2, cos, sin, c.PT[:, 0:32], c.PT[:, 256:288])
        c.vstep(dve.tensor_copy(kcat[:, n, :, NOPE:QKW], kr.broadcast_to([P, MLA_HEADS, ROPE_W])))
        dve.tensor_copy(kcat[:, n, :, 0:NOPE], c.xn[:, n, :].rearrange('p (h d) -> p h d', h=MLA_HEADS)[:, :, 0:NOPE])\
           .then_inc(c.s['la_rot'], 1)
    mla_evacuate(c, dve, 1)
    attend_dve(c, dve, st['att'])


def mla_evacuate(c, eng, par):
    for b in range(par, 8, 2):
        n, what, h0 = b // 4, (b // 2) % 2, 4 * (b % 2)
        eng.wait_ge(c.s['la_T'], b + 1)
        src = c.pb[b][0:QKW, :].rearrange('p (h t) -> p h t', h=4)
        dst = c.zT[0:QKW, 8 * what + h0:8 * what + h0 + 4, n * P:n * P + P]
        ins = eng.tensor_copy(dst, src) if par else eng.activation(dst, src, ACT.Copy)
        ins.then_inc(c.s['la_T_' + 'ab'[par]], 1)


def mla_pe(c, pe, st):
    for b in range(8):
        n, what, h0 = b // 4, (b // 2) % 2, 4 * (b % 2)
        pe.wait_ge(c.s['la_rot'], n + 1)
        for h in range(h0, h0 + 4):
            if what:
                src = c.L[:, (n * MLA_HEADS + h) * QKW:(n * MLA_HEADS + h + 1) * QKW]
            else:
                src = c.z[:, n, OD_Q + h * QKW:OD_Q + (h + 1) * QKW]
            mm = pe.transpose(c.pb[b][0:QKW, (h - h0) * P:(h - h0) * P + P], src, c.ident[:, :])
        mm.then_inc(c.s['la_T'], 1)
    attend_pe(c, pe, st['att'])


def mla_act(c, act, st):
    mla_evacuate(c, act, 0)
    attend_act(c, act, st['att'])


MOE_STEPS = F_EXPERT // FT


MO_TENSOR = in_order(logits=1, counts=1, rows=1, spread=8, summed=1)
MO_VECTOR = in_order(logit_less=1, chosen=1, slots=1, rows_in=1, spread_in=8)


def moe_stage(core):
    st = dict(kind='moe', j0=len(core.jobs))
    assert MOE_STEPS % 2 == 0
    for e in range(N_EXP):
        for i in range(MOE_STEPS):
            m = e * MOE_STEPS + i + 1
            for q in range(3):
                job(core, None, ('me_gu0' if q < 2 else 'me_down0', m))
    return st


def moe_sems(c, p):
    return {name: c.s[f'me_{name}{p}'] for name in
            ('gu', 'down', 'silu', 'act', 'turned', 'actT', 'onehot', 'gathered', 'hTa', 'hTb', 'sums', 'ye', 'scat')}


def moe_load(c, sp, q, e, i, slot, sem):
    w = c.ring[:, slot, :]
    if q < 2:
        w = w.rearrange('p (k s n) -> p k s n', k=4, s=2)
        for s, view in enumerate((c.moe_gate, c.moe_up)):
            sp.dma_start(w[:, :, s, :], view[:, bass.ds(e * KD + 4 * q, 4), bass.ds(i * FT, FT)]).then_inc(sem, 16)
    else:
        w = w.rearrange('p (k n) -> p k n', k=2)
        for a in range(2):
            sp.dma_start(w[:, a:a + 1, :], c.moe_down[:, bass.ds(e * (F_EXPERT // P) + i * 2 + a, 1), :])\
              .then_inc(sem, 16)


def moe_pass_sp(c, sp, st, p):
    j0 = st['j0']
    E = moe_sems(c, p)

    def landed(q, r):
        return c.again[r] if p else c.landed[(j0 + 3 * r + q) % RING]

    def fill(e, i, r, m):
        for q in range(3):
            if m is not None:
                sp.wait_ge(E['gu'] if q < 2 else E['down'], m - 1)
            moe_load(c, sp, q, e, i, (j0 + 3 * r + q) % RING, landed(q, r))
    for r in range(2):
        for q in range(3):
            if p == 0:
                sem, v = c.jobs[j0 + 3 * r + q - RING][1]
                sp.wait_ge(c.s[sem], v)
            moe_load(c, sp, q, 0, r, (j0 + 3 * r + q) % RING, landed(q, r))
    with sp.Fori(1, MOE_STEPS // 2) as it:
        for r in range(2):
            fill(0, it * 2 + r, r, it * 2 + r)
    with sp.Fori(1, N_EXP) as e:
        with sp.Fori(0, MOE_STEPS // 2) as it:
            for r in range(2):
                fill(e, it * 2 + r, r, e * MOE_STEPS + it * 2 + r)


def overflow(c, eng, run):
    eng.wait_ge(c.s['me_count'], 1)
    most = eng.value_load(c.count[0:1, 0:1], min_val=0, max_val=S)
    with eng.If(most > P):
        run()


def moe_sp(c, sp, st):
    moe_pass_sp(c, sp, st, 0)

    def again():
        for q in (0, 2):
            sp.wait_ge(c.s['me_gu0' if q == 0 else 'me_down0'], N_EXP * MOE_STEPS)
        moe_pass_sp(c, sp, st, 1)
        sp.wait_ge(c.s['me_gu1'], N_EXP * MOE_STEPS)
        sp.wait_ge(c.s['me_down1'], N_EXP * MOE_STEPS)
    overflow(c, sp, again)


def moe_pass_pe(c, pe, st, p):
    j0 = st['j0']
    E = moe_sems(c, p)
    G, T = c.pb[6], c.pb[7]

    def gather(e1, half):
        pe.wait_ge(E['onehot'], e1)
        bank = (G, T)[half]
        for kc in range(4):
            for n in range(NT):
                mm = pe.matmul(bank[:, kc * P:kc * P + P], c.xn[:, n, (4 * half + kc) * P:(4 * half + kc) * P + P],
                               c.onehot[:, n, :], start=n == 0, stop=n == NT - 1)
        mm.then_inc(E['gathered'], 1)

    def gate_up(r, m):
        for q in range(2):
            j = j0 + 3 * r + q
            wait_fill(j, r, m)
            w = c.ring[:, j % RING, :].rearrange('p (k w) -> p k w', k=4)
            for i in range(4):
                mm = pe.matmul(G[:, :], c.hTe[:, 4 * q + i, :], w[:, i, :], start=q + i == 0, stop=q + i == 4)
        mm.then_inc(E['gu'], 1)

    def wait_fill(j, r, m):
        if p == 0:
            pe.wait_ge(c.landed[j % RING], (m - r) * (LOAD // 2) + LOAD * (j // RING + 1))
        else:
            pe.wait_ge(c.again[r], (m - r) * (3 * LOAD // 2) + 3 * LOAD)

    def turn(m):
        pe.wait_ge(E['act'], m + 1)
        for a in range(2):
            mm = pe.transpose(T[:, a * P:a * P + P], c.fa[:, 0, a * P:a * P + P], c.ident[:, :])
        mm.then_inc(E['turned'], 1)

    def down(r, m, first, last):
        j = j0 + 3 * r + 2
        wait_fill(j, r, m)
        pe.wait_ge(E['actT'], m + 1)
        w = c.ring[:, j % RING, :].rearrange('p (k n) -> p k n', k=2)
        for h in range(2):
            for a in range(2):
                mm = pe.matmul(c.pb[4 + h][:, :], c.faT[:, 0, a, :], w[:, a, h * 512:h * 512 + 512],
                               start=first and a == 0, stop=last and a == 1, skip_group_check=True)
        mm.then_inc(E['down'], 1)

    gather(1, 0)
    gather(1, 1)
    with pe.Fori(0, N_EXP) as e:
        m0 = e * MOE_STEPS
        pe.wait_ge(E['hTa'], e + 1)
        pe.wait_ge(E['hTb'], e + 1)
        gate_up(0, m0)
        turn(m0)
        gate_up(1, m0 + 1)
        down(0, m0, True, False)
        turn(m0 + 1)
        with pe.Fori(1, MOE_STEPS // 2) as it:
            for r in range(2):
                m = m0 + it * 2 + r
                gate_up(r, m)
                down(1 - r, m - 1, False, False)
                turn(m)
        last = m0 + (MOE_STEPS - 1)
        gather(e + 2, 0)
        down(1, last, False, True)
        gather(e + 2, 1)
        pe.wait_ge(E['ye'], e + 1)
        pe.wait_ge(E['sums'], e + 1)
        for n in range(NT):
            for h in range(2):
                mm = pe.matmul(c.pb[2 * n + h][:, :], c.combine[:, n * P:n * P + P], c.ye[:, h * 512:h * 512 + 512],
                               start=False, stop=False, skip_group_check=True)
        mm.then_inc(E['scat'], 1)


def moe_pe(c, pe, st):
    for sem, v in st['hT']:
        pe.wait_ge(c.s[sem], v)
    for n in range(NT):
        for kc in range(KD):
            mm = pe.matmul(c.pb[0][:, n * N_EXP:n * N_EXP + N_EXP], c.hT[:, kc, n * P:n * P + P],
                           c.wrouter[:, kc, :], start=kc == 0, stop=kc == KD - 1)
    mm.then_inc(c.s['mo_tensor'], 1)
    pe.wait_ge(c.s['mo_vector'], MO_VECTOR['chosen'] + 1)
    for n in range(NT):
        out = c.pb[1][:, n * N_EXP:n * N_EXP + N_EXP]
        pe.matmul(out, c.triT[:, :], c.chosen[:, n, :], start=True, stop=n == 0)
        if n:
            pe.matmul(out, c.ones[:, 0:P], c.chosen[:, 0, :], start=False, stop=True)
    for n in range(NT):
        mm = pe.matmul(c.pb[1][:, 16:16 + N_EXP], c.ones[:, 0:P], c.chosen[:, n, :], start=n == 0, stop=n == NT - 1)
    mm.then_inc(c.s['mo_tensor'], 1)
    pe.wait_ge(c.s['mo_vector'], MO_VECTOR['slots'] + 1)
    for i, buf in enumerate((c.slots, c.gates)):
        for n in range(NT):
            mm = pe.transpose(c.pb[2][0:N_EXP, i * S + n * P:i * S + n * P + P], buf[:, n, 0:N_EXP], c.ident[:, :])
    mm.then_inc(c.s['mo_tensor'], 1)
    pe.wait_ge(c.s['mo_vector'], MO_VECTOR['rows_in'] + 1)
    for i in range(2):
        for e in range(N_EXP):
            b = i * (N_EXP // 2) + e // 2
            if b >= 4 and e % 2 == 0:
                pe.wait_ge(c.s['mo_vector'], MO_VECTOR['spread_in'] + b - 3)
            mm = pe.matmul(c.pb[4 + b % 4][:, (e % 2) * S:(e % 2) * S + S], c.selT[0:N_EXP, e, :], c.mrows[:, i, :],
                           start=True, stop=True)
            if e % 2:
                mm.then_inc(c.s['mo_tensor'], 1)
    pe.wait_ge(c.s['mo_vector'], MO_VECTOR['spread_in'] + 8)
    for b in range(4):
        for h in range(2):
            pe.matmul(c.pb[b][:, h * S:h * S + S], c.zero[:, 0:P], c.zero[:, :], start=h == 0, stop=False,
                      skip_group_check=True)
    moe_pass_pe(c, pe, st, 0)
    overflow(c, pe, lambda: moe_pass_pe(c, pe, st, 1))
    pe.matmul(c.pb[0][:, 0:S], c.zero[:, 0:P], c.zero[:, :], start=False, stop=True, skip_group_check=True)\
      .then_inc(c.s['mo_tensor'], 1)


def moe_pass_act(c, act, st, p):
    E = moe_sems(c, p)

    def take_gather(e1):
        act.wait_ge(E['gathered'], e1 * 2 - 1)
        for kc in range(4):
            ins = act.activation(c.hTe[:, kc, :], c.pb[6][:, kc * P:kc * P + P], ACT.Identity,
                                 bias=c.modC[:, 16 + kc:17 + kc], scale=c.modA[:, 8 + kc:9 + kc])
        ins.then_inc(E['hTa'], 1)

    def step(m):
        act.wait_ge(E['gu'], m + 1)
        act.activation(c.fs[:, 0, :], c.pb[6][:, 0:FT], ACT.Silu).then_inc(E['silu'], 1)
        act.wait_ge(E['turned'], m + 1)
        act.activation(c.faT[:, 0, :, :], c.pb[7][:, 0:2 * P].rearrange('p (a t) -> p a t', a=2), ACT.Copy)\
           .then_inc(E['actT'], 1)
    take_gather(1)
    with act.Fori(0, N_EXP) as e:
        with act.Fori(0, MOE_STEPS) as it:
            step(e * MOE_STEPS + it)
        take_gather(e + 2)
        act.wait_ge(E['down'], (e + 1) * MOE_STEPS)
        for h in range(2):
            ins = act.activation(c.ye[:, h * 512:h * 512 + 512], c.pb[4 + h][:, :], ACT.Copy)
        ins.then_inc(E['ye'], 1)


def moe_act(c, act, st):
    act.wait_ge(c.s['mo_vector'], MO_VECTOR['logit_less'] + 1)
    act.activation(c.mexp[:, :], c.mexp[:, :], ACT.Exp).then_inc(c.s['mo_exp'], 1)
    moe_pass_act(c, act, st, 0)
    overflow(c, act, lambda: moe_pass_act(c, act, st, 1))


def moe_pass_dve(c, dve, st, p):
    E = moe_sems(c, p)

    def one_hot(e1):
        for n in range(NT):
            ins = dve.tensor_tensor(c.onehot[:, n, :], c.slotF2[:, p * P:p * P + P],
                                    c.slots[:, n, bass.ds(e1 - 1, 1)].broadcast_to([P, P]), ALU.is_equal)
        ins.then_inc(E['onehot'], 1)

    def take_gather(e1):
        dve.wait_ge(E['gathered'], e1 * 2)
        for kc in range(4, 8):
            ins = dve.tensor_scalar(c.hTe[:, kc, :], c.pb[7][:, (kc - 4) * P:(kc - 4) * P + P],
                                    c.modA[:, 8 + kc:9 + kc], c.modC[:, 16 + kc:17 + kc], ALU.mult, ALU.add)
        ins.then_inc(E['hTb'], 1)
    one_hot(1)
    take_gather(1)
    with dve.Fori(0, N_EXP) as e:
        one_hot(e + 2)
        with dve.Fori(0, MOE_STEPS) as it:
            m = e * MOE_STEPS + it
            dve.wait_ge(E['silu'], m + 1)
            dve.tensor_tensor(c.fa[:, 0, :], c.fs[:, 0, :], c.pb[6][:, FT:2 * FT], ALU.mult).then_inc(E['act'], 1)
        dve.scalar_tensor_tensor(c.combine[:, :], c.slotsB[:, bass.ds(e, 1), :].rearrange('p a t -> p (a t)'),
                                 c.slotP[:, p:p + 1], c.gatesB[:, bass.ds(e, 1), :].rearrange('p a t -> p (a t)'),
                                 ALU.is_equal, ALU.mult).then_inc(E['sums'], 1)
        take_gather(e + 2)


def moe_dve(c, dve, st):
    dve.wait_ge(c.s['mo_tensor'], MO_TENSOR['logits'] + 1)
    for n in range(NT):
        lg = c.logits[:, n, :]
        c.vstep(dve.tensor_copy(lg, c.pb[0][:, n * N_EXP:n * N_EXP + N_EXP]))
        c.vstep(dve.max(c.top8[:, :], lg))
        sel, eq, pre = c.chosen[:, n, :], c.meq[:, 0:8], c.meq[:, 8:16]
        c.vstep(dve.tensor_scalar(sel, lg, c.top8[:, 1:2], None, ALU.is_gt, ALU.add, accum_out=c.cnt[:, 0:1]))
        c.vstep(dve.tensor_scalar(c.cnt[:, 1:2], c.cnt[:, 0:1], -1.0, 2.0, ALU.mult, ALU.add))
        c.vstep(dve.tensor_scalar(eq, lg, c.top8[:, 1:2], None, ALU.is_equal))
        c.vstep(dve.tensor_tensor_scan(pre, c.ones[:, 0:8], eq, 0.0, ALU.mult, ALU.add))
        c.vstep(dve.scalar_tensor_tensor(eq, pre, c.cnt[:, 1:2], eq, ALU.is_le, ALU.mult))
        c.vstep(dve.tensor_tensor(sel, sel, eq, ALU.add))
        c.vstep(dve.tensor_scalar(c.mexp[:, 9 * n:9 * n + 8], lg, c.top8[:, 0:1], None, ALU.subtract))
        c.vstep(dve.tensor_tensor(c.mexp[:, 9 * n + 8:9 * n + 9], c.top8[:, 1:2], c.top8[:, 0:1], ALU.subtract))
    signal(dve, dve.tensor_scalar(c.mexp[:, :], c.mexp[:, :], 0.0, None, ALU.min), c.s['mo_vector'], MO_VECTOR['logit_less'] + 1)
    dve.tensor_scalar(c.slotP[:, 1:2], c.slotP[:, 0:1], float(P), None, ALU.add).then_inc(c.s['mo_vector'], 1)
    dve.wait_ge(c.s['mo_exp'], 1)
    for n in range(NT):
        c.vstep(dve.tensor_scalar(c.cnt[:, 0:1], c.mexp[:, 9 * n + 8:9 * n + 9], 1.0, None, ALU.add))
        c.vstep(dve.reciprocal(c.cnt[:, 1:2], c.cnt[:, 0:1]))
        c.vstep(dve.scalar_tensor_tensor(c.gates[:, n, 0:8], c.mexp[:, 9 * n:9 * n + 8], c.cnt[:, 1:2],
                                         c.chosen[:, n, :], ALU.mult, ALU.mult))
    dve.wait_ge(c.s['mo_tensor'], MO_TENSOR['counts'] + 1)
    for n in range(NT):
        c.vstep(dve.tensor_tensor(c.slots[:, n, 0:8], c.pb[1][:, n * 8:n * 8 + 8], c.chosen[:, n, :], ALU.mult))
    c.vstep(dve.tensor_reduce(c.cnt[:, 0:1], c.pb[1][:, 16:24], AX, ALU.max))
    dve.tensor_copy(c.count[:, 0:1], c.cnt[:, 0:1]).then_inc(c.s['me_count'], 1)
    c.vstep(dve.memset(c.slots[:, :, 8:9], 0.0))
    signal(dve, dve.tensor_scalar(c.slots[:, :, :], c.slots[:, :, :], 1.0, None, ALU.subtract), c.s['mo_vector'], MO_VECTOR['slots'] + 1)
    dve.wait_ge(c.s['mo_tensor'], MO_TENSOR['rows'] + 1)
    dve.tensor_copy(c.mrows[:, :, :], c.pb[2][0:N_EXP, :].rearrange('p (a t) -> p a t', a=2)).then_inc(c.s['mo_vector'], 1)
    for b in range(8):
        dve.wait_ge(c.s['mo_tensor'], MO_TENSOR['spread'] + b + 1)
        dst = (c.slotsB, c.gatesB)[b // 4][:, 2 * (b % 4):2 * (b % 4) + 2, :]
        signal(dve, dve.tensor_copy(dst, c.pb[4 + b % 4][:, :].rearrange('p (e t) -> p e t', e=2)),
               c.s['mo_vector'], MO_VECTOR['spread_in'] + b + 1)
    moe_pass_dve(c, dve, st, 0)
    overflow(c, dve, lambda: moe_pass_dve(c, dve, st, 1))
    dve.wait_ge(c.s['mo_tensor'], MO_TENSOR['summed'] + 1)
    for n in range(NT):
        for h in range(2):
            out = c.x[:, n, h * 512:h * 512 + 512]
            c.vstep(dve.tensor_tensor(c.tmp[:, :], c.pb[2 * n + h][:, :], c.grow[:, 1, h * 512:h * 512 + 512], ALU.mult))
            c.vstep(dve.tensor_tensor(out, out, c.tmp[:, :], ALU.add))
    c.x_written(dve)


def mem_act(c, act, st):
    act.wait_ge(c.s['x_ready'], st['x_before'])
    for n in range(NT):
        act.dma_start(c.grow[:, n, :], c.t['mem_2'][0, n * P:n * P + P, :]).then_inc(c.s['mem_loaded'], 16)


def make_plan(c):
    t = c.t
    stages = []
    updates = [0]
    count = {}

    def add(st):
        st['x_before'] = updates[0]
        stages.append(st)
        return st

    def number(kind):
        count[kind] = count.get(kind, -1) + 1
        return count[kind]

    def x_waits():
        return [('x_ready', updates[0])] if updates[0] else [('x_loaded', 32)]

    def norm(src, scale, shift=None, waits=None):
        k = number('norm')
        add(dict(kind='norm', k=k, src=src, scale=scale, shift=shift, waits=waits or x_waits()))
        return hT_ready(k)

    def columns(name, layer):
        at = COL1[name] + KD * layer
        return lambda kc: c.col1[:, at + kc:at + kc + 1]

    def tok(view, lo, hi, dst, k=KD, ksrc=0, evac='copy'):
        return [(view, a, min(512, hi - a), k, ksrc, 'tok', evac,
                 (lambda n, a=a: dst(n, a - lo, min(512, hi - a)))) for a in range(lo, hi, 512)]

    def feat(view, lo, hi, chunk):
        return [(view, a, min(512, hi - a), KD, 0, 'feat', 'copy',
                 (lambda u, m, a=a: c.zT[:, chunk + (a - lo) // P + u:chunk + (a - lo) // P + u + m, :]))
                for a in range(lo, hi, 512)]

    def add_x(view, k, gated, src, waits, name):
        tiles = [(view, a, 512, k, 0, 'tok', a if gated else 'add', (lambda n, a=a: c.x[:, n, a:a + 512]))
                 for a in (0, 512)]
        add(proj(c, name, src, waits, tiles))
        updates[0] += 1

    def ffn(gate, up, up_col, down, gated, ready):
        st = ffn_stage(c, gate, up, up_col, down, gated, number('ffn'))
        st['waits'] = ready
        add(st)
        updates[0] += 1

    for l in range(2):
        add(ada_stage(c, l, 0))
        h = norm(c.x, lambda kc: c.modA[:, kc:kc + 1], lambda kc: c.modC[:, kc:kc + 1],
                 x_waits() + [('mod_ready', 2 * l + 1)])
        v = rows_view(t['w_in'][l])
        z = lambda lo: (lambda n, off, w: c.z[:, n, lo + off:lo + off + w])
        p = add(proj(c, 'w_in', c.hT, h, tok(v, 0, Z_BQ, z(0)) + tok(v, Z_UV, IN1, z(Z_UV)) +
                     feat(v, Z_BQ, Z_BI, 0) + tok(v, Z_BI, Z_UV, z(Z_BI))))
        ev = proj_evacuated(p)
        add(ada_stage(c, l, 1))
        add(dsa_stage(c, l, ev))
        add(dict(kind='gmlp', k=l, evacuated=ev))
        add(dict(kind='hgrn', k=l, evacuated=ev))
        tr = add(turn_stage(c, number('turn'), [3, 4, 5, 6, 7], [('mix_ready', 4 * (l + 1))]))
        add_x(rows_view(t['w_out'][l]), KD, True, c.mixT, turned_events(tr) + [('att_mixT', 2 * (l + 1))], 'w_out')
        h = norm(c.x, lambda kc: c.modA[:, 8 + kc:9 + kc], lambda kc: c.modC[:, 16 + kc:17 + kc],
                 x_waits() + [('mod_ready', 2 * l + 2)])
        if l == 0:
            ffn(rows_view(t['ffn_w_gate'][0]), rows_view(t['ffn_w_up'][0]), 0, rows_view(t['ffn_w_down'][0]), True, h)
        else:
            st = add(moe_stage(c))
            st['hT'] = h
            updates[0] += 1
    add(dict(kind='final', k=0, waits=x_waits(), gain=t['g_final']))
    updates[0] += 1
    add(dict(kind='mem'))
    for l in range(2):
        h = norm(c.x, columns('norm_mix_g_2', l))
        if l == 0:
            p = add(proj(c, 'ev_in', c.hT, h, feat(rows_view(t['ev_w_in_2'][0]), 0, 2048, 0)))
            add(dict(kind='even', evacuated=proj_evacuated(p)))
            add_x(rows_view(t['ev_w_out_2'][0]), KD, False, c.mixT, [('ev_mixT', 4)], 'ev_out')
        else:
            v = rows_view(t['od_w_in_2'][0])
            dst = lambda n, off, w: c.z[:, n, off:off + w]
            p = add(proj(c, 'od_in', c.hT, h, feat(v, 0, 1024, 0) + tok(v, 1024, 2728, dst)))
            add(dict(kind='mlstm', evacuated=proj_evacuated(p)))
            add(dict(kind='mla_in', evacuated=proj_evacuated(p)))
            q = lambda n, off, w: c.z[:, n, OD_Q + off:OD_Q + off + w]
            kv = lambda n, off, w: c.xn[:, n, off:off + w]
            p = add(proj(c, 'latents', c.rT, [('la_ready', 5)],
                         tok(rows_view(t['od_w_uq_2'][0]), 0, MLA_HEADS * QKW, q, k=3) +
                         tok(rows_view(t['od_w_ukv_2'][0]), 0, 1024, kv, k=2, ksrc=3)))
            add(mla_stage(c, proj_evacuated(p)))
            tr = add(turn_stage(c, number('turn'), [0, 1, 2, 3], [('mix_ready', 10)]))
            add_x(rows_view(t['od_w_out_2'][0]), KD, False, c.mixT, turned_events(tr) + [('att_mixT', 8)], 'od_out')
        h = norm(c.grow, columns('mem_norm_g_2', l), waits=[('mem_loaded', 32)])
        v = rows_view(t['xattn_wkv_2'][l])
        dst = lambda n, off, w: c.z[:, n, off:off + w]
        add(proj(c, 'xa_kv', c.hT, h, feat(v, 0, 512, 8) + tok(v, 512, 1024, dst)))
        h = norm(c.x, columns('norm_xattn_g_2', l))
        p = add(proj(c, 'xa_q', c.hT, h, feat(rows_view(t['xattn_wq_2'][l]), 0, 512, 0)))
        add(xa_stage(c, proj_evacuated(p)))
        add_x(rows_view(t['xattn_wo_2'][l]), 4, False, c.mixT, [('att_mixT', 6 if l == 0 else 10)], 'xa_out')
        h = norm(c.x, columns('norm_ffn_g_2', l))
        gu = rows_view(t['ffn_w_gate_up_2'][l])
        ffn(gu, gu, F_DENSE, rows_view(t['ffn_w_down_2'][l]), False, h)
    add(dict(kind='final', k=1, waits=x_waits(), gain=t['final_norm_g_2']))
    updates[0] += 1
    c.x_updates = updates[0]
    return stages


def build(nc, tensors, out, stop=None):
    c = Core()
    c.t = tensors
    with ExitStack() as ctx:
        def sb(name, shape, dt=F32):
            return ctx.enter_context(nc.sbuf_tensor(name, shape, dt))

        class Semaphores(dict):
            def __missing__(self, name):
                self[name] = ctx.enter_context(nc.semaphore(name))
                return self[name]
        c.s = Semaphores()
        c.pb = [ctx.enter_context(nc.psum_tensor(f'bank{i}', [P, 512], F32)) for i in range(8)]
        c.landed = [c.s[f'landed{i}'] for i in range(RING)]
        c.again = [c.s[f'landed_again{r}'] for r in range(2)]

        c.x = sb('x', [P, NT, D])
        c.xn = sb('xn', [P, NT, D])
        c.hT = sb('hT', [P, KD, S])
        c.z = sb('z', [P, NT, IN1])
        c.zT = sb('zT', [P, 16, S])
        c.mix = sb('mix', [P, NT, D])
        c.mixT = sb('mixT', [P, KD, S])
        c.ring = sb('ring', [P, RING, SLOT])
        c.rT = sb('rT', [P, 7, S])
        c.L = sb('L', [P, 2048])
        c.PT = sb('PT', [P, 2048])
        c.AT = sb('AT', [P, NT, B_HEADS, P])
        c.grow = sb('grow', [P, NT, D])
        c.gain = c.grow[:, 0, :]
        c.tmp = c.L[:, 1536:2048]
        c.col1, c.col2 = sb('col1', [P, P]), sb('col2', [P, P])
        c.modC, c.modA = sb('modC', [P, 32]), sb('modA', [P, 16])
        c.condT, c.condB = sb('condT', [P, KD]), sb('condB', [P, KD, P])
        c.wsT, c.wpool = sb('wsT', [P, 8, P]), sb('wpool', [P, 4, P])
        c.wrouter = sb('wrouter', [P, KD, N_EXP])
        c.onorm, c.vng, c.vnb = sb('onorm', [P, 2, HD]), sb('vng', [P, 2, 256]), sb('vnb', [P, 2, 256])
        c.mlg, c.gbias = sb('mlg', [P, 512]), sb('gbias', [P, 8])
        c.ident, c.triT = sb('ident', [P, P]), sb('triT', [P, P])
        c.ones, c.zero = sb('ones', [P, S]), sb('zero', [P, S])
        c.maskQ2, c.maskK = sb('maskQ2', [P, 2 * P]), sb('maskK', [P, P])
        c.resume, c.selT = sb('resume', [P, S]), sb('selT', [P, 8, P])
        c.neghalf, c.invf = sb('neghalf', [P, 16]), sb('invf', [P, 32])
        c.lmask = sb('lmask', [P, len(LEVELS) + 1, P], U8)
        c.slotF2, c.slotP, c.inv1 = sb('slotF2', [P, 2 * P]), sb('slotP', [P, 2]), sb('inv1', [P, 16])
        c.sin, c.cos = sb('sin', [P, 96]), sb('cos', [P, 96])
        c.score, c.sel = sb('score', [P, NT, S]), sb('sel', [P, NT, S])
        c.work, c.eq = sb('work', [P, S]), sb('eq', [P, S])
        c.ss, c.ms, c.rstd, c.mx = sb('ss', [P, 2]), sb('ms', [P, 2]), sb('rstd', [P, 2]), sb('mx', [P, 8])
        c.nmx, c.esum, c.rsum, c.top8 = sb('nmx', [P, 8]), sb('esum', [P, 8]), sb('rsum', [P, 8]), sb('top8', [P, 8])
        c.cnt, c.hss, c.hms, c.hrstd = sb('cnt', [P, 2]), sb('hss', [P, 12]), sb('hms', [P, 12]), sb('hrstd', [P, 12])
        c.gss, c.gms, c.grstd, c.gsum = sb('gss', [P, 2]), sb('gms', [P, 2]), sb('grstd', [P, 2]), sb('gsum', [P, 2])
        c.lbd, c.lbe, c.lbl, c.mss = sb('lbd', [P, 6]), sb('lbe', [P, 6]), sb('lbl', [P, 6]), sb('mss', [P, 8])
        c.mrstd, c.mden, c.gcols, c.lss = sb('mrstd', [P, 8]), sb('mden', [P, 8]), sb('gcols', [P, 16]), sb('lss', [P, 4])
        c.lms, c.lrstd, c.meq, c.mexp = sb('lms', [P, 4]), sb('lrstd', [P, 4]), sb('meq', [P, 16]), sb('mexp', [P, 18])
        c.posf, c.sink = sb('posf', [P, 4]), sb('sink', [P, 1])
        c.iw = sb('iw', [P, NT, IDX_HEADS])
        c.logits, c.chosen = sb('logits', [P, NT, N_EXP]), sb('chosen', [P, NT, N_EXP])
        c.slots, c.gates = sb('slots', [P, NT, N_EXP + 1]), sb('gates', [P, NT, N_EXP + 1])
        c.posi, c.count = sb('posi', [P, 4], I32), sb('count', [P, 1], I32)
        c.prow1, c.prow2 = c.PT[:, 0:P], c.PT[:, P:2 * P]
        c.wsraw = c.L[:, 0:8 * P].rearrange('p (g s) -> p g s', g=8)
        zf = c.z[:, :, :].rearrange('p n f -> p (n f)')
        c.ang, c.angc, c.turns = zf[:, 0:96], zf[:, 96:192], zf[:, 192:288]
        zi = zf[:, 512:1536].bitcast(I32)
        c.iotaT, c.iotaS, c.xor, c.less, c.bits = (zi[:, i * P:i * P + P] for i in range(5))
        c.iota1 = zi[:, 5 * P:5 * P + 16]
        c.grows = c.rT[0:ML_HEADS, :, :]
        c.mrows = c.rT[0:N_EXP, 0:2, :]
        c.fs = c.L[:, 0:512].rearrange('p (n f) -> p n f', n=NT)
        c.fa = c.L[:, 512:1024].rearrange('p (n f) -> p n f', n=NT)
        c.faT = c.L[:, 1024:1536].rearrange('p (n a t) -> p n a t', n=NT, a=2)
        c.slotsB = zf[:, 0:2048].rearrange('p (e t) -> p e t', e=N_EXP)
        c.gatesB = zf[:, 2048:4096].rearrange('p (e t) -> p e t', e=N_EXP)
        c.hTe = zf[:, 4096:5120].rearrange('p (k t) -> p k t', k=KD)
        c.ye = c.mix[:, 0, :]
        c.onehot = c.mix[:, 1, 0:256].rearrange('p (n t) -> p n t', n=NT)
        c.combine = c.mix[:, 1, 256:512]
        c.moe_gate = tensors['moe_w_gate'][0].rearrange('e (k p) f -> p (e k) f', p=P)
        c.moe_up = tensors['moe_w_up'][0].rearrange('e (k p) f -> p (e k) f', p=P)
        c.moe_down = tensors['moe_w_down'][0].rearrange('e (k p) n -> p (e k) n', p=P)

        c.jobs, c.n_tiles = [], 0
        c.att = dict(a=0, e=0, t=0, ta=0, tb=0)
        c.turn = dict(a=0, b=0)
        c.n_log_e = 0
        stages = make_plan(c)[:stop]
        last_x = stages[-1]['x_before'] + 1 if stop else c.x_updates

        def x_written(dve):
            dve.sem_inc(c.s['x_ready'], 1)
        c.x_written = x_written

        block = ctx.enter_context(nc.Block())

        @block.sync
        def _(sp):
            j = 0
            for st in stages:
                if st['kind'] == 'ffn':
                    ffn_sp(c, sp, st)
                    j = st['j0'] + 3 * st['steps']
                elif st['kind'] == 'moe':
                    moe_sp(c, sp, st)
                    j = st['j0'] + 3 * MOE_STEPS * N_EXP
                else:
                    mine = [x for x, _ in st.get('cols', [])]
                    mine += [x for jobs, _, _ in st.get('rows', []) for x, _, _ in jobs]
                    mine += [x for tl in st.get('tiles', []) for x, _, _ in tl['jobs']]
                    for x in mine:
                        assert x == j
                        if j >= RING:
                            sem, v = c.jobs[j - RING][1]
                            sp.wait_ge(c.s[sem], v)
                        start_job(c, sp, j)
                        j += 1
            if not stop:
                sp.wait_ge(c.s['x_ready'], last_x)
                for n in range(NT):
                    sp.dma_start(out[0, n * P:n * P + P, :], c.x[:, n, :]).then_inc(c.s['stored'], 16)
                sp.wait_ge(c.s['stored'], 32)

        @block.tensor
        def _(pe):
            setup_pe(c, pe)
            for st in stages:
                run = PE.get(st['kind'])
                if run:
                    run(c, pe, st)

        @block.scalar
        def _(act):
            setup_act(c, act)
            for st in stages:
                run = ACTS.get(st['kind'])
                if run:
                    run(c, act, st)

        @block.vector
        def _(dve):
            c.vstep = chain(dve, c.s['vector_step'])
            setup_dve(c, dve)
            for st in stages:
                run = DVE.get(st['kind'])
                if run:
                    run(c, dve, st)

        @block.gpsimd
        def _(pool):
            c.pstep = chain(pool, c.s['pool_step'])
            setup_pool(c, pool)
            for st in stages:
                run = POOL.get(st['kind'])
                if run:
                    run(c, pool, st)
    return c


def final_all_act(c, act, st):
    final_sp(c, act, st)
    final_act(c, act, st)


PE = dict(ada=ada_pe, norm=norm_pe, proj=proj_pe, dsa=dsa_pe, gmlp=gmlp_pe, hgrn=hgrn_pe, turn=turn_pe, ffn=ffn_pe,
          moe=moe_pe, even=even_pe, xa=xa_pe, mlstm=mlstm_pe, mla_in=mla_in_pe, mla=mla_pe)
ACTS = dict(ada=ada_act, norm=norm_act, proj=proj_act, dsa=dsa_act, gmlp=gmlp_act, hgrn=hgrn_act, turn=turn_act,
            ffn=ffn_act, moe=moe_act, xa=xa_act, mlstm=mlstm_act, mla_in=mla_in_act, mla=mla_act,
            final=final_all_act, mem=mem_act)
DVE = dict(ada=ada_dve, norm=norm_dve, proj=proj_dve, dsa=dsa_dve, gmlp=gmlp_dve, hgrn=hgrn_dve, turn=turn_dve,
           ffn=ffn_dve, moe=moe_dve, even=even_dve, xa=xa_dve, mlstm=mlstm_dve, mla_in=mla_in_dve, mla=mla_dve,
           final=final_dve)
POOL = dict(norm=norm_pool, dsa=dsa_pool, gmlp=gmlp_pool, hgrn=hgrn_pool, final=final_pool, mlstm=mlstm_pool,
            mla_in=mla_in_pool)


def kernel(**inputs):
    import concourse.bacc as bacc
    from concourse.bass_utils import run_bass_kernel_spmd

    nc = bacc.Bacc("TRN2", target_bir_lowering=False, num_devices=1)
    arrays, tensors = {}, {}
    for name in INPUTS:
        a = np.ascontiguousarray(inputs[name])
        arrays[f'in_{name}'] = a
        tensors[name] = nc.dram_tensor(f'in_{name}', a.shape, mybir.dt.from_np(a.dtype), kind="ExternalInput").ap()
    out = nc.dram_tensor('out_x', (1, S, D), F32, kind="ExternalOutput").ap()
    build(nc, tensors, out)
    r = run_bass_kernel_spmd(nc, [arrays], core_ids=[0])
    return r.results[0]['out_x']
```

```python
from contextlib import ExitStack

import numpy as np

import concourse.bass as bass
from concourse import mybir

F32 = mybir.dt.float32
R32 = mybir.dt.float32r
I32 = mybir.dt.int32
U8 = mybir.dt.uint8
ALU = mybir.AluOpType
ACT = mybir.ActivationFunctionType
AX = mybir.AxisListType.X

P = 128
S = 256
NT = S // P
D = 1024
KD = D // P
HD = 64
A_HEADS, IDX_HEADS, TOPK = 6, 4, 64
B_HEADS, PAIRS = 6, 3
CHUNK = 64
IN1 = 2884
Z_AQ, Z_AK, Z_AV, Z_IQ, Z_IK, Z_IW = 0, 384, 448, 512, 768, 832
Z_BQ, Z_BF, Z_BI, Z_BG, Z_UV = 836, 1220, 1604, 1988, 2372
F_DENSE, F_EXPERT, N_EXP = 2816, 3584, 8
FT = 256
ML_HEADS, MLA_HEADS, NOPE, ROPE_W, VD = 4, 8, 64, 32, 64
QKW = NOPE + ROPE_W
XA_HEADS, XA_D = 4, 128
EPS = 1e-6
NEG = -1.0e30
LOWEST = -3.0e38
TAKEN = -3.3e38
RING = 6
SLOT = 2048
LOAD = 32

INPUTS = ['x', 'c', 'positions', 'w_ada', 'b_ada', 'g_norm_mix', 'g_norm_ffn', 'w_in', 'w_out',
          'hgrn_lb_logits', 'hgrn_out_norm', 'gmlp_vnorm_g', 'gmlp_vnorm_b', 'gmlp_w_s', 'gmlp_b_s',
          'ffn_w_gate', 'ffn_w_up', 'ffn_w_down', 'moe_w_router', 'moe_w_gate', 'moe_w_up',
          'moe_w_down', 'g_final', 'mem_2', 'positions_2', 'norm_mix_g_2', 'norm_xattn_g_2',
          'mem_norm_g_2', 'xattn_wq_2', 'xattn_wkv_2', 'xattn_wo_2', 'norm_ffn_g_2',
          'ffn_w_gate_up_2', 'ffn_w_down_2', 'ev_w_in_2', 'ev_conv_w_2', 'ev_pool_w_2',
          'ev_pool_scale_2', 'ev_w_out_2', 'od_w_in_2', 'od_gate_bias_2', 'od_ml_norm_g_2',
          'od_q_norm_g_2', 'od_kv_norm_g_2', 'od_w_uq_2', 'od_w_ukv_2', 'od_w_out_2',
          'final_norm_g_2']

ROWS1 = [('g_norm_mix', 'l (c p) -> (l c) p', 16), ('g_norm_ffn', 'l (c p) -> (l c) p', 16),
         ('norm_mix_g_2', 'l (c p) -> (l c) p', 16), ('norm_xattn_g_2', 'l (c p) -> (l c) p', 16),
         ('mem_norm_g_2', 'l (c p) -> (l c) p', 16), ('norm_ffn_g_2', 'l (c p) -> (l c) p', 16),
         ('od_q_norm_g_2', 'l (c p) -> (l c) p', 3), ('od_kv_norm_g_2', 'l (c p) -> (l c) p', 2),
         ('ev_pool_scale_2', 'l (c p) -> (l c) p', 4), ('ev_conv_w_2', 'l k (c p) -> (l k c) p', 12)]
ROWS2 = [('b_ada', 'l (c p) -> (l c) p', 96), ('hgrn_lb_logits', 'l (c p) -> (l c) p', 6),
         ('gmlp_b_s', 'l g p -> (l g) p', 8), ('c', 'l (c p) -> (l c) p', 8)]


def offsets(rows):
    at, out = 0, {}
    for name, _, n in rows:
        out[name] = at
        at += n
    return out, at


COL1, NCOL1 = offsets(ROWS1)
COL2, NCOL2 = offsets(ROWS2)


class Core:
    pass


def chain(eng, sem):
    done = [0]

    def step(ins):
        done[0] += 1
        ins.then_inc(sem, 1)
        eng.wait_ge(sem, done[0])
    return step


def signal(eng, ins, sem, value):
    ins.then_inc(sem, 1)
    eng.wait_ge(sem, value)


def magnitude(dve, out, x):
    return dve.scalar_tensor_tensor(out, x, -1.0, x, ALU.mult, ALU.max)


def in_order(**events):
    at, before = 0, {}
    for name, times in events.items():
        before[name] = at
        at += times
    return before


ROUNDED = {}


def r32(ap):
    return bass.AP(tensor=ROUNDED[ap.tensor.name], offset=ap.offset, ap=ap.ap)


def high(ap):
    return r32(ap).bitcast(F32)


def product(pe, out, a, b, start, stop):
    pe.matmul(out, r32(a[0]), r32(b[1]), start=start, stop=False, skip_group_check=True)
    pe.matmul(out, r32(a[1]), r32(b[0]), start=False, stop=False, skip_group_check=True)
    return pe.matmul(out, r32(a[0]), r32(b[0]), start=False, stop=stop, skip_group_check=True)


def rows_view(ap):
    return ap.rearrange("(k p) n -> p k n", p=P)


def job(core, loads, release):
    j = len(core.jobs)
    core.jobs.append((loads, release))
    return j


def chunks(ap, k, w):
    return ap[:, 0:k * w].rearrange('p (k w) -> p k w', k=k)


def gemm_jobs(core, view, col, w, k, release, early=None):
    per = min(k, SLOT // w, 4)
    jobs = []
    for k0 in range(0, k, per):
        kk = min(per, k - k0)
        h = (kk + 1) // 2
        loads = [(0, h, w, view[:, k0:k0 + h, col:col + w])]
        if kk > h:
            loads.append((h * w, kk - h, w, view[:, k0 + h:k0 + kk, col:col + w]))
        else:
            hw = w // 2
            loads = [(0, 1, (hw, w), view[:, k0:k0 + 1, col:col + hw]),
                     (hw, 1, (w - hw, w), view[:, k0:k0 + 1, col + hw:col + w])]
        last = k0 + kk == k
        jobs.append((job(core, loads, release if last or not early else early()), k0, kk))
    return jobs


def start_job(core, sp, j):
    loads, _ = core.jobs[j]
    for off, k, w, src in loads:
        dst = core.ring[:, j % RING, off:off + k * (w[0] if isinstance(w, tuple) else w)]
        sp.dma_start(dst.rearrange('p (k w) -> p k w', k=k), src).then_inc(core.landed[j % RING], 16)


def wait_job(core, pe, j):
    pe.wait_ge(core.landed[j % RING], LOAD * (j // RING + 1))


def proj(core, name, src, waits, tiles, hi, ready=None):
    st = dict(kind='proj', name=name, src=src, waits=waits, ready=ready, tiles=[], hi=hi, s0=core.n_split,
              presplit=0)

    def early():
        core.n_early += 1
        return ('proj_read', core.n_early)
    for view, col, w, k, ksrc, layout, evac, dst in tiles:
        t = core.n_tiles
        core.n_tiles += 1
        jobs = gemm_jobs(core, view, col, w, k, ('proj_done', 2 * t + 2), early)
        jobs = [(j, k0, kk, core.n_split + i) for i, (j, k0, kk) in enumerate(jobs)]
        core.n_split += len(jobs)
        st['tiles'].append(dict(t=t, jobs=jobs, w=w, k=k, ksrc=ksrc, layout=layout, evac=evac, dst=dst))
    st['job_of'] = {s: j for tl in st['tiles'] for j, _, _, s in tl['jobs']}
    return st


def proj_pe(c, pe, st):
    for sem, v in st['waits']:
        pe.wait_ge(c.s[sem], v)
    src_hi, src_lo = st['src']
    waited = set()
    for tl in st['tiles']:
        t, w, k = tl['t'], tl['w'], tl['k']
        if t >= 2:
            pe.wait_ge(c.s['proj_evac_a'], t - 1)
            pe.wait_ge(c.s['proj_evac_b'], t - 1)
        for j, k0, kk, s in tl['jobs']:
            pe.wait_ge(c.s['proj_lo'], s + 1)
            wh, wl = (chunks(x, kk, w) for x in (st['hi'][(s - st['s0']) % len(st['hi'])], c.ring[:, j % RING, :]))
            for half in range(2):
                bank = c.pb[4 + 2 * (t % 2) + half]
                for i in range(kk):
                    kc, x = k0 + i, tl['ksrc'] + k0 + i
                    if st['ready'] and x not in waited:
                        waited.add(x)
                        sem, v = st['ready'](x)
                        pe.wait_ge(c.s[sem], v)
                    last = kc == k - 1
                    if tl['layout'] == 'tok':
                        tok = slice(half * P, half * P + P)
                        mm = product(pe, bank[:, 0:w], (src_hi[:, x, tok], src_lo[:, x, tok]), (wh[:, i, :], wl[:, i, :]),
                                     kc == 0, last)
                    else:
                        n = w // (2 * P)
                        for u in range(n):
                            f = slice((half * n + u) * P, (half * n + u + 1) * P)
                            mm = product(pe, bank[:, u * S:u * S + S], (wh[:, i, f], wl[:, i, f]),
                                         (src_hi[:, x, :], src_lo[:, x, :]), kc == 0 and u == 0, last)
                if last:
                    mm.then_inc(c.s['proj_done'], 1)
            if not last:
                mm.then_inc(c.s['proj_read'], 1)


def proj_out(c, tl, half):
    w = tl['w']
    bank = c.pb[4 + 2 * (tl['t'] % 2) + half]
    if tl['layout'] == 'tok':
        return bank[:, 0:w], tl['dst'](half)
    n = w // (2 * P)
    return bank[:, 0:n * S].rearrange('p (u t) -> p u t', u=n), tl['dst'](half * n, n)


def proj_split_act(c, act, st, j, kk, w, s):
    wait_job(c, act, j)
    H = len(st['hi'])
    if s - H >= st['s0']:
        sem, v = c.jobs[st['job_of'][s - H]][1]
        act.wait_ge(c.s[sem], v)
    n = kk * w
    act.activation(r32(st['hi'][(s - st['s0']) % H][:, 0:n]), c.ring[:, j % RING, 0:n], ACT.Copy)\
       .then_inc(c.s['proj_hi'], 1)


def proj_split_dve(c, dve, st, j, kk, w, s):
    dve.wait_ge(c.s['proj_hi'], s + 1)
    n = kk * w
    words = c.ring[:, j % RING, 0:n]
    dve.tensor_tensor(r32(words), words, high(st['hi'][(s - st['s0']) % len(st['hi'])][:, 0:n]), ALU.subtract)\
       .then_inc(c.s['proj_lo'], 1)


def first_split(c, eng, st, i):
    if st is None:
        return
    if st['kind'] == 'ffn':
        (ffn_hi if eng is c.act else ffn_lo)(c, eng, st, i, 0, 0)
    else:
        j, k0, kk, s = [x for tl in st['tiles'] for x in tl['jobs']][i]
        w = st['tiles'][0]['w']
        (proj_split_act if eng is c.act else proj_split_dve)(c, eng, st, j, kk, w, s)


def proj_act(c, act, st):
    for sem, v in st['waits']:
        act.wait_ge(c.s[sem], v)

    def evacuate(tl):
        if tl['evac'] == 'copy':
            act.wait_ge(c.s['proj_done'], 2 * tl['t'] + 1)
            src, dst = proj_out(c, tl, 0)
            act.activation(dst, src, ACT.Copy).then_inc(c.s['proj_evac_a'], 1)
    before = None
    for tl in st['tiles']:
        for j, k0, kk, s in tl['jobs']:
            if s >= st['s0'] + st['presplit']:
                proj_split_act(c, act, st, j, kk, tl['w'], s)
        if before:
            evacuate(before)
        before = tl
    evacuate(before)


def proj_dve(c, dve, st):
    def evacuate(tl):
        t, w = tl['t'], tl['w']
        if tl['evac'] == 'copy':
            dve.wait_ge(c.s['proj_done'], 2 * t + 2)
            src, dst = proj_out(c, tl, 1)
            dve.tensor_copy(dst, src).then_inc(c.s['proj_evac_b'], 1)
            return
        for half in range(2):
            dve.wait_ge(c.s['proj_done'], 2 * t + 1 + half)
            src, dst = proj_out(c, tl, half)
            if tl['evac'] == 'add':
                signal(dve, dve.tensor_tensor(dst, src, dst, ALU.add), c.s['proj_evac_' + 'ab'[half]], t + 1)
            else:
                tmp = c.tmp[:, 0:w]
                gate = c.grow[:, 0, tl['evac']:tl['evac'] + w]
                signal(dve, dve.tensor_tensor(tmp, src, gate, ALU.mult), c.s['proj_evac_' + 'ab'[half]], t + 1)
                c.vstep(dve.tensor_tensor(dst, dst, tmp, ALU.add))
    before = None
    for tl in st['tiles']:
        for j, k0, kk, s in tl['jobs']:
            if s >= st['s0'] + st['presplit']:
                proj_split_dve(c, dve, st, j, kk, tl['w'], s)
        if before:
            evacuate(before)
        before = tl
    evacuate(before)
    if before['evac'] != 'copy':
        dve.wait_ge(c.s['proj_evac_b'], before['t'] + 1)
        c.x_written(dve)


def proj_evacuated(st):
    last = st['tiles'][-1]['t'] + 1
    return [('proj_evac_a', last), ('proj_evac_b', last)]


def norm_act(c, act, st):
    k = st['k']
    for sem, v in st['waits']:
        act.wait_ge(c.s[sem], v)
    for n in range(NT):
        act.activation(c.xn[:, n, :], st['src'][:, n, :], ACT.Square,
                       accum_out=c.ss[:, n:n + 1]).then_inc(c.s['norm_ss'], 1)
        act.wait_ge(c.s['norm_ss'], NT * k + n + 1)
    if st['x_before']:
        act.wait_ge(c.s['x_ready'], st['x_before'])
    if st['last_tile'] is not None:
        act.wait_ge(c.s['proj_done'], 2 * st['last_tile'] + 2)
    for i in range(2):
        first_split(c, act, st['next'], i)
    for j in range(4):
        act.wait_ge(c.s['norm_turned'], 4 * k + j + 1)
        for i in range(2):
            kc = 2 * j + i
            scale, shift = st['scale'](kc), st['shift'](kc) if st['shift'] else 0.0
            o = act.activation(r32(c.hT[:, kc, :]), c.pb[j][:, i * S:i * S + S],
                               ACT.Identity if st['shift'] else ACT.Copy, bias=shift, scale=scale)
        o.then_inc(c.s['h_hi'], 1)


def norm_pool(c, pool, st):
    k = st['k']
    pool.wait_ge(c.s['norm_ss'], NT * k + NT)
    c.pstep(pool.tensor_scalar(c.ms[:, 0:NT], c.ss[:, 0:NT], 1.0 / D, EPS, ALU.mult, ALU.add))
    pool.tensor_tensor(c.rstd[:, 0:NT], c.ms[:, 0:NT], c.neghalf[:, 0:NT], ALU.pow)\
        .then_inc(c.s['norm_rstd'], 1)


def norm_dve(c, dve, st):
    k = st['k']
    dve.wait_ge(c.s['norm_rstd'], k + 1)
    for sem, v in st['waits']:
        dve.wait_ge(c.s[sem], v)
    for n in range(NT):
        dve.tensor_scalar(c.xn[:, n, :], st['src'][:, n, :], c.rstd[:, n:n + 1], None, ALU.mult)\
           .then_inc(c.s['norm_xn'], 1)
    first_split(c, dve, st['next'], 0)
    for j in range(4):
        if j == 2:
            first_split(c, dve, st['next'], 1)
        dve.wait_ge(c.s['h_hi'], 4 * k + j + 1)
        both = c.hL[:, 2 * j:2 * j + 2, :]
        for i in range(2):
            kc = 2 * j + i
            src = c.pb[j][:, i * S:i * S + S]
            if st['shift']:
                o = dve.tensor_scalar(c.hL[:, kc, :], src, st['scale'](kc), st['shift'](kc), ALU.mult, ALU.add)
                if i:
                    c.vstep(o)
                    o = dve.tensor_tensor(r32(both), both, high(c.hT[:, 2 * j:2 * j + 2, :]), ALU.subtract)
            else:
                o = dve.scalar_tensor_tensor(r32(c.hL[:, kc, :]), src, st['scale'](kc), high(c.hT[:, kc, :]),
                                             ALU.mult, ALU.subtract)
        o.then_inc(c.s['h_lo'], 1)


def norm_pe(c, pe, st):
    k = st['k']
    pe.wait_ge(c.s['norm_xn'], NT * (k + 1))
    for j in range(4):
        for i in range(2):
            for n in range(NT):
                kc = 2 * j + i
                mm = pe.transpose(c.pb[j][:, i * S + n * P:i * S + n * P + P],
                                  c.xn[:, n, kc * P:kc * P + P], c.ident[:, :])
        mm.then_inc(c.s['norm_turned'], 1)


def h_chunk(k):
    return lambda kc: ('h_lo', 4 * k + kc // 2 + 1)


def final_act(c, act, st):
    k = st['k']
    act.wait_ge(c.s['x_ready'], st['x_before'])
    for n in range(NT):
        act.activation(c.xn[:, n, :], c.x[:, n, :], ACT.Square,
                       accum_out=c.ss[:, n:n + 1]).then_inc(c.s['final_ss'], 1)
        act.wait_ge(c.s['final_ss'], NT * k + n + 1)


def final_pool(c, pool, st):
    k = st['k']
    pool.wait_ge(c.s['final_ss'], NT * (k + 1))
    c.pstep(pool.tensor_scalar(c.ms[:, 0:NT], c.ss[:, 0:NT], 1.0 / D, EPS, ALU.mult, ALU.add))
    pool.tensor_tensor(c.rstd[:, 0:NT], c.ms[:, 0:NT], c.neghalf[:, 0:NT], ALU.pow)\
        .then_inc(c.s['final_rstd'], 1)


def final_dve(c, dve, st):
    k = st['k']
    dve.wait_ge(c.s['final_rstd'], k + 1)
    dve.wait_ge(c.s['gain_row'], 16 * (k + 1))
    for n in range(NT):
        c.vstep(dve.scalar_tensor_tensor(c.x[:, n, :], c.x[:, n, :], c.rstd[:, n:n + 1], c.gain[:, :],
                                         ALU.mult, ALU.mult))
    c.x_written(dve)


def final_sp(c, act, st):
    for sem, v in st['waits']:
        act.wait_ge(c.s[sem], v)
    act.dma_start(c.gain[:, :], st['gain'].rearrange('(a n) -> a n', a=1).partition_broadcast(P))\
       .then_inc(c.s['gain_row'], 16)


def ffn_stage(core, gate_view, up_view, up_col, down_view, gated, k):
    st = dict(kind='ffn', k=k, gate=gate_view, up=up_view, up_col=up_col, down=down_view, gated=gated,
              j0=len(core.jobs), steps=F_DENSE // FT, split0=core.n_steps)
    core.n_steps += st['steps']
    for i in range(st['steps']):
        for q in range(2):
            job(core, None, ('ffn_gu', st['steps'] * 2 * k + 2 * i + 2))
        job(core, None, ('ffn_down', st['steps'] * 2 * k + 2 * i + 2))
    return st


def ffn_load(c, sp, st, q, i, slot):
    w = c.ring[:, slot, :]
    if q < 2:
        w = w.rearrange('p (k s n) -> p k s n', k=4, s=2)
        sp.dma_start(w[:, :, 0, :], st['gate'][:, 4 * q:4 * q + 4, bass.ds(i * FT, FT)])\
          .then_inc(c.landed[slot], 16)
        sp.dma_start(w[:, :, 1, :], st['up'][:, 4 * q:4 * q + 4, bass.ds(i * FT + st['up_col'], FT)])\
          .then_inc(c.landed[slot], 16)
    else:
        w = w.rearrange('p (k n) -> p k n', k=2)
        for a in range(2):
            sp.dma_start(w[:, a:a + 1, :], st['down'][:, bass.ds(i * 2 + a, 1), :])\
              .then_inc(c.landed[slot], 16)


def ffn_sp(c, sp, st):
    k, j0, steps = st['k'], st['j0'], st['steps']
    base = 2 * steps * k

    def load(q, i):
        j = j0 + 3 * i + q
        if i < 2:
            sem, v = c.jobs[j - RING][1]
            sp.wait_ge(c.s[sem], v)
        else:
            sp.wait_ge(c.s['ffn_gu' if q < 2 else 'ffn_down'], base + 2 * i - 2)
        ffn_load(c, sp, st, q, i, j % RING)
    for i in range(3):
        load(0, i)
        load(1, i)
        if i:
            load(2, i - 1)
    with sp.Fori(1, (steps - 1) // 2) as it:
        for r in (1, 0):
            i = it * 2 + (2 - r)
            for q, back in ((0, 0), (1, 0), (2, 1)):
                sp.wait_ge(c.s['ffn_gu' if q < 2 else 'ffn_down'], i * 2 + (base - 2 - 2 * back))
                par = (r + back) % 2
                ffn_load(c, sp, st, q, i - back, (j0 + 3 * par + q) % RING)
    load(2, steps - 1)


def ffn_loop(eng, steps, body):
    for i in range(2):
        body(i, i % 2, i)
    with eng.Fori(1, steps // 2) as it:
        for r in range(2):
            body(None, r, it * 2 + r)
    body(steps - 1, 0, steps - 1)


def ffn_slot(st, q, r):
    return (st['j0'] + 3 * r + q) % RING


def split_hi(c, act, st, q, r, m, hi, landed, sem):
    slot = ffn_slot(st, q, r)
    landed(q, r, m)
    act.activation(r32(hi[slot]), c.ring[:, slot, :], ACT.Copy).then_inc(sem, 1)


def split_lo(c, dve, st, q, r, hi, sem_in, value, sem_out):
    slot = ffn_slot(st, q, r)
    dve.wait_ge(sem_in, value)
    w = c.ring[:, slot, :]
    dve.tensor_tensor(r32(w), w, high(hi[slot]), ALU.subtract).then_inc(sem_out, 1)


def split_names(q):
    return ('gu_hi', 'gu_lo') if q < 2 else ('down_hi', 'down_lo')


def split_value(st, q, m):
    b = st['split0']
    return m * 2 + (2 * b + q + 1) if q < 2 else m + (b + 1)


def ffn_hi(c, act, st, q, r, m):
    def landed(q, r, m):
        j = st['j0'] + 3 * r + q
        act.wait_ge(c.landed[j % RING], (m - r) * (LOAD // 2) + LOAD * (j // RING + 1))
    split_hi(c, act, st, q, r, m, c.hi_ffn, landed, c.s[split_names(q)[0]])


def ffn_lo(c, dve, st, q, r, m):
    a, b = split_names(q)
    split_lo(c, dve, st, q, r, c.hi_ffn, c.s[a], split_value(st, q, m), c.s[b])


def ffn_pe(c, pe, st):
    k, steps = st['k'], st['steps']

    def parts(q, r, n):
        slot = ffn_slot(st, q, r)
        return chunks(c.hi_ffn[slot], n, SLOT // n), chunks(c.ring[:, slot, :], n, SLOT // n)

    def gate_up(n, r, q, m):
        if n == 0:
            pe.wait_ge(c.s['gu_lo'], split_value(st, q, m))
        wh, wl = parts(q, r, 4)
        tok = slice(n * P, n * P + P)
        for i in range(4):
            x = 4 * q + i
            if n == 0 and isinstance(m, int) and m == 0:
                sem, v = st['ready'](x)
                pe.wait_ge(c.s[sem], v)
            mm = product(pe, c.pb[4 + n][:, :], (c.hT[:, x, tok], c.hL[:, x, tok]), (wh[:, i, :], wl[:, i, :]),
                         x == 0, x == KD - 1)
        return mm

    def turn(n, m):
        pe.wait_ge(c.s[f'ffn_act{n}'], m + (steps * k + 1))
        for a in range(2):
            mm = pe.transpose(c.pb[6 + n][:, a * P:a * P + P], c.fa[:, n, a * P:a * P + P], c.ident[:, :])
        mm.then_inc(c.s[f'ffn_turned{n}'], 1)

    def down(n, r, m, first, last):
        pe.wait_ge(c.s['down_lo'], split_value(st, 2, m))
        pe.wait_ge(c.s[f'ffn_actT{n}'], m + (steps * k + 1))
        wh, wl = parts(2, r, 2)
        for h in range(2):
            col = slice(h * 512, h * 512 + 512)
            for a in range(2):
                mm = product(pe, c.pb[2 * n + h][:, :], (c.faT[:, n, a, :], c.faL[:, n, a, :]),
                             (wh[:, a, col], wl[:, a, col]), first and a == 0, last and a == 1)
        mm.then_inc(c.s['ffn_down'], 1)

    def body(i, r, m):
        first = i == 0
        if not first:
            pe.wait_ge(c.s['ffn_act0'], m + steps * k)
        gate_up(0, r, 0, m)
        if not first:
            turn(1, m - 1)
        gate_up(0, r, 1, m).then_inc(c.s['ffn_gu'], 1)
        if not first:
            down(1, 1 - r, m - 1, i == 1, False)
        gate_up(1, r, 0, None)
        turn(0, m)
        gate_up(1, r, 1, None).then_inc(c.s['ffn_gu'], 1)
        down(0, r, m, first, i == steps - 1)
    ffn_loop(pe, steps, body)
    turn(1, steps - 1)
    down(1, 0, steps - 1, False, True)


def ffn_act(c, act, st):
    k, steps = st['k'], st['steps']
    base = 2 * steps * k

    def hi(q, r, m):
        ffn_hi(c, act, st, q, r, m)

    def silu(n, m):
        act.wait_ge(c.s['ffn_gu'], m * 2 + (base + n + 1))
        act.activation(c.fs[:, n, :], c.pb[4 + n][:, 0:FT], ACT.Silu).then_inc(c.s[f'ffn_silu{n}'], 1)

    def copyT(n, m):
        act.wait_ge(c.s[f'ffn_turned{n}'], m + (steps * k + 1))
        act.activation(r32(c.faT[:, n, :, :]), c.pb[6 + n][:, 0:2 * P].rearrange('p (a t) -> p a t', a=2),
                       ACT.Copy).then_inc(c.s[f'ffn_T_hi{n}'], 1)

    def body(i, r, m):
        more = i != steps - 1
        if i != 0:
            copyT(1, m - 1)
        if more:
            hi(0, 1 - r, m + 1)
        silu(0, m)
        if more:
            hi(1, 1 - r, m + 1)
        hi(2, r, m)
        copyT(0, m)
        silu(1, m)
    ffn_loop(act, steps, body)
    copyT(1, steps - 1)


def ffn_dve(c, dve, st):
    k, steps = st['k'], st['steps']

    def lo(q, r, m):
        ffn_lo(c, dve, st, q, r, m)

    def mult(n, m):
        dve.wait_ge(c.s[f'ffn_silu{n}'], m + (steps * k + 1))
        dve.tensor_tensor(c.fa[:, n, :], c.fs[:, n, :], c.pb[4 + n][:, FT:2 * FT], ALU.mult)\
           .then_inc(c.s[f'ffn_act{n}'], 1)

    def lowT(n, m):
        dve.wait_ge(c.s[f'ffn_T_hi{n}'], m + (steps * k + 1))
        dve.tensor_tensor(r32(c.faL[:, n, :, :]), c.pb[6 + n][:, 0:2 * P].rearrange('p (a t) -> p a t', a=2),
                          high(c.faT[:, n, :, :]), ALU.subtract).then_inc(c.s[f'ffn_actT{n}'], 1)

    def body(i, r, m):
        more = i != steps - 1
        if i != 0:
            lowT(1, m - 1)
        if more:
            lo(0, 1 - r, m + 1)
        mult(0, m)
        if more:
            lo(1, 1 - r, m + 1)
        lo(2, r, m)
        lowT(0, m)
        mult(1, m)
    ffn_loop(dve, steps, body)
    lowT(1, steps - 1)
    base = 2 * steps * k
    for n in range(NT):
        dve.wait_ge(c.s['ffn_down'], base + 2 * steps - 1 + n)
        for h in range(2):
            out = c.x[:, n, h * 512:h * 512 + 512]
            if st['gated']:
                c.vstep(dve.tensor_tensor(c.tmp[:, :], c.pb[2 * n + h][:, :],
                                          c.grow[:, 1, h * 512:h * 512 + 512], ALU.mult))
                c.vstep(dve.tensor_tensor(out, out, c.tmp[:, :], ALU.add))
            else:
                c.vstep(dve.tensor_tensor(out, out, c.pb[2 * n + h][:, :], ALU.add))
    c.x_written(dve)


ADA_VECTORS = ((0, 1), (3, 4))
ADA_EVENTS = 20
ADA_FIRST = 2


def ada_stage(core, layer, part):
    view = rows_view(core.t['w_ada'][layer])
    st = dict(kind='ada', k=layer, part=part, cols=[], rows=[])
    n = ADA_EVENTS * layer + 8 * part
    for vi, vec in enumerate(ADA_VECTORS[part]):
        for q in range(4):
            n += 1
            col = vec * D + q * 256
            loads = [(0, 4, 256, view[:, 0:4, col:col + 256]), (1024, 4, 256, view[:, 4:8, col:col + 256])]
            st['cols'].append((job(core, loads, ('ada_done', n)), 16 * part + 8 * vi + 2 * q))
    if part:
        for g, vec in enumerate((2, 5)):
            for h in range(2):
                n += 1
                st['rows'].append((gemm_jobs(core, view, vec * D + 512 * h, 512, KD, ('ada_done', n)), g, h))
    return st


def ada_cols_pe(c, pe, st, lo, hi):
    for j, at in st['cols'][lo:hi]:
        wait_job(c, pe, j)
        w = chunks(c.ring[:, j % RING, :], KD, 256)
        for u in range(2):
            for kc in range(KD):
                mm = pe.matmul(c.pb[4][:, at + u:at + u + 1], w[:, kc, u * P:u * P + P],
                               c.condT[:, kc:kc + 1], start=kc == 0, stop=kc == KD - 1)
        mm.then_inc(c.s['ada_done'], 1)


def ada_rows_pe(c, pe, st, lo, hi):
    for i in range(lo, hi):
        jobs, g, h = st['rows'][i]
        for j, _, _ in jobs:
            wait_job(c, pe, j)
        for j, k0, kk in jobs:
            for a in range(kk):
                mm = pe.matmul(c.pb[4 + i][:, :], c.condB[:, k0 + a, :], chunks(c.ring[:, j % RING, :], kk, 512)[:, a, :],
                               start=k0 + a == 0, stop=k0 + a == KD - 1)
        mm.then_inc(c.s['ada_done'], 1)


def ada_pe(c, pe, st):
    if st['part'] == 0:
        pe.wait_ge(c.s['cond_ready'], 2)
        if st['x_before']:
            pe.wait_ge(c.s['x_ready'], st['x_before'])
        ada_cols_pe(c, pe, st, 0, len(st['cols']))


def ada_act(c, act, st):
    if st['part']:
        if st['x_before']:
            act.wait_ge(c.s['x_ready'], st['x_before'])
        for g, vec in enumerate((2, 5)):
            act.dma_start(c.grow[:, g, :], c.t['b_ada'][st['k']:st['k'] + 1, vec * D:vec * D + D]
                          .partition_broadcast(P)).then_inc(c.s['gate_bias'], 16)


def ada_dve(c, dve, st):
    if st['part'] == 0:
        ada_cols_dve(c, dve, st)


def ada_cols_dve(c, dve, st):
    k, part = st['k'], st['part']
    dve.wait_ge(c.s['ada_done'], ADA_EVENTS * k + 8 + 8 * part)
    lo = 16 * part
    bias = COL2['b_ada'] + 48 * k + 8 * ADA_VECTORS[part][0]
    signal(dve, dve.tensor_tensor(c.modC[:, lo:lo + 16], c.pb[4][:, lo:lo + 16],
                                  c.col2[:, bias:bias + 16], ALU.add), c.s['ada_cols'], 2 * k + part + 1)
    gain = COL1['g_norm_ffn' if part else 'g_norm_mix'] + 8 * k
    dve.scalar_tensor_tensor(c.modA[:, 8 * part:8 * part + 8], c.modC[:, lo + 8:lo + 16], 1.0,
                             c.col1[:, gain:gain + 8], ALU.add, ALU.mult).then_inc(c.s['mod_ready'], 1)


def ada_rows_dve(c, dve, st):
    k = st['k']
    dve.wait_ge(c.s['gate_bias'], 32 * (k + 1))
    for i, (_, g, h) in enumerate(st['rows']):
        dve.wait_ge(c.s['ada_done'], ADA_EVENTS * k + 17 + i)
        row = c.grow[:, g, h * 512:h * 512 + 512]
        dve.tensor_tensor(row, row, c.pb[4 + i][:, :], ALU.add).then_inc(c.s['ada_rows'], 1)


def setup_act(c, act):
    t = c.t
    for n in range(NT):
        act.dma_start(c.x[:, n, :], t['x'][0, n * P:n * P + P, :]).then_inc(c.s['x_loaded'], 16)
    n_in = 0

    def load(dst, src, **kw):
        act.dma_start(dst, src, **kw).then_inc(c.s['params_loaded'], 16)
    for rows, buf, at in ((ROWS1, c.prow1, COL1), (ROWS2, c.prow2, COL2)):
        for name, how, n in rows:
            a = t[name]
            load(buf[at[name]:at[name] + n, :], a.rearrange(how, p=P))
    for i, name in enumerate(('positions', 'positions_2')):
        load(c.posi[:, 2 * i:2 * i + 2], t[name].rearrange('a (n p) -> p (a n)', p=P), allow_slow_non_contiguous=True)
    load(c.onorm[:, :, :], t['hgrn_out_norm'].rearrange('(a l) v -> a l v', a=1).partition_broadcast(P))
    load(c.vng[:, :, :], t['gmlp_vnorm_g'].rearrange('(a l) v -> a l v', a=1).partition_broadcast(P))
    load(c.vnb[:, :, :], t['gmlp_vnorm_b'].rearrange('(a l) v -> a l v', a=1).partition_broadcast(P))
    load(c.mlg[:, :], t['od_ml_norm_g_2'].partition_broadcast(P))
    load(c.gbias[:, :], t['od_gate_bias_2'].partition_broadcast(P))
    load(c.wrouter[:, :, :], t['moe_w_router'][0].rearrange('(k p) e -> p k e', p=P))
    load(c.wpool[:, :, :], t['ev_pool_w_2'][0].rearrange('g c d -> c g d'))
    load(c.wsraw[:, :, :], t['gmlp_w_s'].rearrange('l g t s -> t (l g) s'))
    act.wait_ge(c.s['cols_ready'], 2)
    at = COL2['c']
    signal(act, act.activation(c.condT[:, :], c.col2[:, at:at + KD], ACT.Silu), c.s['cond_ready'], 1)
    act.wait_ge(c.s['angles_ready'], 2)
    act.activation(c.sin[:, :], c.ang[:, :], ACT.Sin).then_inc(c.s['rope_ready'], 1)
    act.activation(c.cos[:, :], c.angc[:, :], ACT.Sin).then_inc(c.s['rope_ready'], 1)


N_PARAM_LOADS = len(ROWS1) + len(ROWS2) + 2 + 3 + 2 + 1 + 2


def setup_pool(c, pool):
    step = c.pstep
    step(pool.memset(c.ident[:, :], 0.0))
    step(pool.affine_select(out=c.ident[:, :], in_=c.ident[:, :], compare_op=ALU.not_equal, fill=1.0, base=0,
                            pattern=[[-1, P]], channel_multiplier=1))
    step(pool.memset(c.ones[:, :], 1.0))
    step(pool.affine_select(out=c.triT[:, :], in_=c.ones[:, 0:P], compare_op=ALU.is_ge, fill=0.0, base=0,
                            pattern=[[1, P]], channel_multiplier=-1))
    step(pool.memset(c.zero[:, :], 0.0))
    step(pool.memset(c.maskQ2[:, 0:P], 0.0))
    step(pool.affine_select(out=c.maskQ2[:, P:2 * P], in_=c.zero[:, 0:P], compare_op=ALU.is_ge, fill=NEG, base=0,
                            pattern=[[-1, P]], channel_multiplier=1))
    step(pool.affine_select(out=c.maskK[:, :], in_=c.zero[:, 0:P], compare_op=ALU.is_ge, fill=NEG, base=0,
                            pattern=[[1, P]], channel_multiplier=-1))
    step(pool.memset(c.neghalf[:, :], -0.5))
    for j in range(HD // 2):
        step(pool.memset(c.invf[:, j:j + 1], float(np.float32(10000.0 ** (-j / 32.0)))))
    step(pool.memset(c.selT[:, :, :], 0.0))
    step(pool.affine_select(out=c.selT[:, :, :], in_=c.selT[:, :, :], compare_op=ALU.not_equal, fill=1.0, base=0,
                            pattern=[[-1, 8], [0, P]], channel_multiplier=1))
    step(pool.iota(c.iotaT[:, :], pattern=[[1, P]], base=0, channel_multiplier=0))
    step(pool.iota(c.iotaS[:, :], pattern=[[0, P]], base=0, channel_multiplier=1))
    step(pool.iota(c.iota1[:, :], pattern=[[1, 16]], base=1, channel_multiplier=0))
    step(pool.memset(c.resume[:, :], 1.0))
    step(pool.memset(c.resume[:, :].rearrange('p (c t) -> p c t', t=CHUNK)[:, :, 0:1], 0.0))
    step(pool.memset(c.AT[:, :, :, :], 0.0))
    pool.memset(c.sink[:, :], 0.0).then_inc(c.s['consts_ready'], 1)


LEVELS = (64, 32, 16, 8, 4, 2, 1)


def setup_dve(c, dve):
    step = c.vstep
    dve.wait_ge(c.s['consts_ready'], 1)
    dve.wait_ge(c.s['params_loaded'], 16 * N_PARAM_LOADS)
    for i, (buf, n) in enumerate(((c.col1, NCOL1), (c.col2, NCOL2))):
        dve.wait_ge(c.s['params_turned'], i + 1)
        signal(dve, dve.tensor_copy(buf[:, 0:n], c.pb[i][:, 0:n]), c.s['cols_ready'], i + 1)
    for i in range(2):
        dve.wait_ge(c.s['ws_turned'], i + 1)
        step(dve.tensor_tensor(c.wsT[:, 4 * i:4 * i + 4, :], c.pb[2 + i][:, :].rearrange('p (g t) -> p g t', g=4),
                               c.triT[:, :].unsqueeze(1).broadcast_to([P, 4, P]), ALU.mult))
    dve.wait_ge(c.s['cond_ready'], 1)
    signal(dve, dve.tensor_copy(c.condB[:, :, :], c.condT[:, :].unsqueeze(2).broadcast_to([P, KD, P])),
           c.s['cond_ready'], 2)
    step(dve.tensor_copy(c.posf[:, :], c.posi[:, :]))
    for i in range(2):
        step(dve.tensor_scalar(c.ang[:, 32 * i:32 * i + 32], c.invf[:, :], c.posf[:, i:i + 1], None, ALU.mult))
        step(dve.tensor_scalar(c.ang[:, 64 + 16 * i:80 + 16 * i], c.invf[:, 0:32:2], c.posf[:, 2 + i:3 + i], None,
                               ALU.mult))
    turn = 2 * np.pi
    c1 = 6.28125
    c2 = float(np.float32(np.round((turn - c1) * 2 ** 24) / 2 ** 24))
    c3 = float(np.float32(turn - c1 - c2))
    magic = 12582912.0
    step(dve.tensor_scalar(c.turns[:, :], c.ang[:, :], float(1 / turn), magic, ALU.mult, ALU.add))
    step(dve.tensor_scalar(c.turns[:, :], c.turns[:, :], magic, None, ALU.subtract))
    for part in (c1, c2, c3):
        step(dve.scalar_tensor_tensor(c.ang[:, :], c.turns[:, :], -part, c.ang[:, :], ALU.mult, ALU.add))
    signal(dve, dve.tensor_scalar(c.ang[:, :], c.ang[:, :], 3.1415925, -3.1415925, ALU.min, ALU.max),
           c.s['angles_ready'], 1)
    step(dve.scalar_tensor_tensor(c.angc[:, :], c.ang[:, :], -1.0, c.ang[:, :], ALU.mult, ALU.min))
    signal(dve, dve.tensor_scalar(c.angc[:, :], c.angc[:, :], float(np.pi / 2), None, ALU.add),
           c.s['angles_ready'], 2)
    step(dve.tensor_tensor(c.xor[:, :], c.iotaS[:, :], c.iotaT[:, :], ALU.bitwise_xor))
    step(dve.tensor_tensor(c.less[:, :], c.iotaS[:, :], c.iotaT[:, :], ALU.is_lt))
    for i, b in enumerate(LEVELS):
        step(dve.tensor_scalar(c.bits[:, :], c.xor[:, :], int(np.log2(b)), None, ALU.logical_shift_right))
        step(dve.scalar_tensor_tensor(c.lmask[:, i, :], c.bits[:, :], 1.0, c.less[:, :], ALU.is_equal, ALU.mult))
    step(dve.tensor_tensor(c.lmask[:, len(LEVELS), :], c.iotaS[:, :], c.iotaT[:, :], ALU.is_equal))
    step(dve.tensor_copy(c.slotF2[:, 0:P], c.iotaT[:, :]))
    step(dve.tensor_scalar(c.slotF2[:, P:2 * P], c.slotF2[:, 0:P], float(P), None, ALU.add))
    step(dve.tensor_copy(c.slotP[:, 0:1], c.iotaS[:, 0:1]))
    step(dve.tensor_copy(c.inv1[:, :], c.iota1[:, :]))
    step(dve.reciprocal(c.inv1[:, :], c.inv1[:, :]))


def setup_pe(c, pe):
    pe.wait_ge(c.s['consts_ready'], 1)
    pe.wait_ge(c.s['params_loaded'], 16 * N_PARAM_LOADS)
    for i, (buf, n) in enumerate(((c.prow1, NCOL1), (c.prow2, NCOL2))):
        pe.transpose(c.pb[i][:, 0:n], buf[0:n, :], c.ident[0:n, 0:n]).then_inc(c.s['params_turned'], 1)
    for i in range(2):
        for g in range(4):
            mm = pe.transpose(c.pb[2 + i][:, g * P:g * P + P], c.wsraw[:, 4 * i + g, :], c.ident[:, :])
        mm.then_inc(c.s['ws_turned'], 1)


def att_blocks(a, n):
    return a['heads'] * (a['keys'](n) // P)


def attend_plan(core, a):
    a['calls'] = []
    for n in range(NT):
        nb = -(-att_blocks(a, n) // 4)
        a['calls'].append(dict(a=core.att['a'], e0=core.att['e'], t0=core.att['t'], a0=core.att['ta'],
                               b0=core.att['tb'], nb=nb))
        core.att['a'] += 1
        core.att['e'] += a['heads']
        core.att['t'] += nb
        core.att['ta'] += (nb + 1) // 2
        core.att['tb'] += nb // 2
    return a


def attend_pe(c, pe, a):
    H = a['heads']
    for sem, v in a['ready']:
        pe.wait_ge(c.s[sem], v)
    for n in range(NT):
        call, s = a['calls'][n], a['keys'](n)
        for bank, rows in enumerate(a['banks']):
            for u, i in enumerate(rows):
                mm = pe.matmul(c.pb[bank][:, u * S:u * S + s], a['q'](i, n), a['k'](i, n), start=True, stop=True)
        mm.then_inc(c.s['att_scores'], 1)
        pe.wait_ge(c.s['att_probs'], call['a'] + 1)
        nblk = att_blocks(a, n)
        for b in range(call['nb']):
            if b >= 3:
                x = b - 3
                pe.wait_ge(c.s['att_PT_' + 'ab'[x % 2]], call['ab'[x % 2] + '0'] + x // 2 + 1)
            for blk in range(4 * b, min(4 * b + 4, nblk)):
                ch, i = divmod(blk, H)
                mm = pe.transpose(c.pb[4 + b % 3][:, (blk % 4) * P:(blk % 4) * P + P],
                                  c.L[:, i * S + ch * P:i * S + ch * P + P], c.ident[:, :])
            mm.then_inc(c.s['att_turned'], 1)
        pe.wait_ge(c.s['att_PT_a'], call['a0'] + (call['nb'] + 1) // 2)
        if call['nb'] > 1:
            pe.wait_ge(c.s['att_PT_b'], call['b0'] + call['nb'] // 2)
        if call['a']:
            pe.wait_ge(c.s['att_mixT'], call['a'])
        for out, terms in a['pv'](n):
            for x, (v, blk, m) in enumerate(terms):
                mm = pe.matmul(out, v, c.PT[:, blk * P:(blk + m) * P], start=x == 0, stop=x == len(terms) - 1)
        mm.then_inc(c.s['att_out'], 1)


def attend_dve(c, dve, a):
    H = a['heads']
    L = c.L[:, :].rearrange('p (h s) -> p h s', s=S)
    for n in range(NT):
        call, s = a['calls'][n], a['keys'](n)
        if a['mask'] is not None:
            for sem, v in a['mask_ready'](n):
                dve.wait_ge(c.s[sem], v)
        dve.wait_ge(c.s['att_scores'], call['a'] + 1)
        for bank, rows in enumerate(a['banks']):
            m, i = len(rows), rows[0]
            src = c.pb[bank][:, 0:m * S].rearrange('p (h s) -> p h s', s=S)[:, :, 0:s]
            if a['mask'] is None:
                c.vstep(dve.tensor_copy(L[:, i:i + m, 0:s], src))
            else:
                mask = a['mask'](n).unsqueeze(1).broadcast_to([P, m, s])
                c.vstep(dve.tensor_tensor(L[:, i:i + m, 0:s], src, mask, ALU.add))
        c.vstep(dve.tensor_reduce(c.mx[:, 0:H], L[:, 0:H, 0:s], AX, ALU.max))
        dve.tensor_scalar(c.nmx[:, 0:H], c.mx[:, 0:H], -a['scale'], None, ALU.mult)\
           .then_inc(c.s['att_max'], 1)
        dve.wait_ge(c.s['att_exp'], call['e0'] + H)
        c.vstep(dve.reciprocal(c.rsum[:, 0:H], c.esum[:, 0:H]))
        dve.tensor_tensor(L[:, 0:H, 0:s], L[:, 0:H, 0:s], c.rsum[:, 0:H].unsqueeze(2).broadcast_to([P, H, s]),
                          ALU.mult).then_inc(c.s['att_probs'], 1)
        nblk = att_blocks(a, n)
        for b in range(1, call['nb'], 2):
            dve.wait_ge(c.s['att_turned'], call['t0'] + b + 1)
            w = min(4, nblk - 4 * b) * P
            dve.tensor_copy(c.PT[:, 4 * b * P:4 * b * P + w], c.pb[4 + b % 3][:, 0:w]).then_inc(c.s['att_PT_b'], 1)
        dve.wait_ge(c.s['att_mix_hi'], call['a'] + 1)
        lo, hi = a['out']
        dve.tensor_tensor(r32(c.hL[:, lo:hi, n * P:n * P + P]), c.pb[7][:, 0:(hi - lo) * P]
                          .rearrange('p (m t) -> p m t', t=P), high(c.hT[:, lo:hi, n * P:n * P + P]), ALU.subtract)\
           .then_inc(c.s['att_mixT'], 1)


def attend_act(c, act, a):
    H = a['heads']
    for n in range(NT):
        call, s = a['calls'][n], a['keys'](n)
        act.wait_ge(c.s['att_max'], call['a'] + 1)
        for i in range(H):
            row = c.L[:, i * S:i * S + s]
            act.activation(row, row, ACT.Exp, bias=c.nmx[:, i:i + 1], scale=a['scale'],
                           accum_out=c.esum[:, i:i + 1]).then_inc(c.s['att_exp'], 1)
        nblk = att_blocks(a, n)
        for b in range(0, call['nb'], 2):
            act.wait_ge(c.s['att_turned'], call['t0'] + b + 1)
            w = min(4, nblk - 4 * b) * P
            act.activation(c.PT[:, 4 * b * P:4 * b * P + w], c.pb[4 + b % 3][:, 0:w], ACT.Copy)\
               .then_inc(c.s['att_PT_a'], 1)
        act.wait_ge(c.s['att_out'], call['a'] + 1)
        lo, hi = a['out']
        act.activation(r32(c.hT[:, lo:hi, n * P:n * P + P]), c.pb[7][:, 0:(hi - lo) * P]
                       .rearrange('p (m t) -> p m t', t=P), ACT.Copy).then_inc(c.s['att_mix_hi'], 1)


def rotate(c, dve, x, out, heads, half, cos, sin, s1, s2):
    x4 = x.rearrange('p h (a j) -> p h a j', a=2)
    o4 = out.rearrange('p h (a j) -> p h a j', a=2)
    v1 = s1.rearrange('p (h a j) -> p h a j', a=2, j=half)
    v2 = s2.rearrange('p (h a j) -> p h a j', a=2, j=half)
    full = [P, heads, 2, half]
    c.vstep(dve.tensor_tensor(v1, x4, cos.unsqueeze(1).unsqueeze(1).broadcast_to(full), ALU.mult))
    c.vstep(dve.tensor_tensor(v2, x4, sin.unsqueeze(1).unsqueeze(1).broadcast_to(full), ALU.mult))
    c.vstep(dve.tensor_tensor(o4[:, :, 0, :], v1[:, :, 0, :], v2[:, :, 1, :], ALU.subtract))
    c.vstep(dve.tensor_tensor(o4[:, :, 1, :], v1[:, :, 1, :], v2[:, :, 0, :], ALU.add))


def dsa_stage(core, k, evacuated):
    c = core
    order = [0, 2, 4, 1, 3, 5]
    a = dict(heads=A_HEADS, scale=HD ** -0.5, banks=[[0, 1], [2], [3, 4], [5]],
             keys=lambda n: P * (n + 1),
             q=lambda i, n: c.rT[HD * (order[i] % 2):HD * (order[i] % 2) + HD, order[i] // 2, n * P:n * P + P],
             k=lambda i, n: c.rT[HD * (order[i] % 2):HD * (order[i] % 2) + HD, 3, 0:P * (n + 1)],
             mask=lambda n: c.sel[:, n, 0:P * (n + 1)],
             mask_ready=lambda n: [('dsa_bias', 2 * k + n + 1)],
             pv=lambda n: [(c.pb[7][HD * g:HD * g + HD, 0:3 * P],
                            [(c.z[:, ch, Z_AV:Z_AV + HD], ch * A_HEADS + 3 * g, 3) for ch in range(n + 1)])
                           for g in range(2)],
             out=(0, 3), ready=[('dsa_rel', 2 * k + 2)])
    return dict(kind='dsa', k=k, evacuated=evacuated, att=attend_plan(core, a))


def dsa_dve(c, dve, st):
    k = st['k']
    for sem, v in st['evacuated']:
        dve.wait_ge(c.s[sem], v)
    if k == 0:
        dve.wait_ge(c.s['rope_ready'], 2)
    rot = c.xn[:, :, :].rearrange('p n d -> p (n d)')[:, 0:NT * 14 * HD].rearrange('p (n h d) -> p n h d', n=NT, h=14)
    for n in range(NT):
        cos, sin = c.cos[:, 32 * n:32 * n + 32], c.sin[:, 32 * n:32 * n + 32]
        for at, slot, heads in ((Z_AQ, 0, 7), (Z_IQ, 8, 5)):
            w = heads * HD
            rotate(c, dve, c.z[:, n, at:at + w].rearrange('p (h d) -> p h d', d=HD), rot[:, n, slot:slot + heads, :],
                   heads, HD // 2, cos, sin, c.L[:, 0:w], c.L[:, 512:512 + w])
        c.vstep(dve.tensor_copy(rot[:, n, 7, :], rot[:, n, 6, :]))
        dve.tensor_copy(rot[:, n, 13, :], rot[:, n, 12, :]).then_inc(c.s['dsa_rot'], 1)
        c.vstep(dve.tensor_scalar(c.iw[:, n, :], c.z[:, n, Z_IW:Z_IW + IDX_HEADS], IDX_HEADS ** -0.5, None, ALU.mult))
    for n in range(NT):
        dve.wait_ge(c.s['dsa_turned'], 4 * k + 2 * n + 2)
        dve.tensor_copy(c.rT[:, 4:7, n * P:n * P + P], c.pb[2 * n + 1][:, 0:3 * P]
                        .rearrange('p (m t) -> p m t', t=P)).then_inc(c.s['dsa_rT_b'], 1)
    for n in range(NT):
        s = P * (n + 1)
        dve.wait_ge(c.s['dsa_rel'], 2 * k + n + 1)
        score = c.score[:, n, 0:s]
        rel = c.L[:, n * 1024:n * 1024 + 1024].rearrange('p (h s) -> p h s', s=S)
        for h in range(IDX_HEADS):
            r = rel[:, 2 * (h % 2) + h // 2, 0:s]
            if h == 0:
                c.vstep(dve.tensor_scalar(score, r, c.iw[:, n, 0:1], None, ALU.mult))
            else:
                ins = dve.scalar_tensor_tensor(score, r, c.iw[:, n, h:h + 1], score, ALU.mult, ALU.add)
                if h < IDX_HEADS - 1:
                    c.vstep(ins)
        ins.then_inc(c.s['dsa_score'], 1)
    for n in range(NT):
        s = P * (n + 1)
        score, work, top = c.score[:, n, 0:s], c.work[:, 0:s], c.top8[:, :]
        dve.wait_ge(c.s['dsa_causal'], 2 * k + n + 1)
        src = score
        for r in range(TOPK // 8):
            c.vstep(dve.max(top, src))
            if r < TOPK // 8 - 1:
                c.vstep(dve.match_replace(work, top, src, TAKEN))
                src = work
        thr = c.top8[:, 7:8]
        sel, eq, pre = c.sel[:, n, 0:s], c.eq[:, 0:s], c.work[:, 0:s]
        c.vstep(dve.tensor_scalar(sel, score, thr, None, ALU.is_gt, ALU.add, accum_out=c.cnt[:, 0:1]))
        c.vstep(dve.tensor_scalar(c.cnt[:, 1:2], c.cnt[:, 0:1], -1.0, float(TOPK), ALU.mult, ALU.add))
        c.vstep(dve.tensor_scalar(eq, score, thr, None, ALU.is_equal))
        c.vstep(dve.tensor_tensor_scan(pre, c.ones[:, 0:s], eq, 0.0, ALU.mult, ALU.add))
        c.vstep(dve.scalar_tensor_tensor(eq, pre, c.cnt[:, 1:2], eq, ALU.is_le, ALU.mult))
        c.vstep(dve.tensor_tensor(sel, sel, eq, ALU.add))
        dve.tensor_scalar(sel, sel, 1.0, -NEG, ALU.subtract, ALU.mult).then_inc(c.s['dsa_sel'], 1)
    ada_cols_dve(c, dve, st['ada'])
    attend_dve(c, dve, st['att'])


def dsa_pool(c, pool, st):
    k = st['k']
    for buf, sem_in, sem_out, fill in ((c.score, 'dsa_score', 'dsa_causal', LOWEST), (c.sel, 'dsa_sel', 'dsa_bias', NEG)):
        for n in range(NT):
            pool.wait_ge(c.s[sem_in], 2 * k + n + 1)
            v = buf[:, n, 0:P * (n + 1)]
            pool.affine_select(out=v, in_=v, compare_op=ALU.is_ge, fill=fill, base=n * P,
                               pattern=[[-1, P * (n + 1)]], channel_multiplier=1).then_inc(c.s[sem_out], 1)


def dsa_pe(c, pe, st):
    k = st['k']
    rot = c.xn[:, :, :].rearrange('p n d -> p (n d)')
    for sem, v in st['evacuated']:
        pe.wait_ge(c.s[sem], v)
    ada_cols_pe(c, pe, st['ada'], 0, ADA_FIRST)
    for n in range(NT):
        pe.wait_ge(c.s['dsa_rot'], 2 * k + n + 1)
        for m in range(7):
            mm = pe.transpose(c.pb[2 * n + m // 4][:, (m % 4) * P:(m % 4) * P + P],
                              rot[:, (n * 7 + m) * P:(n * 7 + m) * P + P], c.ident[:, :])
            if m in (3, 6):
                mm.then_inc(c.s['dsa_turned'], 1)
    pe.wait_ge(c.s['dsa_rT_a'], 2 * k + 2)
    pe.wait_ge(c.s['dsa_rT_b'], 2 * k + 2)
    for n in range(NT):
        s = P * (n + 1)
        for g in range(2):
            for u in range(2):
                mm = pe.matmul(c.pb[2 * n + g][:, u * S:u * S + s], c.rT[HD * g:HD * g + HD, 4 + u, n * P:n * P + P],
                               c.rT[HD * g:HD * g + HD, 6, 0:s], start=True, stop=True)
        mm.then_inc(c.s['dsa_index'], 1)
    ada_cols_pe(c, pe, st['ada'], ADA_FIRST, len(st['ada']['cols']))
    pe.wait_ge(c.s['ada_cols'], 2 * k + 2)
    attend_pe(c, pe, st['att'])


def dsa_act(c, act, st):
    k = st['k']
    for n in range(NT):
        act.wait_ge(c.s['dsa_turned'], 4 * k + 2 * n + 1)
        act.activation(c.rT[:, 0:4, n * P:n * P + P], c.pb[2 * n][:, :].rearrange('p (m t) -> p m t', t=P),
                       ACT.Copy).then_inc(c.s['dsa_rT_a'], 1)
    for n in range(NT):
        s = P * (n + 1)
        act.wait_ge(c.s['dsa_index'], 2 * k + n + 1)
        rel = c.L[:, n * 1024:n * 1024 + 1024].rearrange('p (h s) -> p h s', s=S)
        for g in range(2):
            ins = act.activation(rel[:, 2 * g:2 * g + 2, 0:s],
                                 c.pb[2 * n + g][:, :].rearrange('p (u s) -> p u s', s=S)[:, :, 0:s],
                                 ACT.Relu, scale=HD ** -0.5)
        ins.then_inc(c.s['dsa_rel'], 1)
    attend_act(c, act, st['att'])


HG_LEVELS = ['cross'] + list(LEVELS) + ['diag']
HG_GROUPS = 1 + 2 * (len(LEVELS) + 1)
HG_EXPS = len(LEVELS) + 1


def hg_groups():
    return [(lv, n) for lv in range(len(HG_LEVELS)) for n in ((1,) if lv == 0 else (0, 1))]


def hg_buffers(c):
    w = PAIRS * S
    zT = c.zT[:, :, :].rearrange('p m t -> p (m t)')
    PT = c.PT[:, :]
    b = Core()
    b.q, b.f = zT[:, 0:w], zT[:, w:2 * w]
    b.D = [zT[:, 2 * w:3 * w], zT[:, 3 * w:4 * w]]
    b.k, b.b = zT[:, 4 * w:5 * w], PT[:, 0:w]
    b.QK = [PT[:, w:2 * w], c.L[:, 1024:1024 + w]]
    b.cross = c.L[:, 0:w]
    b.o = c.xn[:, 0, 0:w]
    b.sq = c.xn[:, 1, 0:w]
    return b


def by_block(ap, B):
    return ap.rearrange('p (b t) -> p b t', t=2 * B)


def hgrn_dve(c, dve, st):
    k = st['k']
    h = hg_buffers(c)
    for sem, v in st['evacuated']:
        dve.wait_ge(c.s[sem], v)

    def to_act(ins, sem='hg_gate'):
        ins.then_inc(c.s[sem], 1)
    to_act(magnitude(dve, h.D[0], h.f))
    if k:
        lb = COL2['hgrn_lb_logits']
        c.vstep(dve.tensor_tensor(c.lbd[:, 0:3], c.col2[:, lb:lb + 3], c.col2[:, lb + 3:lb + 6], ALU.subtract))
        c.vstep(dve.tensor_scalar(c.lbd[:, 3:6], c.lbd[:, 0:3], -1.0, None, ALU.mult))
        to_act(magnitude(dve, c.lbe[:, :], c.lbd[:, :]))
    dve.wait_ge(c.s['hg_log'], 1 if k == 0 else 4)
    c.vstep(dve.scalar_tensor_tensor(h.b, h.f, 0.0, h.D[0], ALU.min, ALU.subtract))
    if k:
        c.vstep(dve.scalar_tensor_tensor(c.lbl[:, :], c.lbd[:, :], 0.0, c.lbe[:, :], ALU.min, ALU.subtract))
    to_act(dve.tensor_tensor(h.k, h.b, h.f, ALU.subtract))
    lf = h.b
    if k:
        for p in range(PAIRS):
            v = slice(p * S, p * S + S)
            c.vstep(dve.tensor_scalar(h.D[1][:, v], h.b[:, v], c.lbd[:, p:p + 1], None, ALU.add))
        to_act(magnitude(dve, h.D[1], h.D[1]))
        for p in range(PAIRS):
            v = slice(p * S, p * S + S)
            c.vstep(dve.tensor_scalar(h.b[:, v], h.b[:, v], c.lbl[:, p:p + 1], c.lbl[:, 3 + p:4 + p], ALU.add, ALU.max))
        dve.wait_ge(c.s['hg_log'], 6)
        c.vstep(dve.tensor_tensor(h.b, h.b, h.D[1], ALU.add))
    c.vstep(dve.tensor_copy(h.D[0], lf))
    for p in range(PAIRS):
        v = slice(p * S, p * S + S)
        c.vstep(dve.tensor_tensor_scan(h.b[:, v], c.resume[:, :], h.D[0][:, v], 0.0, ALU.mult, ALU.add))
    dve.wait_ge(c.s['hg_log'], 2 if k == 0 else 5)
    b4 = h.b.rearrange('p (a c t) -> p a c t', a=PAIRS, c=4)
    n_exp = HG_EXPS * k

    def diff(lv):
        Dn = h.D[lv % 2]
        B = HG_LEVELS[lv]
        if B == 'cross':
            d4 = Dn.rearrange('p (a c t) -> p a c t', a=PAIRS, c=4)
            half = [P, PAIRS, 2, CHUNK]
            last = b4[:, :, :, CHUNK - 1:CHUNK]
            c.vstep(dve.tensor_tensor(d4[:, :, 0:2, :], b4[:, :, 0:2, :], last[:, :, 0:2, :].broadcast_to(half), ALU.subtract))
            one = [P, PAIRS, CHUNK]
            c.vstep(dve.tensor_tensor(d4[:, :, 0, :], d4[:, :, 0, :], last[:, :, 1, :].broadcast_to(one), ALU.subtract))
            c.vstep(dve.tensor_copy(d4[:, :, 2, :], b4[:, :, 2, :]))
            ins = dve.tensor_tensor(d4[:, :, 3, :], b4[:, :, 3, :], last[:, :, 2, :].broadcast_to(one), ALU.add)
        elif B == CHUNK:
            dv, bv = by_block(Dn, B), by_block(h.b, B)
            nb = S * PAIRS // (2 * B)
            c.vstep(dve.tensor_tensor(dv[:, :, 0:B], bv[:, :, 0:B], bv[:, :, B - 1:B].broadcast_to([P, nb, B]), ALU.subtract))
            ins = dve.tensor_copy(dv[:, :, B:2 * B], bv[:, :, B:2 * B])
        else:
            dv, bv = by_block(Dn, B), by_block(h.b, B)
            nb = S * PAIRS // (2 * B)
            ins = dve.tensor_tensor(dv, bv, bv[:, :, B - 1:B].broadcast_to([P, nb, 2 * B]), ALU.subtract)
        ins.then_inc(c.s['hg_diff'], 1)

    def queries_keys(lv):
        B = P if HG_LEVELS[lv] == 'cross' else HG_LEVELS[lv]
        dve.wait_ge(c.s['hg_exp'], n_exp + lv + 1)
        if lv >= 2:
            dve.wait_ge(c.s['hg_pairs'], HG_GROUPS * k + (1 + 2 * (lv - 2)))
        o, e = by_block(h.QK[lv % 2], B), by_block(h.D[lv % 2], B)
        c.vstep(dve.tensor_tensor(o[:, :, 0:B], e[:, :, 0:B], by_block(h.k, B)[:, :, 0:B], ALU.mult))
        dve.tensor_tensor(o[:, :, B:2 * B], e[:, :, B:2 * B], by_block(h.q, B)[:, :, B:2 * B], ALU.mult)\
           .then_inc(c.s['hg_QK'], 1)

    groups = hg_groups()

    def take(lv):
        for g, (glv, n) in enumerate(groups):
            if glv != lv:
                continue
            dve.wait_ge(c.s['hg_pairs'], HG_GROUPS * k + g + 1)
            for par in range(2):
                src = c.pb[2 * (g % 4) + par][:, 0:3 * P].rearrange('p (m t) -> p m t', t=P)
                if lv == 0:
                    dst = h.cross[:, par * 3 * P:(par + 1) * 3 * P].rearrange('p (m t) -> p m t', t=P)
                    ins = dve.tensor_copy(dst, src)
                else:
                    mask = c.lmask[:, lv - 1, :].unsqueeze(1).broadcast_to([P, 3, P])
                    ins = dve.copy_predicated(c.AT[:, n, 3 * par:3 * par + 3, :], mask, src)
            signal(dve, ins, c.s['hg_taken'], HG_GROUPS * k + g + 1)

    diff(0)
    for lv in range(HG_EXPS):
        queries_keys(lv)
        if lv == 0:
            ada_rows_dve(c, dve, st['ada'])
        if lv + 1 < HG_EXPS:
            diff(lv + 1)
        if lv:
            take(lv - 1)
    take(HG_EXPS - 1)
    take(HG_EXPS)
    dve.wait_ge(c.s['hg_square'], 2 * (k + 1))
    dve.tensor_reduce(c.hss[:, :], h.sq.rearrange('p (m v) -> p m v', v=HD), AX, ALU.add).then_inc(c.s['hg_ss'], 1)
    for n in range(NT):
        dve.wait_ge(c.s['hg_silu'], 2 * k + n + 1)
        g = c.z[:, n, Z_BG:Z_BG + 384].rearrange('p (m v) -> p m v', v=HD)
        c.vstep(dve.tensor_tensor(g, g, c.onorm[:, k, :].unsqueeze(1).broadcast_to([P, B_HEADS, HD]), ALU.mult))
    dve.wait_ge(c.s['hg_rstd'], k + 1)
    o3 = h.o.rearrange('p (m v) -> p m v', v=HD)
    c.vstep(dve.tensor_tensor(o3, o3, c.hrstd[:, :].unsqueeze(2).broadcast_to([P, NT * B_HEADS, HD]), ALU.mult))
    for n in range(NT):
        dve.tensor_tensor(c.mix[:, n, 384:768], h.o[:, n * 384:n * 384 + 384], c.z[:, n, Z_BG:Z_BG + 384], ALU.mult)\
           .then_inc(c.s['mix_ready'], 1)


def hgrn_act(c, act, st):
    k = st['k']
    h = hg_buffers(c)

    def log_one_plus(buf, n_in, n_out):
        act.wait_ge(c.s['hg_gate'], n_in)
        signal(act, act.activation(buf, buf, ACT.Exp, scale=-1.0), c.s['hg_log_e'], c.n_log_e + 1)
        c.n_log_e += 1
        act.activation(buf, buf, ACT.Ln, bias=1.0).then_inc(c.s['hg_log'], 1)
    g0, l0 = (0, 0) if k == 0 else (2, 2)
    log_one_plus(h.D[0], g0 + 1, l0 + 1)
    if k:
        log_one_plus(c.lbe[:, :], g0 + 2, l0 + 2)
        act.wait_ge(c.s['hg_gate'], g0 + 3)
        for p in range(PAIRS):
            v = slice(p * S, p * S + S)
            ins = act.activation(h.k[:, v], h.k[:, v], ACT.Exp, bias=c.lbl[:, p:p + 1])
        ins.then_inc(c.s['hg_log'], 1)
        log_one_plus(h.D[1], g0 + 4, l0 + 4)
    else:
        act.wait_ge(c.s['hg_gate'], 2)
        act.activation(h.k, h.k, ACT.Exp).then_inc(c.s['hg_log'], 1)
    for lv in range(HG_EXPS):
        B = P if HG_LEVELS[lv] == 'cross' else HG_LEVELS[lv]
        act.wait_ge(c.s['hg_diff'], HG_EXPS * k + lv + 1)
        v = by_block(h.D[lv % 2], B)
        act.activation(v[:, :, 0:B], v[:, :, 0:B], ACT.Exp, scale=-1.0)
        act.activation(v[:, :, B:2 * B], v[:, :, B:2 * B], ACT.Exp).then_inc(c.s['hg_exp'], 1)
    for n in range(NT):
        act.wait_ge(c.s['hg_out'], 2 * k + n + 1)
        o = h.o[:, n * 384:n * 384 + 384]
        signal(act, act.activation(o, c.pb[n][:, 0:384], ACT.Copy), c.s['hg_o'], 2 * k + n + 1)
        act.activation(h.sq[:, n * 384:n * 384 + 384], o, ACT.Square).then_inc(c.s['hg_square'], 1)


def hgrn_pool(c, pool, st):
    pool.wait_ge(c.s['hg_ss'], st['k'] + 1)
    c.pstep(pool.tensor_scalar(c.hms[:, :], c.hss[:, :], 1.0 / HD, EPS, ALU.mult, ALU.add))
    pool.tensor_tensor(c.hrstd[:, :], c.hms[:, :], c.neghalf[:, 0:NT * B_HEADS], ALU.pow).then_inc(c.s['hg_rstd'], 1)


def hgrn_pe(c, pe, st):
    k = st['k']
    h = hg_buffers(c)
    for g, (lv, n) in enumerate(hg_groups()):
        if lv < HG_EXPS:
            pe.wait_ge(c.s['hg_QK'], HG_EXPS * k + lv + 1)
            keys = queries = h.QK[lv % 2]
        else:
            keys, queries = h.k, h.q
        if g >= 4:
            pe.wait_ge(c.s['hg_taken'], HG_GROUPS * k + g - 3)
        elif g == 2:
            pe.wait_ge(c.s['ada_rows'], 4 * (k + 1))
        m = 0 if lv == 0 else n
        for par in range(2):
            half = slice(HD * par, HD * par + HD)
            for p in range(PAIRS):
                mm = pe.matmul(c.pb[2 * (g % 4) + par][:, p * P:p * P + P],
                               keys[half, p * S + m * P:p * S + m * P + P],
                               queries[half, p * S + n * P:p * S + n * P + P], start=True, stop=True)
        mm.then_inc(c.s['hg_pairs'], 1)
    pe.wait_ge(c.s['hg_taken'], HG_GROUPS * (k + 1))
    for n in range(NT):
        for hd in range(B_HEADS):
            i = 3 * (hd % 2) + hd // 2
            out = c.pb[n][:, hd * HD:hd * HD + HD]
            v = slice(Z_BI + hd * HD, Z_BI + hd * HD + HD)
            mm = pe.matmul(out, c.AT[:, n, i, :], c.z[:, n, v], start=True, stop=n == 0)
            if n:
                mm = pe.matmul(out, h.cross[:, i * P:i * P + P], c.z[:, 0, v], start=False, stop=True)
        mm.then_inc(c.s['hg_out'], 1)


def gmlp_act(c, act, st):
    k = st['k']
    for n in range(NT):
        uv = c.z[:, n, Z_UV:Z_UV + 512]
        act.activation(uv, uv, ACT.Gelu).then_inc(c.s['gm_gelu'], 1)
    for n in range(NT):
        act.wait_ge(c.s['gm_centred'], 2 * k + n + 1)
        act.activation(c.L[:, 0:256], c.z[:, n, Z_UV + 256:Z_UV + 512], ACT.Square,
                       accum_out=c.gss[:, n:n + 1]).then_inc(c.s['gm_ss'], 1)
        act.wait_ge(c.s['gm_ss'], 2 * k + n + 1)
    for n in range(NT):
        g = c.z[:, n, Z_BG:Z_BG + 384]
        act.activation(g, g, ACT.Silu).then_inc(c.s['hg_silu'], 1)


def gmlp_pool(c, pool, st):
    k = st['k']
    pool.wait_ge(c.s['gm_ss'], 2 * (k + 1))
    c.pstep(pool.tensor_scalar(c.gms[:, :], c.gss[:, :], 1.0 / 256, EPS, ALU.mult, ALU.add))
    pool.tensor_tensor(c.grstd[:, :], c.gms[:, :], c.neghalf[:, 0:NT], ALU.pow).then_inc(c.s['gm_rstd'], 1)


def gmlp_dve(c, dve, st):
    k = st['k']
    for sem, v in st['evacuated']:
        dve.wait_ge(c.s[sem], v)
    for n in range(NT):
        v = c.z[:, n, Z_UV + 256:Z_UV + 512]
        dve.wait_ge(c.s['gm_gelu'], 2 * k + n + 1)
        c.vstep(dve.tensor_reduce(c.gsum[:, n:n + 1], v, AX, ALU.add))
        c.vstep(dve.tensor_scalar(c.gsum[:, n:n + 1], c.gsum[:, n:n + 1], 1.0 / 256, None, ALU.mult))
        signal(dve, dve.tensor_scalar(v, v, c.gsum[:, n:n + 1], None, ALU.subtract), c.s['gm_centred'], 2 * k + n + 1)
    dve.wait_ge(c.s['gm_rstd'], k + 1)
    for n in range(NT):
        v = c.z[:, n, Z_UV + 256:Z_UV + 512]
        c.vstep(dve.scalar_tensor_tensor(v, v, c.grstd[:, n:n + 1], c.vng[:, k, :], ALU.mult, ALU.mult))
        dve.tensor_tensor(v, v, c.vnb[:, k, :], ALU.add).then_inc(c.s['gm_v'], 1)
    for n in range(NT):
        dve.wait_ge(c.s['gm_mixed'], 2 * k + n + 1)
        for g in range(4):
            bs = COL2['gmlp_b_s'] + 4 * k + g
            u = c.z[:, n, Z_UV + 64 * g:Z_UV + 64 * g + 64]
            ins = dve.scalar_tensor_tensor(c.mix[:, n, 768 + 64 * g:832 + 64 * g], c.pb[2 + n][:, 64 * g:64 * g + 64],
                                           c.col2[:, bs:bs + 1], u, ALU.add, ALU.mult)
        ins.then_inc(c.s['mix_ready'], 1)


def gmlp_pe(c, pe, st):
    k = st['k']
    pe.wait_ge(c.s['att_mixT'], 2 * (k + 1))
    ada_rows_pe(c, pe, st['ada'], 0, 2)
    for n in range(NT):
        pe.wait_ge(c.s['gm_v'], 2 * k + n + 1)
        for g in range(4):
            at = Z_UV + 256 + 64 * g
            mm = pe.matmul(c.pb[2 + n][:, 64 * g:64 * g + 64], c.wsT[:, 4 * k + g, :], c.z[:, n, at:at + 64],
                           start=True, stop=True)
        mm.then_inc(c.s['gm_mixed'], 1)
    ada_rows_pe(c, pe, st['ada'], 2, 4)


def turn_stage(core, k, chunks, ready):
    st = dict(kind='turn', k=k, ready=ready, banks=[chunks[i:i + 2] for i in range(0, len(chunks), 2)],
              b0=core.turn['b'])
    core.turn['b'] += len(st['banks'])
    return st


def turn_pe(c, pe, st):
    for sem, v in st['ready']:
        pe.wait_ge(c.s[sem], v)
    for b, chunks in enumerate(st['banks']):
        for i, ch in enumerate(chunks):
            for n in range(NT):
                mm = pe.transpose(c.pb[b][:, i * S + n * P:i * S + n * P + P], c.mix[:, n, ch * P:ch * P + P], c.ident[:, :])
        mm.then_inc(c.s['turned'], 1)


def turn_act(c, act, st):
    for b, chunks in enumerate(st['banks']):
        m = len(chunks)
        act.wait_ge(c.s['turned'], st['b0'] + b + 1)
        act.activation(r32(c.hT[:, chunks[0]:chunks[0] + m, :]), c.pb[b][:, 0:m * S].rearrange('p (m t) -> p m t', t=S),
                       ACT.Copy).then_inc(c.s['turn_hi'], 1)


def turn_dve(c, dve, st):
    for b, chunks in enumerate(st['banks']):
        m = len(chunks)
        dve.wait_ge(c.s['turn_hi'], st['b0'] + b + 1)
        part = (slice(None), slice(chunks[0], chunks[0] + m))
        dve.tensor_tensor(r32(c.hL[part]), c.pb[b][:, 0:m * S].rearrange('p (m t) -> p m t', t=S), high(c.hT[part]),
                          ALU.subtract).then_inc(c.s['turn_lo'], 1)


def turned_events(st):
    return [('turn_lo', st['b0'] + len(st['banks']))]


POOL_WINDOWS = (2, 4, 8, 16)


def even_dve(c, dve, st):
    for sem, v in st['evacuated']:
        dve.wait_ge(c.s[sem], v)
    flat = c.zT[:, :, :].rearrange('p m t -> p (m t)')
    gb, gc, xa = flat[:, 0:4 * S], flat[:, 4 * S:8 * S], flat[:, 8 * S:12 * S]
    c.vstep(dve.tensor_tensor(gc, gc, xa, ALU.mult))
    for m in range(4):
        u, y = c.zT[:, 4 + m, :], c.zT[:, 8 + m, :]
        w = [c.col1[:, COL1['ev_conv_w_2'] + 4 * j + m:COL1['ev_conv_w_2'] + 4 * j + m + 1] for j in range(3)]
        c.vstep(dve.tensor_scalar(y, u, w[2], None, ALU.mult))
        for lag in (1, 2):
            c.vstep(dve.scalar_tensor_tensor(y[:, lag:], u[:, 0:S - lag], w[2 - lag], y[:, lag:], ALU.mult, ALU.add))
    hi, lo = (b[:, 0:4, :].rearrange('p m t -> p (m t)') for b in (c.hT, c.hL))
    c.vstep(dve.tensor_tensor(lo, gb, xa, ALU.mult))
    c.vstep(dve.tensor_copy(r32(hi), lo))
    c.vstep(dve.tensor_tensor(r32(lo), lo, high(hi), ALU.subtract))
    for g, w in enumerate(POOL_WINDOWS):
        x, cs, d = c.zT[:, 12 + g, :], c.work[:, 0:S], c.L[:, g * S:g * S + S]
        c.vstep(dve.tensor_tensor_scan(cs, c.ones[:, 0:S], x, 0.0, ALU.mult, ALU.add))
        c.vstep(dve.tensor_tensor(d[:, w:], cs[:, w:], cs[:, 0:S - w], ALU.subtract))
        c.vstep(dve.tensor_tensor(d[:, 0:w], cs[:, 0:w], c.inv1[:, 0:w], ALU.mult))
        c.vstep(dve.tensor_tensor(d[:, 0:w], d[:, 0:w], x[:, 0:w], ALU.subtract))
        dve.scalar_tensor_tensor(d[:, w:], d[:, w:], 1.0 / w, x[:, w:], ALU.mult, ALU.subtract)\
           .then_inc(c.s['ev_pooled'], 1)
    for b in range(2):
        dve.wait_ge(c.s['ev_product'], b + 1)
        for g in (2 * b, 2 * b + 1):
            sc = COL1['ev_pool_scale_2'] + g
            c.vstep(dve.tensor_scalar(c.hL[:, 4 + g, :], c.pb[b][:, (g % 2) * S:(g % 2) * S + S], c.col1[:, sc:sc + 1],
                                      None, ALU.mult))
        hi, lo = (x[:, 4 + 2 * b:6 + 2 * b, :] for x in (c.hT, c.hL))
        c.vstep(dve.tensor_copy(r32(hi), lo))
        dve.tensor_tensor(r32(lo), lo, high(hi), ALU.subtract).then_inc(c.s['ev_mixT'], 1)


def even_pe(c, pe, st):
    for g in range(4):
        pe.wait_ge(c.s['ev_pooled'], g + 1)
        mm = pe.matmul(c.pb[g // 2][:, (g % 2) * S:(g % 2) * S + S], c.wpool[:, g, :], c.L[:, g * S:g * S + S],
                       start=True, stop=True)
        if g % 2:
            mm.then_inc(c.s['ev_product'], 1)


def xa_stage(core, ready):
    c = core
    a = dict(heads=XA_HEADS, scale=XA_D ** -0.5, banks=[[0, 1], [2, 3]], keys=lambda n: S,
             q=lambda i, n: c.zT[:, i, n * P:n * P + P], k=lambda i, n: c.zT[:, 8 + i, :], mask=None,
             pv=lambda n: [(c.pb[7][:, h * P:h * P + P],
                            [(c.z[:, ch, h * P:h * P + P], ch * XA_HEADS + h, 1) for ch in range(NT)])
                           for h in range(XA_HEADS)],
             out=(0, 4), ready=ready)
    return dict(kind='xa', att=attend_plan(core, a))


def xa_pe(c, pe, st):
    attend_pe(c, pe, st['att'])


def xa_act(c, act, st):
    attend_act(c, act, st['att'])


def xa_dve(c, dve, st):
    attend_dve(c, dve, st['att'])


OD_V, OD_O, OD_G, OD_CQ, OD_CKV, OD_KR, OD_Q = 0, 512, 1024, 1032, 1416, 1672, 1704
ML_TILES = ((0, 0), (0, 1), (1, 1))


ML_TENSOR = in_order(rows=1, scores=3, turned=1, num=2)
ML_VECTOR = in_order(gates=2, abs=1, scans=1, cols=1, exponent=3, sw=3, h=2, ms=1)
ML_SCALAR = in_order(log=2, weight=3, em=1, sigmoid=2, square=2)


def mlstm_dve(c, dve, st):
    for sem, v in st['evacuated']:
        dve.wait_ge(c.s[sem], v)
    H = ML_HEADS
    for n in range(NT):
        g = c.z[:, n, OD_G:OD_G + 8]
        dve.tensor_tensor(g, g, c.gbias[:, :], ALU.add).then_inc(c.s['ml_vector'], 1)
    dve.wait_ge(c.s['ml_tensor'], ML_TENSOR['rows'] + 1)
    r = c.grows
    c.vstep(dve.tensor_copy(r[:, 0:2, :], c.pb[0][0:H, 0:512].rearrange('p (a t) -> p a t', a=2)))
    magnitude(dve, r[:, 2, :], r[:, 1, :]).then_inc(c.s['ml_vector'], 1)
    dve.wait_ge(c.s['ml_scalar'], ML_SCALAR['log'] + 2)
    c.vstep(dve.scalar_tensor_tensor(r[:, 1, :], r[:, 1, :], 0.0, r[:, 2, :], ALU.min, ALU.subtract))
    c.vstep(dve.tensor_tensor_scan(r[:, 3, :], c.ones[0:H, 0:S], r[:, 1, :], 0.0, ALU.mult, ALU.add))
    c.vstep(dve.tensor_tensor(r[:, 4, :], r[:, 0, :], r[:, 3, :], ALU.subtract))
    c.vstep(dve.tensor_tensor_scan(r[:, 5, :], r[:, 4, :], r[:, 4, :], 0.0, ALU.max, ALU.max))
    c.vstep(dve.tensor_tensor(r[:, 6, :], r[:, 3, :], r[:, 5, :], ALU.add))
    dve.tensor_scalar(r[:, 5, :], r[:, 5, :], -1.0, None, ALU.mult).then_inc(c.s['ml_vector'], 1)
    dve.wait_ge(c.s['ml_tensor'], ML_TENSOR['turned'] + 1)
    signal(dve, dve.tensor_copy(c.gcols[:, :], c.pb[1][:, 0:4 * H]), c.s['ml_vector'], ML_VECTOR['cols'] + 1)
    w = c.PT[:, 0:3 * H * P].rearrange('p (x h t) -> p x h t', x=3, h=H)
    for x, (m, n) in enumerate(ML_TILES):
        for h in range(H):
            row = c.pb[2 + h // 2][:, (h % 2) * S + n * P:(h % 2) * S + n * P + P]
            a = c.gcols[:, m * H + h:m * H + h + 1]
            if m == n:
                ins = dve.scalar_tensor_tensor(w[:, x, h, :], row, a, c.maskK[:, :], ALU.add, ALU.min)
            else:
                ins = dve.tensor_scalar(w[:, x, h, :], row, a, 0.0, ALU.add, ALU.min)
        ins.then_inc(c.s['ml_vector'], 1)
    for x in range(3):
        dve.wait_ge(c.s['ml_scalar'], ML_SCALAR['weight'] + x + 1)
        dve.wait_ge(c.s['ml_tensor'], ML_TENSOR['scores'] + x + 1)
        dve.scalar_tensor_tensor(w[:, x, :, :], c.pb[4 + x][:, :].rearrange('p (h t) -> p h t', h=H),
                                 XA_D ** -0.5, w[:, x, :, :], ALU.mult, ALU.mult).then_inc(c.s['ml_vector'], 1)
    dve.wait_ge(c.s['ml_scalar'], ML_SCALAR['em'] + 1)
    dve.wait_ge(c.s['ml_tensor'], ML_TENSOR['num'] + 2)
    sums = c.pb[1][:, 0:NT * H]
    c.vstep(dve.tensor_tensor(c.mden[:, :], sums, c.gcols[:, NT * H:2 * NT * H], ALU.max))
    c.vstep(dve.scalar_tensor_tensor(c.mden[:, :], sums, -1.0, c.mden[:, :], ALU.mult, ALU.max))
    c.vstep(dve.reciprocal(c.mden[:, :], c.mden[:, :]))
    for n in range(NT):
        bank = c.pb[0 if n == 0 else 7]
        out = c.mix[:, n, 0:512].rearrange('p (h v) -> p h v', h=H)
        c.vstep(dve.tensor_tensor(out, bank[:, :].rearrange('p (h v) -> p h v', h=H),
                                  c.mden[:, n * H:n * H + H].unsqueeze(2).broadcast_to([P, H, P]), ALU.mult))
        dve.wait_ge(c.s['ml_scalar'], ML_SCALAR['sigmoid'] + n + 1)
        dve.tensor_tensor(c.mix[:, n, 0:512], c.mix[:, n, 0:512], c.z[:, n, OD_O:OD_O + 512], ALU.mult)\
           .then_inc(c.s['ml_vector'], 1)
    for n in range(NT):
        dve.wait_ge(c.s['ml_scalar'], ML_SCALAR['square'] + n + 1)
        c.vstep(dve.tensor_reduce(c.mss[:, n * H:n * H + H], c.z[:, n, OD_O:OD_O + 512]
                                  .rearrange('p (h v) -> p h v', h=H), AX, ALU.add))
    dve.tensor_scalar(c.mss[:, :], c.mss[:, :], 1.0 / P, EPS, ALU.mult, ALU.add).then_inc(c.s['ml_vector'], 1)
    dve.wait_ge(c.s['ml_rstd'], 1)
    for n in range(NT):
        out = c.mix[:, n, 0:512].rearrange('p (h v) -> p h v', h=H)
        c.vstep(dve.tensor_tensor(out, out, c.mrstd[:, n * H:n * H + H].unsqueeze(2).broadcast_to([P, H, P]), ALU.mult))
        dve.tensor_tensor(c.mix[:, n, 0:512], c.mix[:, n, 0:512], c.mlg[:, :], ALU.mult).then_inc(c.s['mix_ready'], 1)


def mlstm_pool(c, pool, st):
    pool.wait_ge(c.s['ml_vector'], ML_VECTOR['ms'] + 1)
    pool.tensor_tensor(c.mrstd[:, :], c.mss[:, :], c.neghalf[:, 0:NT * ML_HEADS], ALU.pow).then_inc(c.s['ml_rstd'], 1)


def mlstm_act(c, act, st):
    r = c.grows
    act.wait_ge(c.s['ml_vector'], ML_VECTOR['abs'] + 1)
    signal(act, act.activation(r[:, 2, :], r[:, 2, :], ACT.Exp, scale=-1.0), c.s['ml_scalar'], ML_SCALAR['log'] + 1)
    act.activation(r[:, 2, :], r[:, 2, :], ACT.Ln, bias=1.0).then_inc(c.s['ml_scalar'], 1)
    w = c.PT[:, 0:3 * ML_HEADS * P].rearrange('p (x f) -> p x f', x=3)
    for x in range(3):
        act.wait_ge(c.s['ml_vector'], ML_VECTOR['exponent'] + x + 1)
        act.activation(w[:, x, :], w[:, x, :], ACT.Exp).then_inc(c.s['ml_scalar'], 1)
    act.wait_ge(c.s['ml_vector'], ML_VECTOR['cols'] + 1)
    em = c.gcols[:, NT * ML_HEADS:2 * NT * ML_HEADS]
    act.activation(em, em, ACT.Exp, scale=-1.0).then_inc(c.s['ml_scalar'], 1)
    for n in range(NT):
        o = c.z[:, n, OD_O:OD_O + 512]
        act.activation(o, o, ACT.Sigmoid).then_inc(c.s['ml_scalar'], 1)
    for n in range(NT):
        act.wait_ge(c.s['ml_vector'], ML_VECTOR['h'] + n + 1)
        act.activation(c.z[:, n, OD_O:OD_O + 512], c.mix[:, n, 0:512], ACT.Square).then_inc(c.s['ml_scalar'], 1)


def mlstm_pe(c, pe, st):
    H = ML_HEADS
    pe.wait_ge(c.s['ml_vector'], ML_VECTOR['gates'] + 2)
    for a in range(2):
        for n in range(NT):
            mm = pe.transpose(c.pb[0][0:H, a * S + n * P:a * S + n * P + P],
                              c.z[:, n, OD_G + a * H:OD_G + a * H + H], c.ident[:, :])
    mm.then_inc(c.s['ml_tensor'], 1)
    for x, (m, n) in enumerate(ML_TILES):
        for h in range(H):
            mm = pe.matmul(c.pb[4 + x][:, h * P:h * P + P], c.zT[:, 4 + h, m * P:m * P + P],
                           c.zT[:, h, n * P:n * P + P], start=True, stop=True)
        mm.then_inc(c.s['ml_tensor'], 1)
    pe.wait_ge(c.s['ml_vector'], ML_VECTOR['scans'] + 1)
    for i, row in enumerate((4, 6)):
        for n in range(NT):
            at = (i * NT + n) * H
            mm = pe.transpose(c.pb[1][:, at:at + H], c.grows[:, row, n * P:n * P + P], c.ident[0:H, 0:H])
    for h in range(H):
        mm = pe.matmul(c.pb[2 + h // 2][:, (h % 2) * S:(h % 2) * S + S], c.selT[0:H, h, :], c.grows[:, 5, :],
                       start=True, stop=True)
    mm.then_inc(c.s['ml_tensor'], 1)
    pe.wait_ge(c.s['ml_vector'], ML_VECTOR['cols'] + 1)
    for n in range(NT):
        pe.wait_ge(c.s['ml_vector'], ML_VECTOR['sw'] + (1 if n == 0 else 3))
        bank = c.pb[0 if n == 0 else 7]
        for h in range(H):
            xs = [x for x, (_, nn) in enumerate(ML_TILES) if nn == n]
            for i, x in enumerate(xs):
                lhs = c.PT[:, (x * H + h) * P:(x * H + h) * P + P]
                m = ML_TILES[x][0]
                pe.matmul(bank[:, h * P:h * P + P], lhs, c.z[:, m, OD_V + h * P:OD_V + h * P + P],
                          start=i == 0, stop=i == len(xs) - 1)
            for i, x in enumerate(xs):
                lhs = c.PT[:, (x * H + h) * P:(x * H + h) * P + P]
                mm = pe.matmul(c.pb[1][:, n * H + h:n * H + h + 1], lhs, c.ones[:, 0:1],
                               start=i == 0, stop=i == len(xs) - 1)
        mm.then_inc(c.s['ml_tensor'], 1)


LATENTS = ((OD_CQ, 3), (OD_CKV, 2))


def mla_in_act(c, act, st):
    for i, (at, m) in enumerate(LATENTS):
        for n in range(NT):
            act.activation(c.L[:, 0:m * P], c.z[:, n, at:at + m * P], ACT.Square,
                           accum_out=c.lss[:, 2 * i + n:2 * i + n + 1]).then_inc(c.s['la_ss'], 1)
            act.wait_ge(c.s['la_ss'], 2 * i + n + 1)


def mla_in_pool(c, pool, st):
    pool.wait_ge(c.s['la_ss'], 4)
    for i, (_, m) in enumerate(LATENTS):
        c.pstep(pool.tensor_scalar(c.lms[:, 2 * i:2 * i + 2], c.lss[:, 2 * i:2 * i + 2], 1.0 / (m * P), EPS,
                                   ALU.mult, ALU.add))
    pool.tensor_tensor(c.lrstd[:, :], c.lms[:, :], c.neghalf[:, 0:4], ALU.pow).then_inc(c.s['la_rstd'], 1)


def mla_in_dve(c, dve, st):
    dve.wait_ge(c.s['la_rstd'], 1)
    for i, (at, m) in enumerate(LATENTS):
        for n in range(NT):
            v = c.z[:, n, at:at + m * P]
            dve.tensor_scalar(v, v, c.lrstd[:, 2 * i + n:2 * i + n + 1], None, ALU.mult).then_inc(c.s['la_normed'], 1)
    dve.wait_ge(c.s['la_turned'], 1)
    for ch in range(5):
        col = COL1['od_q_norm_g_2'] + ch
        c.vstep(dve.tensor_scalar(c.hL[:, ch, :], c.pb[ch // 2][:, (ch % 2) * S:(ch % 2) * S + S],
                                  c.col1[:, col:col + 1], None, ALU.mult))
    c.vstep(dve.tensor_copy(r32(c.rT[:, 0:5, :]), c.hL[:, 0:5, :]))
    dve.tensor_tensor(r32(c.hL[:, 0:5, :]), c.hL[:, 0:5, :], high(c.rT[:, 0:5, :]), ALU.subtract).then_inc(c.s['la_ready'], 1)


def mla_in_pe(c, pe, st):
    pe.wait_ge(c.s['la_normed'], 4)
    ch = 0
    for at, m in LATENTS:
        for u in range(m):
            for n in range(NT):
                mm = pe.transpose(c.pb[ch // 2][:, (ch % 2) * S + n * P:(ch % 2) * S + n * P + P],
                                  c.z[:, n, at + u * P:at + u * P + P], c.ident[:, :])
            ch += 1
    mm.then_inc(c.s['la_turned'], 1)


def mla_stage(core, ready):
    c = core
    a = dict(heads=MLA_HEADS, scale=QKW ** -0.5, banks=[[0, 1], [2, 3], [4, 5], [6, 7]],
             keys=lambda n: P * (n + 1),
             q=lambda i, n: c.zT[0:QKW, i, n * P:n * P + P], k=lambda i, n: c.zT[0:QKW, 8 + i, 0:P * (n + 1)],
             mask=lambda n: c.maskQ2[:, P - n * P:2 * P], mask_ready=lambda n: [],
             pv=lambda n: [(c.pb[7][HD * (h % 2):HD * (h % 2) + HD, (h // 2) * P:(h // 2) * P + P],
                            [(c.xn[:, ch, h * P + NOPE:h * P + P], ch * MLA_HEADS + h, 1) for ch in range(n + 1)])
                           for h in range(MLA_HEADS)],
             out=(4, 8), ready=[('la_T_a', 4), ('la_T_b', 4)])
    return dict(kind='mla', evacuated=ready, att=attend_plan(core, a))


def mla_dve(c, dve, st):
    for sem, v in st['evacuated']:
        dve.wait_ge(c.s[sem], v)
    kcat = c.L[:, 0:NT * MLA_HEADS * QKW].rearrange('p (n h d) -> p n h d', n=NT, h=MLA_HEADS)
    for n in range(NT):
        cos, sin = c.cos[:, 64 + 16 * n:80 + 16 * n], c.sin[:, 64 + 16 * n:80 + 16 * n]
        q = c.z[:, n, OD_Q:OD_Q + MLA_HEADS * QKW].rearrange('p (h d) -> p h d', h=MLA_HEADS)[:, :, NOPE:QKW]
        rotate(c, dve, q, q, MLA_HEADS, ROPE_W // 2, cos, sin, c.PT[:, 0:256], c.PT[:, 256:512])
        kr = c.z[:, n, OD_KR:OD_KR + ROPE_W].unsqueeze(1)
        rotate(c, dve, kr, kr, 1, ROPE_W // 2, cos, sin, c.PT[:, 0:32], c.PT[:, 256:288])
        c.vstep(dve.tensor_copy(kcat[:, n, :, NOPE:QKW], kr.broadcast_to([P, MLA_HEADS, ROPE_W])))
        dve.tensor_copy(kcat[:, n, :, 0:NOPE], c.xn[:, n, :].rearrange('p (h d) -> p h d', h=MLA_HEADS)[:, :, 0:NOPE])\
           .then_inc(c.s['la_rot'], 1)
    mla_evacuate(c, dve, 1)
    attend_dve(c, dve, st['att'])


def mla_evacuate(c, eng, par):
    for b in range(par, 8, 2):
        n, what, h0 = b // 4, (b // 2) % 2, 4 * (b % 2)
        eng.wait_ge(c.s['la_T'], b + 1)
        src = c.pb[b][0:QKW, :].rearrange('p (h t) -> p h t', h=4)
        dst = c.zT[0:QKW, 8 * what + h0:8 * what + h0 + 4, n * P:n * P + P]
        ins = eng.tensor_copy(dst, src) if par else eng.activation(dst, src, ACT.Copy)
        ins.then_inc(c.s['la_T_' + 'ab'[par]], 1)


def mla_pe(c, pe, st):
    for b in range(8):
        n, what, h0 = b // 4, (b // 2) % 2, 4 * (b % 2)
        pe.wait_ge(c.s['la_rot'], n + 1)
        for h in range(h0, h0 + 4):
            if what:
                src = c.L[:, (n * MLA_HEADS + h) * QKW:(n * MLA_HEADS + h + 1) * QKW]
            else:
                src = c.z[:, n, OD_Q + h * QKW:OD_Q + (h + 1) * QKW]
            mm = pe.transpose(c.pb[b][0:QKW, (h - h0) * P:(h - h0) * P + P], src, c.ident[:, :])
        mm.then_inc(c.s['la_T'], 1)
    attend_pe(c, pe, st['att'])


def mla_act(c, act, st):
    mla_evacuate(c, act, 0)
    attend_act(c, act, st['att'])


MOE_STEPS = F_EXPERT // FT


MO_TENSOR = in_order(logits=1, counts=1, rows=1, spread=8, summed=1)
MO_VECTOR = in_order(logit_less=1, chosen=1, slots=1, rows_in=1, spread_in=8)


def moe_stage(core):
    st = dict(kind='moe', j0=len(core.jobs), split0=core.n_steps)
    core.n_steps += MOE_STEPS * N_EXP
    assert MOE_STEPS % 2 == 0
    for e in range(N_EXP):
        for i in range(MOE_STEPS):
            m = e * MOE_STEPS + i + 1
            for q in range(3):
                job(core, None, ('me_gu0' if q < 2 else 'me_down0', m))
    return st


def moe_sems(c, p):
    E = {name: c.s[name if p == 0 else f'me_{name}1'] for name in ('gu_hi', 'gu_lo', 'down_hi', 'down_lo')}
    return E | {name: c.s[f'me_{name}{p}'] for name in
            ('gu', 'down', 'silu', 'act', 'T_hi', 'turned', 'actT', 'onehot', 'gathered', 'hTa', 'hTb', 'sums', 'ye', 'scat', 'hLe_sum')}


def moe_load(c, sp, q, e, i, m, slot, sem):
    w = c.ring[:, slot, :]
    if q < 2:
        w = w.rearrange('p (k s n) -> p k s n', k=4, s=2)
        for s, view in enumerate((c.moe_gate, c.moe_up)):
            sp.dma_start(w[:, :, s, :], view[:, bass.ds(e * KD + 4 * q, 4), bass.ds(i * FT, FT)]).then_inc(sem, 16)
    else:
        w = w.rearrange('p (k n) -> p k n', k=2)
        for a in range(2):
            sp.dma_start(w[:, a:a + 1, :], c.moe_down[:, bass.ds(m * 2 + a, 1), :])\
              .then_inc(sem, 16)


def moe_pass_sp(c, sp, st, p):
    j0 = st['j0']
    E = moe_sems(c, p)

    def load(q, e, i, r, m, first=False):
        if not first:
            sp.wait_ge(E['gu'] if q < 2 else E['down'], m - 1)
        elif p == 0:
            sem, v = c.jobs[j0 + 3 * r + q - RING][1]
            sp.wait_ge(c.s[sem], v)
        moe_load(c, sp, q, e, i, m, (j0 + 3 * r + q) % RING, c.again[r] if p else c.landed[(j0 + 3 * r + q) % RING])

    def step(e, i, r, m):
        load(0, e, i, r, m)
        load(1, e, i, r, m)
        load(2, None, None, 1 - r, m - 1)
    for m in range(3):
        for q in range(2):
            load(q, 0, m, m % 2, m, m < 2)
        if m:
            load(2, None, None, (m - 1) % 2, m - 1, True)
    with sp.Fori(1, (MOE_STEPS - 2) // 2) as it:
        for r in (1, 0):
            i = it * 2 + (2 - r)
            step(0, i, r, i)
    step(0, MOE_STEPS - 1, 1, MOE_STEPS - 1)
    with sp.Fori(1, N_EXP) as e:
        with sp.Fori(0, MOE_STEPS // 2) as it:
            for r in range(2):
                step(e, it * 2 + r, r, e * MOE_STEPS + it * 2 + r)
    last = N_EXP * MOE_STEPS - 1
    load(2, None, None, last % 2, last)


def overflow(c, eng, run):
    eng.wait_ge(c.s['me_count'], 1)
    most = eng.value_load(c.count[0:1, 0:1], min_val=0, max_val=S)
    with eng.If(most > P):
        run()


def moe_sp(c, sp, st):
    moe_pass_sp(c, sp, st, 0)

    def again():
        for q in (0, 2):
            sp.wait_ge(c.s['me_gu0' if q == 0 else 'me_down0'], N_EXP * MOE_STEPS)
        moe_pass_sp(c, sp, st, 1)
        sp.wait_ge(c.s['me_gu1'], N_EXP * MOE_STEPS)
        sp.wait_ge(c.s['me_down1'], N_EXP * MOE_STEPS)
    overflow(c, sp, again)


def moe_split_value(st, q, m, p):
    return split_value(st if p == 0 else dict(split0=0), q, m)


def moe_loop(eng, body, end):
    def expert(e, last):
        m0 = e * MOE_STEPS
        with eng.Fori(0, MOE_STEPS // 2 - 1) as it:
            for r in range(2):
                body(r, m0 + it * 2 + r, 2)
        for r in range(2):
            body(r, m0 + (MOE_STEPS - 2 + r), 1 - r if last else 2)
        end(e, last)
    with eng.Fori(0, N_EXP - 1) as e:
        expert(e, False)
    expert(N_EXP - 1, True)


def moe_pass_pe(c, pe, st, p):
    E = moe_sems(c, p)
    G, T = c.pb[6], c.pb[7]

    def gather(e1, half):
        pe.wait_ge(E['onehot'], e1)
        bank = (G, T)[half]
        for kc in range(4):
            for n in range(NT):
                mm = pe.matmul(bank[:, kc * P:kc * P + P], c.xn[:, n, (4 * half + kc) * P:(4 * half + kc) * P + P],
                               c.onehot[:, n, :], start=n == 0, stop=n == NT - 1)
        mm.then_inc(E['gathered'], 1)

    def parts(q, r, n):
        slot = ffn_slot(st, q, r)
        return chunks(c.hi_moe[slot], n, SLOT // n), chunks(c.ring[:, slot, :], n, SLOT // n)

    def gate_up(r, m):
        for q in range(2):
            pe.wait_ge(E['gu_lo'], moe_split_value(st, q, m, p))
            wh, wl = parts(q, r, 4)
            for i in range(4):
                x = 4 * q + i
                mm = product(pe, G[:, :], (c.hTe[:, x, :], c.hLe[:, x, :]), (wh[:, i, :], wl[:, i, :]), x == 0, x == KD - 1)
        mm.then_inc(E['gu'], 1)

    def turn(m):
        pe.wait_ge(E['act'], m + 1)
        for a in range(2):
            mm = pe.transpose(T[:, a * P:a * P + P], c.fa[:, 0, a * P:a * P + P], c.ident[:, :])
        mm.then_inc(E['turned'], 1)

    def down(r, m, first, last):
        pe.wait_ge(E['down_lo'], moe_split_value(st, 2, m, p))
        pe.wait_ge(E['actT'], m + 1)
        wh, wl = parts(2, r, 2)
        for h in range(2):
            col = slice(h * 512, h * 512 + 512)
            for a in range(2):
                mm = product(pe, c.pb[4 + h][:, :], (c.faT[:, 0, a, :], c.faL[:, 0, a, :]), (wh[:, a, col], wl[:, a, col]),
                             first and a == 0, last and a == 1)
        mm.then_inc(E['down'], 1)

    gather(1, 0)
    gather(1, 1)
    with pe.Fori(0, N_EXP) as e:
        m0 = e * MOE_STEPS
        pe.wait_ge(E['hTb'], e * 2 + 2)
        gate_up(0, m0)
        turn(m0)
        gate_up(1, m0 + 1)
        down(0, m0, True, False)
        turn(m0 + 1)
        with pe.Fori(1, MOE_STEPS // 2) as it:
            for r in range(2):
                m = m0 + it * 2 + r
                gate_up(r, m)
                down(1 - r, m - 1, False, False)
                turn(m)
        last = m0 + (MOE_STEPS - 1)
        gather(e + 2, 0)
        down(1, last, False, True)
        gather(e + 2, 1)
        pe.wait_ge(E['ye'], e + 1)
        pe.wait_ge(E['sums'], e + 1)
        for n in range(NT):
            for h in range(2):
                mm = pe.matmul(c.pb[2 * n + h][:, :], c.combine[:, n * P:n * P + P], c.ye[:, h * 512:h * 512 + 512],
                               start=False, stop=False, skip_group_check=True)
        mm.then_inc(E['scat'], 1)


def moe_pe(c, pe, st):
    for sem, v in st['hT']:
        pe.wait_ge(c.s[sem], v)
    for n in range(NT):
        for i, h in enumerate((c.hL, c.hT)):
            for kc in range(KD):
                mm = pe.matmul(c.pb[0][:, n * N_EXP:n * N_EXP + N_EXP], high(h[:, kc, n * P:n * P + P]),
                               c.wrouter[:, kc, :], start=i + kc == 0, stop=i == 1 and kc == KD - 1)
    mm.then_inc(c.s['mo_tensor'], 1)
    pe.wait_ge(c.s['mo_vector'], MO_VECTOR['chosen'] + 1)
    for n in range(NT):
        out = c.pb[1][:, n * N_EXP:n * N_EXP + N_EXP]
        pe.matmul(out, c.triT[:, :], c.chosen[:, n, :], start=True, stop=n == 0)
        if n:
            pe.matmul(out, c.ones[:, 0:P], c.chosen[:, 0, :], start=False, stop=True)
    for n in range(NT):
        mm = pe.matmul(c.pb[1][:, 16:16 + N_EXP], c.ones[:, 0:P], c.chosen[:, n, :], start=n == 0, stop=n == NT - 1)
    mm.then_inc(c.s['mo_tensor'], 1)
    pe.wait_ge(c.s['mo_vector'], MO_VECTOR['slots'] + 1)
    for i, buf in enumerate((c.slots, c.gates)):
        for n in range(NT):
            mm = pe.transpose(c.pb[2][0:N_EXP, i * S + n * P:i * S + n * P + P], buf[:, n, 0:N_EXP], c.ident[:, :])
    mm.then_inc(c.s['mo_tensor'], 1)
    pe.wait_ge(c.s['mo_vector'], MO_VECTOR['rows_in'] + 1)
    for i in range(2):
        for e in range(N_EXP):
            b = i * (N_EXP // 2) + e // 2
            if b >= 4 and e % 2 == 0:
                pe.wait_ge(c.s['mo_vector'], MO_VECTOR['spread_in'] + b - 3)
            mm = pe.matmul(c.pb[4 + b % 4][:, (e % 2) * S:(e % 2) * S + S], c.selT[0:N_EXP, e, :], c.mrows[:, i, :],
                           start=True, stop=True)
            if e % 2:
                mm.then_inc(c.s['mo_tensor'], 1)
    pe.wait_ge(c.s['mo_vector'], MO_VECTOR['spread_in'] + 8)
    for b in range(4):
        for h in range(2):
            pe.matmul(c.pb[b][:, h * S:h * S + S], c.zero[:, 0:P], c.zero[:, :], start=h == 0, stop=False,
                      skip_group_check=True)
    moe_pass_pe(c, pe, st, 0)
    overflow(c, pe, lambda: moe_pass_pe(c, pe, st, 1))
    pe.matmul(c.pb[0][:, 0:S], c.zero[:, 0:P], c.zero[:, :], start=False, stop=True, skip_group_check=True)\
      .then_inc(c.s['mo_tensor'], 1)


def moe_pass_act(c, act, st, p):
    E = moe_sems(c, p)

    def take_gather(e1):
        for half in range(2):
            act.wait_ge(E['gathered'], e1 * 2 - 1 + half)
            for i in range(4):
                kc = 4 * half + i
                ins = act.activation(r32(c.hTe[:, kc, :]), c.pb[6 + half][:, i * P:i * P + P], ACT.Identity,
                                     bias=c.modC[:, 16 + kc:17 + kc], scale=c.modA[:, 8 + kc:9 + kc])
            ins.then_inc(E['hTa'], 1)

    def landed(q, r, m):
        j = st['j0'] + 3 * r + q
        if p == 0:
            act.wait_ge(c.landed[j % RING], (m - r) * (LOAD // 2) + LOAD * (j // RING + 1))
        elif q < 2:
            act.wait_ge(c.again[r], (m - r) * (3 * LOAD // 2) + 2 * LOAD)
        else:
            act.wait_ge(c.again[r], (m - r) * (3 * LOAD // 2) + 3 * LOAD)

    def hi(q, r, m):
        split_hi(c, act, st, q, r, m, c.hi_moe, landed, E[split_names(q)[0]])

    def body(r, m, ahead):
        act.wait_ge(E['gu'], m + 1)
        act.activation(c.fs[:, 0, :], c.pb[6][:, 0:FT], ACT.Silu).then_inc(E['silu'], 1)
        if ahead:
            hi(1, 1 - r, m + 1)
        act.wait_ge(E['turned'], m + 1)
        act.activation(r32(c.faT[:, 0, :, :]), c.pb[7][:, 0:2 * P].rearrange('p (a t) -> p a t', a=2), ACT.Copy)\
           .then_inc(E['T_hi'], 1)
        hi(2, r, m)
        if ahead == 2:
            hi(0, r, m + 2)

    def end(e, last):
        take_gather(e + 2)
        act.wait_ge(E['down'], (e + 1) * MOE_STEPS)
        for h in range(2):
            ins = act.activation(c.ye[:, h * 512:h * 512 + 512], c.pb[4 + h][:, :], ACT.Copy)
        ins.then_inc(E['ye'], 1)
    hi(0, 0, 0)
    hi(1, 0, 0)
    hi(0, 1, 1)
    take_gather(1)
    moe_loop(act, body, end)


def moe_act(c, act, st):
    act.wait_ge(c.s['mo_vector'], MO_VECTOR['logit_less'] + 1)
    act.activation(c.mexp[:, :], c.mexp[:, :], ACT.Exp).then_inc(c.s['mo_exp'], 1)
    moe_pass_act(c, act, st, 0)
    overflow(c, act, lambda: moe_pass_act(c, act, st, 1))


def moe_pass_dve(c, dve, st, p):
    E = moe_sems(c, p)

    def one_hot(e1):
        for n in range(NT):
            ins = dve.tensor_tensor(c.onehot[:, n, :], c.slotF2[:, p * P:p * P + P],
                                    c.slots[:, n, bass.ds(e1 - 1, 1)].broadcast_to([P, P]), ALU.is_equal)
        ins.then_inc(E['onehot'], 1)

    def take_gather(e1):
        for half in range(2):
            dve.wait_ge(E['hTa'], e1 * 2 - 1 + half)
            for i in range(4):
                kc = 4 * half + i
                ins = dve.tensor_scalar(c.hLe[:, kc, :], c.pb[6 + half][:, i * P:i * P + P],
                                        c.modA[:, 8 + kc:9 + kc], c.modC[:, 16 + kc:17 + kc], ALU.mult, ALU.add)
            signal(dve, ins, E['hLe_sum'], e1 * 2 - 1 + half)
            v = slice(4 * half, 4 * half + 4)
            dve.tensor_tensor(r32(c.hLe[:, v, :]), c.hLe[:, v, :], high(c.hTe[:, v, :]), ALU.subtract).then_inc(E['hTb'], 1)

    def lo(q, r, m):
        a, b = split_names(q)
        split_lo(c, dve, st, q, r, c.hi_moe, E[a], moe_split_value(st, q, m, p), E[b])

    def body(r, m, ahead):
        dve.wait_ge(E['silu'], m + 1)
        dve.tensor_tensor(c.fa[:, 0, :], c.fs[:, 0, :], c.pb[6][:, FT:2 * FT], ALU.mult).then_inc(E['act'], 1)
        if ahead:
            lo(1, 1 - r, m + 1)
        dve.wait_ge(E['T_hi'], m + 1)
        dve.tensor_tensor(r32(c.faL[:, 0, :, :]), c.pb[7][:, 0:2 * P].rearrange('p (a t) -> p a t', a=2),
                          high(c.faT[:, 0, :, :]), ALU.subtract).then_inc(E['actT'], 1)
        lo(2, r, m)
        if ahead == 2:
            lo(0, r, m + 2)

    def end(e, last):
        dve.scalar_tensor_tensor(c.combine[:, :], c.slotsB[:, bass.ds(e, 1), :].rearrange('p a t -> p (a t)'),
                                 c.slotP[:, p:p + 1], c.gatesB[:, bass.ds(e, 1), :].rearrange('p a t -> p (a t)'),
                                 ALU.is_equal, ALU.mult).then_inc(E['sums'], 1)
        take_gather(e + 2)
        if not last:
            one_hot(e + 3)
    one_hot(1)
    lo(0, 0, 0)
    lo(1, 0, 0)
    lo(0, 1, 1)
    take_gather(1)
    one_hot(2)
    moe_loop(dve, body, end)


def moe_dve(c, dve, st):
    dve.wait_ge(c.s['mo_tensor'], MO_TENSOR['logits'] + 1)
    for n in range(NT):
        lg = c.logits[:, n, :]
        c.vstep(dve.tensor_copy(lg, c.pb[0][:, n * N_EXP:n * N_EXP + N_EXP]))
        c.vstep(dve.max(c.top8[:, :], lg))
        sel, eq, pre = c.chosen[:, n, :], c.meq[:, 0:8], c.meq[:, 8:16]
        c.vstep(dve.tensor_scalar(sel, lg, c.top8[:, 1:2], None, ALU.is_gt, ALU.add, accum_out=c.cnt[:, 0:1]))
        c.vstep(dve.tensor_scalar(c.cnt[:, 1:2], c.cnt[:, 0:1], -1.0, 2.0, ALU.mult, ALU.add))
        c.vstep(dve.tensor_scalar(eq, lg, c.top8[:, 1:2], None, ALU.is_equal))
        c.vstep(dve.tensor_tensor_scan(pre, c.ones[:, 0:8], eq, 0.0, ALU.mult, ALU.add))
        c.vstep(dve.scalar_tensor_tensor(eq, pre, c.cnt[:, 1:2], eq, ALU.is_le, ALU.mult))
        c.vstep(dve.tensor_tensor(sel, sel, eq, ALU.add))
        c.vstep(dve.tensor_scalar(c.mexp[:, 9 * n:9 * n + 8], lg, c.top8[:, 0:1], None, ALU.subtract))
        c.vstep(dve.tensor_tensor(c.mexp[:, 9 * n + 8:9 * n + 9], c.top8[:, 1:2], c.top8[:, 0:1], ALU.subtract))
    signal(dve, dve.tensor_scalar(c.mexp[:, :], c.mexp[:, :], 0.0, None, ALU.min), c.s['mo_vector'], MO_VECTOR['logit_less'] + 1)
    dve.tensor_scalar(c.slotP[:, 1:2], c.slotP[:, 0:1], float(P), None, ALU.add).then_inc(c.s['mo_vector'], 1)
    dve.wait_ge(c.s['mo_exp'], 1)
    for n in range(NT):
        c.vstep(dve.tensor_scalar(c.cnt[:, 0:1], c.mexp[:, 9 * n + 8:9 * n + 9], 1.0, None, ALU.add))
        c.vstep(dve.reciprocal(c.cnt[:, 1:2], c.cnt[:, 0:1]))
        c.vstep(dve.scalar_tensor_tensor(c.gates[:, n, 0:8], c.mexp[:, 9 * n:9 * n + 8], c.cnt[:, 1:2],
                                         c.chosen[:, n, :], ALU.mult, ALU.mult))
    dve.wait_ge(c.s['mo_tensor'], MO_TENSOR['counts'] + 1)
    for n in range(NT):
        c.vstep(dve.tensor_tensor(c.slots[:, n, 0:8], c.pb[1][:, n * 8:n * 8 + 8], c.chosen[:, n, :], ALU.mult))
    c.vstep(dve.tensor_reduce(c.cnt[:, 0:1], c.pb[1][:, 16:24], AX, ALU.max))
    dve.tensor_copy(c.count[:, 0:1], c.cnt[:, 0:1]).then_inc(c.s['me_count'], 1)
    c.vstep(dve.memset(c.slots[:, :, 8:9], 0.0))
    signal(dve, dve.tensor_scalar(c.slots[:, :, :], c.slots[:, :, :], 1.0, None, ALU.subtract), c.s['mo_vector'], MO_VECTOR['slots'] + 1)
    dve.wait_ge(c.s['mo_tensor'], MO_TENSOR['rows'] + 1)
    dve.tensor_copy(c.mrows[:, :, :], c.pb[2][0:N_EXP, :].rearrange('p (a t) -> p a t', a=2)).then_inc(c.s['mo_vector'], 1)
    for b in range(8):
        dve.wait_ge(c.s['mo_tensor'], MO_TENSOR['spread'] + b + 1)
        dst = (c.slotsB, c.gatesB)[b // 4][:, 2 * (b % 4):2 * (b % 4) + 2, :]
        signal(dve, dve.tensor_copy(dst, c.pb[4 + b % 4][:, :].rearrange('p (e t) -> p e t', e=2)),
               c.s['mo_vector'], MO_VECTOR['spread_in'] + b + 1)
    moe_pass_dve(c, dve, st, 0)
    overflow(c, dve, lambda: moe_pass_dve(c, dve, st, 1))
    dve.wait_ge(c.s['mo_tensor'], MO_TENSOR['summed'] + 1)
    for n in range(NT):
        for h in range(2):
            out = c.x[:, n, h * 512:h * 512 + 512]
            c.vstep(dve.tensor_tensor(c.tmp[:, :], c.pb[2 * n + h][:, :], c.grow[:, 1, h * 512:h * 512 + 512], ALU.mult))
            c.vstep(dve.tensor_tensor(out, out, c.tmp[:, :], ALU.add))
    c.x_written(dve)


def mem_act(c, act, st):
    act.wait_ge(c.s['x_ready'], st['x_before'])
    for n in range(NT):
        act.dma_start(c.grow[:, n, :], c.t['mem_2'][0, n * P:n * P + P, :]).then_inc(c.s['mem_loaded'], 16)


def make_plan(c):
    t = c.t
    stages = []
    updates = [0]
    count = {}

    def add(st):
        st['x_before'] = updates[0]
        stages.append(st)
        return st

    def number(kind):
        count[kind] = count.get(kind, -1) + 1
        return count[kind]

    def x_waits():
        return [('x_ready', updates[0])] if updates[0] else [('x_loaded', 32)]

    def norm(src, scale, shift=None, waits=None):
        k = number('norm')
        add(dict(kind='norm', k=k, src=src, scale=scale, shift=shift, waits=waits or x_waits()))
        return h_chunk(k)

    def columns(name, layer):
        at = COL1[name] + KD * layer
        return lambda kc: c.col1[:, at + kc:at + kc + 1]

    def tok(view, lo, hi, dst, k=KD, ksrc=0, evac='copy'):
        return [(view, a, min(512, hi - a), k, ksrc, 'tok', evac,
                 (lambda n, a=a: dst(n, a - lo, min(512, hi - a)))) for a in range(lo, hi, 512)]

    def feat(view, lo, hi, chunk):
        return [(view, a, min(512, hi - a), KD, 0, 'feat', 'copy',
                 (lambda u, m, a=a: c.zT[:, chunk + (a - lo) // P + u:chunk + (a - lo) // P + u + m, :]))
                for a in range(lo, hi, 512)]

    def add_x(view, k, gated, src, waits, name):
        tiles = [(view, a, 512, k, 0, 'tok', a if gated else 'add', (lambda n, a=a: c.x[:, n, a:a + 512]))
                 for a in (0, 512)]
        add(proj(c, name, src, waits, tiles, c.hi_out))
        updates[0] += 1

    def ffn(gate, up, up_col, down, gated, ready):
        st = ffn_stage(c, gate, up, up_col, down, gated, number('ffn'))
        st['ready'] = ready
        add(st)
        updates[0] += 1

    for l in range(2):
        add(ada_stage(c, l, 0))
        h = norm(c.x, lambda kc: c.modA[:, kc:kc + 1], lambda kc: c.modC[:, kc:kc + 1],
                 x_waits() + [('mod_ready', 2 * l + 1)])
        v = rows_view(t['w_in'][l])
        z = lambda lo: (lambda n, off, w: c.z[:, n, lo + off:lo + off + w])
        p = add(proj(c, 'w_in', c.hsplit, [], tok(v, 0, Z_BQ, z(0)) + tok(v, Z_UV, IN1, z(Z_UV)) +
                     feat(v, Z_BQ, Z_BI, 0) + tok(v, Z_BI, Z_UV, z(Z_BI)), c.hi_in, h))
        ev = proj_evacuated(p)
        ada = add(ada_stage(c, l, 1))
        for st in (dsa_stage(c, l, ev), dict(kind='gmlp', k=l, evacuated=ev), dict(kind='hgrn', k=l, evacuated=ev)):
            st['ada'] = ada
            add(st)
        tr = add(turn_stage(c, number('turn'), [3, 4, 5, 6, 7], [('mix_ready', 4 * (l + 1))]))
        add_x(rows_view(t['w_out'][l]), KD, True, c.hsplit, turned_events(tr) + [('att_mixT', 2 * (l + 1))], 'w_out')
        h = norm(c.x, lambda kc: c.modA[:, 8 + kc:9 + kc], lambda kc: c.modC[:, 16 + kc:17 + kc],
                 x_waits() + [('mod_ready', 2 * l + 2)])
        if l == 0:
            ffn(rows_view(t['ffn_w_gate'][0]), rows_view(t['ffn_w_up'][0]), 0, rows_view(t['ffn_w_down'][0]), True, h)
        else:
            st = add(moe_stage(c))
            st['hT'] = [h(KD - 1)]
            updates[0] += 1
    add(dict(kind='final', k=0, waits=x_waits(), gain=t['g_final']))
    updates[0] += 1
    add(dict(kind='mem'))
    for l in range(2):
        h = norm(c.x, columns('norm_mix_g_2', l))
        if l == 0:
            p = add(proj(c, 'ev_in', c.hsplit, [], feat(rows_view(t['ev_w_in_2'][0]), 0, 2048, 0), c.hi_in, h))
            add(dict(kind='even', evacuated=proj_evacuated(p)))
            add_x(rows_view(t['ev_w_out_2'][0]), KD, False, c.hsplit, [('ev_mixT', 2)], 'ev_out')
        else:
            v = rows_view(t['od_w_in_2'][0])
            dst = lambda n, off, w: c.z[:, n, off:off + w]
            p = add(proj(c, 'od_in', c.hsplit, [], feat(v, 0, 1024, 0) + tok(v, 1024, 2728, dst), c.hi_in, h))
            add(dict(kind='mlstm', evacuated=proj_evacuated(p)))
            add(dict(kind='mla_in', evacuated=proj_evacuated(p)))
            q = lambda n, off, w: c.z[:, n, OD_Q + off:OD_Q + off + w]
            kv = lambda n, off, w: c.xn[:, n, off:off + w]
            p = add(proj(c, 'latents', (c.rT, c.hL), [('la_ready', 1)],
                         tok(rows_view(t['od_w_uq_2'][0]), 0, MLA_HEADS * QKW, q, k=3) +
                         tok(rows_view(t['od_w_ukv_2'][0]), 0, 1024, kv, k=2, ksrc=3), c.hi_latent))
            add(mla_stage(c, proj_evacuated(p)))
            tr = add(turn_stage(c, number('turn'), [0, 1, 2, 3], [('mix_ready', 10)]))
            add_x(rows_view(t['od_w_out_2'][0]), KD, False, c.hsplit, turned_events(tr) + [('att_mixT', 8)], 'od_out')
        h = norm(c.grow, columns('mem_norm_g_2', l), waits=[('mem_loaded', 32)])
        v = rows_view(t['xattn_wkv_2'][l])
        dst = lambda n, off, w: c.z[:, n, off:off + w]
        add(proj(c, 'xa_kv', c.hsplit, [], feat(v, 0, 512, 8) + tok(v, 512, 1024, dst), c.hi_in, h))
        h = norm(c.x, columns('norm_xattn_g_2', l))
        p = add(proj(c, 'xa_q', c.hsplit, [], feat(rows_view(t['xattn_wq_2'][l]), 0, 512, 0), c.hi_in, h))
        add(xa_stage(c, proj_evacuated(p)))
        add_x(rows_view(t['xattn_wo_2'][l]), 4, False, c.hsplit, [('att_mixT', 6 if l == 0 else 10)], 'xa_out')
        h = norm(c.x, columns('norm_ffn_g_2', l))
        gu = rows_view(t['ffn_w_gate_up_2'][l])
        ffn(gu, gu, F_DENSE, rows_view(t['ffn_w_down_2'][l]), False, h)
    add(dict(kind='final', k=1, waits=x_waits(), gain=t['final_norm_g_2']))
    updates[0] += 1
    c.x_updates = updates[0]
    last_tile = None
    for st, after in zip(stages, stages[1:]):
        if st['kind'] == 'proj':
            last_tile = st['tiles'][-1]['t']
        if st['kind'] == 'norm':
            st['last_tile'] = last_tile
            st['next'] = after if after['kind'] != 'moe' else None
            after['presplit'] = 2
    return stages


def build(nc, tensors, out, stop=None):
    c = Core()
    c.t = tensors
    with ExitStack() as ctx:
        def sb(name, shape, dt=F32):
            return ctx.enter_context(nc.sbuf_tensor(name, shape, dt))

        def shared(name, shape):
            with nc.sbuf_tensor(name + '_rounded', shape, R32) as rounded:
                ROUNDED[name] = rounded
            return sb(name, shape)

        class Semaphores(dict):
            def __missing__(self, name):
                self[name] = ctx.enter_context(nc.semaphore(name))
                return self[name]
        c.s = Semaphores()
        c.pb = [ctx.enter_context(nc.psum_tensor(f'bank{i}', [P, 512], F32)) for i in range(8)]
        c.landed = [c.s[f'landed{i}'] for i in range(RING)]
        c.again = [c.s[f'landed_again{r}'] for r in range(2)]

        c.x = sb('x', [P, NT, D])
        c.xn = sb('xn', [P, NT, D])
        c.hT, c.hL = shared('hT', [P, KD, S]), shared('hL', [P, KD, S])
        c.hsplit = (c.hT, c.hL)
        c.z = shared('z', [P, NT, IN1])
        c.zT = shared('zT', [P, 16, S])
        c.mix = shared('mix', [P, NT, D])
        c.ring = shared('ring', [P, RING, SLOT])
        c.rT = shared('rT', [P, 7, S])
        c.L = shared('L', [P, 2048])
        c.PT = shared('PT', [P, 2048])
        c.AT = shared('AT', [P, NT, B_HEADS, P])
        c.grow = sb('grow', [P, NT, D])
        c.gain = c.grow[:, 0, :]
        c.tmp = c.L[:, 1536:2048]
        c.col1, c.col2 = sb('col1', [P, P]), sb('col2', [P, P])
        c.modC, c.modA = sb('modC', [P, 32]), sb('modA', [P, 16])
        c.condT, c.condB = sb('condT', [P, KD]), sb('condB', [P, KD, P])
        c.wsT, c.wpool = sb('wsT', [P, 8, P]), sb('wpool', [P, 4, P])
        c.wrouter = sb('wrouter', [P, KD, N_EXP])
        c.onorm, c.vng, c.vnb = sb('onorm', [P, 2, HD]), sb('vng', [P, 2, 256]), sb('vnb', [P, 2, 256])
        c.mlg, c.gbias = sb('mlg', [P, 512]), sb('gbias', [P, 8])
        c.ident, c.triT = sb('ident', [P, P]), sb('triT', [P, P])
        c.ones, c.zero = sb('ones', [P, S]), sb('zero', [P, S])
        c.maskQ2, c.maskK = sb('maskQ2', [P, 2 * P]), sb('maskK', [P, P])
        c.resume, c.selT = sb('resume', [P, S]), sb('selT', [P, 8, P])
        c.neghalf, c.invf = sb('neghalf', [P, 16]), sb('invf', [P, 32])
        c.lmask = sb('lmask', [P, len(LEVELS) + 1, P], U8)
        c.slotF2, c.slotP, c.inv1 = sb('slotF2', [P, 2 * P]), sb('slotP', [P, 2]), sb('inv1', [P, 16])
        c.sin, c.cos = sb('sin', [P, 96]), sb('cos', [P, 96])
        c.score, c.sel = shared('score', [P, NT, S]), sb('sel', [P, NT, S])
        c.work, c.eq = sb('work', [P, S]), sb('eq', [P, S])
        c.ss, c.ms, c.rstd, c.mx = sb('ss', [P, 2]), sb('ms', [P, 2]), sb('rstd', [P, 2]), sb('mx', [P, 8])
        c.nmx, c.esum, c.rsum, c.top8 = sb('nmx', [P, 8]), sb('esum', [P, 8]), sb('rsum', [P, 8]), sb('top8', [P, 8])
        c.cnt, c.hss, c.hms, c.hrstd = sb('cnt', [P, 2]), sb('hss', [P, 12]), sb('hms', [P, 12]), sb('hrstd', [P, 12])
        c.gss, c.gms, c.grstd, c.gsum = sb('gss', [P, 2]), sb('gms', [P, 2]), sb('grstd', [P, 2]), sb('gsum', [P, 2])
        c.lbd, c.lbe, c.lbl, c.mss = sb('lbd', [P, 6]), sb('lbe', [P, 6]), sb('lbl', [P, 6]), sb('mss', [P, 8])
        c.mrstd, c.mden, c.gcols, c.lss = sb('mrstd', [P, 8]), sb('mden', [P, 8]), sb('gcols', [P, 16]), sb('lss', [P, 4])
        c.lms, c.lrstd, c.meq, c.mexp = sb('lms', [P, 4]), sb('lrstd', [P, 4]), sb('meq', [P, 16]), sb('mexp', [P, 18])
        c.posf, c.sink = sb('posf', [P, 4]), sb('sink', [P, 1])
        c.iw = sb('iw', [P, NT, IDX_HEADS])
        c.logits, c.chosen = sb('logits', [P, NT, N_EXP]), sb('chosen', [P, NT, N_EXP])
        c.slots, c.gates = sb('slots', [P, NT, N_EXP + 1]), sb('gates', [P, NT, N_EXP + 1])
        c.posi, c.count = sb('posi', [P, 4], I32), sb('count', [P, 1], I32)
        c.prow1, c.prow2 = c.PT[:, 0:P], c.PT[:, P:2 * P]
        c.wsraw = c.L[:, 0:8 * P].rearrange('p (g s) -> p g s', g=8)
        zf = c.z[:, :, :].rearrange('p n f -> p (n f)')
        c.ang, c.angc, c.turns = zf[:, 0:96], zf[:, 96:192], zf[:, 192:288]
        zi = zf[:, 512:1536].bitcast(I32)
        c.iotaT, c.iotaS, c.xor, c.less, c.bits = (zi[:, i * P:i * P + P] for i in range(5))
        c.iota1 = zi[:, 5 * P:5 * P + 16]
        c.grows = c.rT[0:ML_HEADS, :, :]
        c.mrows = c.rT[0:N_EXP, 0:2, :]
        c.fs = c.L[:, 0:512].rearrange('p (n f) -> p n f', n=NT)
        c.fa = c.L[:, 512:1024].rearrange('p (n f) -> p n f', n=NT)
        c.faT = c.L[:, 1024:1536].rearrange('p (n a t) -> p n a t', n=NT, a=2)
        c.slotsB = zf[:, 0:2048].rearrange('p (e t) -> p e t', e=N_EXP)
        c.gatesB = zf[:, 2048:4096].rearrange('p (e t) -> p e t', e=N_EXP)
        c.hTe = zf[:, 4096:5120].rearrange('p (k t) -> p k t', k=KD)
        rf = c.rT[:, :, :].rearrange('p m t -> p (m t)')
        c.ye, c.combine = rf[:, 0:D], rf[:, D:D + S]
        c.onehot = rf[:, D + S:D + 2 * S].rearrange('p (n t) -> p n t', n=NT)
        c.hLe = c.AT[:, :, :, :].rearrange('p n h t -> p (n h t)')[:, 0:KD * P].rearrange('p (k t) -> p k t', k=KD)
        c.faL = c.score[:, :, :].rearrange('p n (a t) -> p n a t', a=2)
        zTf = c.zT[:, :, :].rearrange('p m t -> p (m t)')
        mixf = c.mix[:, :, :].rearrange('p n d -> p (n d)')
        hTf, hLf = (b[:, :, :].rearrange('p m t -> p (m t)') for b in c.hsplit)
        zT0, zT1 = zTf[:, 0:SLOT], zTf[:, SLOT:2 * SLOT]
        PTf, Lf = c.PT[:, :], c.L[:, :]
        c.hi_in = [PTf, mixf, Lf]
        c.hi_latent = [PTf, zT0, zT1]
        c.hi_out = c.hi_ffn = [PTf, zT0, zT1, mixf, zf[:, 0:SLOT], zf[:, SLOT:2 * SLOT]]
        c.hi_moe = [PTf, zT0, zT1, mixf, hTf, hLf]
        c.moe_gate = tensors['moe_w_gate'][0].rearrange('e (k p) f -> p (e k) f', p=P)
        c.moe_up = tensors['moe_w_up'][0].rearrange('e (k p) f -> p (e k) f', p=P)
        c.moe_down = tensors['moe_w_down'][0].rearrange('e (k p) n -> p (e k) n', p=P)

        c.jobs, c.n_tiles = [], 0
        c.att = dict(a=0, e=0, t=0, ta=0, tb=0)
        c.turn = dict(b=0)
        c.n_split, c.n_early, c.n_steps = 0, 0, 0
        c.n_log_e = 0
        stages = make_plan(c)[:stop]
        last_x = stages[-1]['x_before'] + 1 if stop else c.x_updates

        def x_written(dve):
            dve.sem_inc(c.s['x_ready'], 1)
        c.x_written = x_written

        block = ctx.enter_context(nc.Block())

        @block.sync
        def _(sp):
            j = 0
            for st in stages:
                if st['kind'] == 'ffn':
                    ffn_sp(c, sp, st)
                    j = st['j0'] + 3 * st['steps']
                elif st['kind'] == 'moe':
                    moe_sp(c, sp, st)
                    j = st['j0'] + 3 * MOE_STEPS * N_EXP
                else:
                    mine = [x for x, _ in st.get('cols', [])]
                    mine += [x for jobs, _, _ in st.get('rows', []) for x, _, _ in jobs]
                    mine += [x[0] for tl in st.get('tiles', []) for x in tl['jobs']]
                    for x in mine:
                        assert x == j
                        if j >= RING:
                            sem, v = c.jobs[j - RING][1]
                            sp.wait_ge(c.s[sem], v)
                        start_job(c, sp, j)
                        j += 1
            if not stop:
                sp.wait_ge(c.s['x_ready'], last_x)
                for n in range(NT):
                    sp.dma_start(out[0, n * P:n * P + P, :], c.x[:, n, :]).then_inc(c.s['stored'], 16)
                sp.wait_ge(c.s['stored'], 32)

        @block.tensor
        def _(pe):
            setup_pe(c, pe)
            for st in stages:
                run = PE.get(st['kind'])
                if run:
                    run(c, pe, st)

        @block.scalar
        def _(act):
            c.act = act
            setup_act(c, act)
            for st in stages:
                run = ACTS.get(st['kind'])
                if run:
                    run(c, act, st)

        @block.vector
        def _(dve):
            c.vstep = chain(dve, c.s['vector_step'])
            setup_dve(c, dve)
            for st in stages:
                run = DVE.get(st['kind'])
                if run:
                    run(c, dve, st)

        @block.gpsimd
        def _(pool):
            c.pstep = chain(pool, c.s['pool_step'])
            setup_pool(c, pool)
            for st in stages:
                run = POOL.get(st['kind'])
                if run:
                    run(c, pool, st)
    return c


def final_all_act(c, act, st):
    final_sp(c, act, st)
    final_act(c, act, st)


PE = dict(ada=ada_pe, norm=norm_pe, proj=proj_pe, dsa=dsa_pe, gmlp=gmlp_pe, hgrn=hgrn_pe, turn=turn_pe, ffn=ffn_pe,
          moe=moe_pe, even=even_pe, xa=xa_pe, mlstm=mlstm_pe, mla_in=mla_in_pe, mla=mla_pe)
ACTS = dict(ada=ada_act, norm=norm_act, proj=proj_act, dsa=dsa_act, gmlp=gmlp_act, hgrn=hgrn_act, turn=turn_act,
            ffn=ffn_act, moe=moe_act, xa=xa_act, mlstm=mlstm_act, mla_in=mla_in_act, mla=mla_act,
            final=final_all_act, mem=mem_act)
DVE = dict(ada=ada_dve, norm=norm_dve, proj=proj_dve, dsa=dsa_dve, gmlp=gmlp_dve, hgrn=hgrn_dve, turn=turn_dve,
           ffn=ffn_dve, moe=moe_dve, even=even_dve, xa=xa_dve, mlstm=mlstm_dve, mla_in=mla_in_dve, mla=mla_dve,
           final=final_dve)
POOL = dict(norm=norm_pool, dsa=dsa_pool, gmlp=gmlp_pool, hgrn=hgrn_pool, final=final_pool, mlstm=mlstm_pool,
            mla_in=mla_in_pool)


def kernel(**inputs):
    import concourse.bacc as bacc
    from concourse.bass_utils import run_bass_kernel_spmd

    nc = bacc.Bacc("TRN2", target_bir_lowering=False, num_devices=1)
    arrays, tensors = {}, {}
    for name in INPUTS:
        a = np.ascontiguousarray(inputs[name])
        arrays[f'in_{name}'] = a
        tensors[name] = nc.dram_tensor(f'in_{name}', a.shape, mybir.dt.from_np(a.dtype), kind="ExternalInput").ap()
    out = nc.dram_tensor('out_x', (1, S, D), F32, kind="ExternalOutput").ap()
    build(nc, tensors, out)
    r = run_bass_kernel_spmd(nc, [arrays], core_ids=[0])
    return r.results[0]['out_x']
```
